# Optimizing a Trainium2 kernel written in Bass

```python
import jax
import jax.numpy as jnp
from jax import lax
import numpy as np

D_MODEL = 1024
BATCH = 1
SEQ = 256
DEPTH = 2

N_A_LAYERS = DEPTH // 2
N_B_LAYERS = DEPTH - N_A_LAYERS
RMS_EPS = 1e-6

GLA_HEADS = 4
GLA_DK = D_MODEL // 2 // GLA_HEADS
GLA_DV = D_MODEL // GLA_HEADS
GLA_GATE_RANK = 16
GLA_GATE_TAU = 16.0
GLA_CHUNK = 64
GLA_IN_WIDTH = 2 * GLA_HEADS * GLA_DK + 2 * GLA_HEADS * GLA_DV + GLA_GATE_RANK

FOX_HEADS = 16
FOX_HEAD_DIM = D_MODEL // FOX_HEADS
FOX_WIDTH = FOX_HEADS * FOX_HEAD_DIM
FOX_Q_BLOCK = 128

MOE_GROUPS = 4
MOE_EXPERTS_PER_GROUP = 8
MOE_EXPERTS = MOE_GROUPS * MOE_EXPERTS_PER_GROUP
MOE_TOP_K = 2
MOE_D_FF = D_MODEL // 2
MOE_BLOCK = 256

kernel_name = 'hybrid_gla_fox_hmoe'

def rmsnorm(x, g):
    xf = x.astype(jnp.float32)
    y = xf * lax.rsqrt(jnp.mean(xf * xf, axis=-1, keepdims=True) + RMS_EPS)
    return (y * g.astype(jnp.float32)).astype(x.dtype)

def gla_chunked(q, k, v, log_a):
    b_, s_, h_, dk = q.shape
    dv = v.shape[-1]
    nc = s_ // GLA_CHUNK

    def to_chunks(t):
        return t.reshape(b_, nc, GLA_CHUNK, h_, t.shape[-1]).transpose(1, 0, 3, 2, 4)

    causal = jnp.tril(jnp.ones((GLA_CHUNK, GLA_CHUNK), dtype=bool))[None, None, :, :, None]

    def step(state, inp):
        qc, kc, vc, gc = inp
        qf = qc.astype(jnp.float32)
        kf = kc.astype(jnp.float32)
        vf = vc.astype(jnp.float32)
        cum = jnp.cumsum(gc.astype(jnp.float32), axis=2)
        last = cum[:, :, -1:, :]
        o_inter = jnp.einsum('bhid,bhde->bhie', qf * jnp.exp(cum), state)
        rel = jnp.where(causal, cum[:, :, :, None, :] - cum[:, :, None, :, :], -jnp.inf)
        scores = jnp.einsum('bhijd,bhjd->bhij', qf[:, :, :, None, :] * jnp.exp(rel), kf)
        o_intra = jnp.einsum('bhij,bhje->bhie', scores, vf)
        state = state * jnp.exp(last)[:, :, 0, :, None] + jnp.einsum(
            'bhjd,bhje->bhde', kf * jnp.exp(last - cum), vf)
        return state, o_inter + o_intra

    state0 = jnp.zeros((b_, h_, dk, dv), jnp.float32)
    _, o = lax.scan(step, state0, (to_chunks(q), to_chunks(k), to_chunks(v), to_chunks(log_a)))
    return o.transpose(1, 0, 3, 2, 4).reshape(b_, s_, h_, dv).astype(v.dtype)

def gla_mixer(x, w_in, w_a2, b_a, out_norm, w_out):
    b_, s_, _ = x.shape
    qk = GLA_HEADS * GLA_DK
    vw = GLA_HEADS * GLA_DV
    proj = x @ w_in
    q, k, v, r, a = jnp.split(proj, [qk, 2 * qk, 2 * qk + vw, 2 * qk + 2 * vw], axis=-1)
    q = q.reshape(b_, s_, GLA_HEADS, GLA_DK) * (GLA_DK ** -0.5)
    k = k.reshape(b_, s_, GLA_HEADS, GLA_DK)
    v = v.reshape(b_, s_, GLA_HEADS, GLA_DV)
    log_a = jax.nn.log_sigmoid((a @ w_a2 + b_a).astype(jnp.float32)) / GLA_GATE_TAU
    o = gla_chunked(q, k, v, log_a.reshape(b_, s_, GLA_HEADS, GLA_DK))
    o = rmsnorm(o, out_norm)
    o = o.reshape(b_, s_, vw) * jax.nn.silu(r)
    return o @ w_out

def shared_kv(h, kv_norm, kv_w, kv_b_f):
    b_, s_, _ = h.shape
    proj = rmsnorm(h, kv_norm) @ kv_w
    k, v, f = jnp.split(proj, [FOX_WIDTH, 2 * FOX_WIDTH], axis=-1)
    k = k.reshape(b_, s_, FOX_HEADS, FOX_HEAD_DIM)
    v = v.reshape(b_, s_, FOX_HEADS, FOX_HEAD_DIM)
    log_f = jax.nn.log_sigmoid((f + kv_b_f).astype(jnp.float32))
    c = jnp.cumsum(log_f, axis=1).transpose(0, 2, 1)
    return k, v, c

def forgetting_attention(q, k, v, c):
    b_, s_, h_, dh = q.shape
    scale = dh ** -0.5
    outs = []
    for blk in range(s_ // FOX_Q_BLOCK):
        q0 = blk * FOX_Q_BLOCK
        q1 = q0 + FOX_Q_BLOCK
        logits = jnp.einsum('bqhd,bkhd->bhqk', q[:, q0:q1], k[:, :q1]).astype(jnp.float32) * scale
        logits = logits + c[:, :, q0:q1, None] - c[:, :, None, :q1]
        mask = (q0 + jnp.arange(FOX_Q_BLOCK))[:, None] >= jnp.arange(q1)[None, :]
        p = jax.nn.softmax(jnp.where(mask, logits, -jnp.inf), axis=-1)
        outs.append(jnp.einsum('bhqk,bkhd->bqhd', p.astype(v.dtype), v[:, :q1]))
    return jnp.concatenate(outs, axis=1)

def fox_mixer(x, k, v, c, w_in, w_out):
    b_, s_, _ = x.shape
    q, og = jnp.split(x @ w_in, [FOX_WIDTH], axis=-1)
    q = q.reshape(b_, s_, FOX_HEADS, FOX_HEAD_DIM)
    o = forgetting_attention(q, k, v, c).reshape(b_, s_, FOX_WIDTH)
    return (o * jax.nn.sigmoid(og)) @ w_out

def grouped_experts(xt, e_idx, gate, w_gate, w_up, w_down):
    n_tok, d = xt.shape
    n_slot = n_tok * MOE_TOP_K
    flat_e = e_idx.reshape(n_slot)
    order = jnp.argsort(flat_e)
    sorted_e = flat_e[order]
    sorted_tok = order // MOE_TOP_K
    counts = jnp.bincount(flat_e, length=MOE_EXPERTS)
    padded = (counts + MOE_BLOCK - 1) // MOE_BLOCK * MOE_BLOCK
    start = jnp.cumsum(counts) - counts
    pad_end = jnp.cumsum(padded)
    pad_start = pad_end - padded
    dest = pad_start[sorted_e] + jnp.arange(n_slot) - start[sorted_e]
    n_blocks = -(-n_slot // MOE_BLOCK) + MOE_EXPERTS
    xbuf = jnp.zeros((n_blocks * MOE_BLOCK, d), xt.dtype).at[dest].set(xt[sorted_tok])
    block_e = jnp.minimum(
        jnp.searchsorted(pad_end, jnp.arange(n_blocks) * MOE_BLOCK, side='right'), MOE_EXPERTS - 1)

    def expert_block(args):
        xb, e = args
        hb = jax.nn.silu(xb @ w_gate[e]) * (xb @ w_up[e])
        return hb @ w_down[e]

    ybuf = lax.map(expert_block, (xbuf.reshape(n_blocks, MOE_BLOCK, d), block_e))
    y_sorted = ybuf.reshape(n_blocks * MOE_BLOCK, d)[dest]
    w_sorted = gate.reshape(n_slot)[order].astype(y_sorted.dtype)
    return jax.ops.segment_sum(y_sorted * w_sorted[:, None], sorted_tok, num_segments=n_tok)

def hier_moe(x, w_coarse, b_coarse, w_fine, b_fine, w_gate, w_up, w_down):
    b_, s_, d = x.shape
    xt = x.reshape(b_ * s_, d)
    p_coarse = jax.nn.softmax((xt @ w_coarse).astype(jnp.float32) + b_coarse, axis=-1)
    pc_top, g_idx = lax.top_k(p_coarse, 1)
    lf = ((xt @ w_fine).astype(jnp.float32) + b_fine).reshape(-1, MOE_GROUPS, MOE_EXPERTS_PER_GROUP)
    lf_sel = jnp.take_along_axis(lf, g_idx[:, :, None], axis=1)[:, 0]
    pf_top, j_idx = lax.top_k(jax.nn.softmax(lf_sel, axis=-1), MOE_TOP_K)
    gate = pc_top * pf_top / jnp.sum(pf_top, axis=-1, keepdims=True)
    e_idx = g_idx * MOE_EXPERTS_PER_GROUP + j_idx
    y = grouped_experts(xt, e_idx, gate, w_gate, w_up, w_down)
    return y.reshape(b_, s_, d).astype(x.dtype)

def setup_inputs(seed: int = 0) -> dict:
    key = jax.random.key(seed)
    ks = jax.random.split(key, 24)
    d = D_MODEL

    def nrm(k, shape, fan_in):
        return jax.random.normal(k, shape, jnp.float32) * (fan_in ** -0.5)

    def gain(k, shape):
        return 1.0 + 0.02 * jax.random.normal(k, shape, jnp.float32)

    def bias(k, shape):
        return 0.01 * jax.random.normal(k, shape, jnp.float32)

    return {
        'x': jax.random.normal(ks[0], (BATCH, SEQ, d), jnp.float32),
        'gla_norm': gain(ks[1], (N_A_LAYERS, d)),
        'gla_w_in': nrm(ks[2], (N_A_LAYERS, d, GLA_IN_WIDTH), d),
        'gla_w_a2': nrm(ks[3], (N_A_LAYERS, GLA_GATE_RANK, GLA_HEADS * GLA_DK), GLA_GATE_RANK),
        'gla_b_a': bias(ks[4], (N_A_LAYERS, GLA_HEADS * GLA_DK)),
        'gla_out_norm': gain(ks[5], (N_A_LAYERS, GLA_HEADS, GLA_DV)),
        'gla_w_out': nrm(ks[6], (N_A_LAYERS, GLA_HEADS * GLA_DV, d), GLA_HEADS * GLA_DV),
        'kv_norm': gain(ks[7], (d,)),
        'kv_w': nrm(ks[8], (d, 2 * FOX_WIDTH + FOX_HEADS), d),
        'kv_b_f': bias(ks[9], (FOX_HEADS,)),
        'fox_norm': gain(ks[10], (N_B_LAYERS, d)),
        'fox_w_in': nrm(ks[11], (N_B_LAYERS, d, 2 * FOX_WIDTH), d),
        'fox_w_out': nrm(ks[12], (N_B_LAYERS, FOX_WIDTH, d), FOX_WIDTH),
        'ffn_norm': gain(ks[13], (DEPTH, d)),
        'router_coarse_w': nrm(ks[14], (DEPTH, d, MOE_GROUPS), d),
        'router_coarse_b': bias(ks[15], (DEPTH, MOE_GROUPS)),
        'router_fine_w': nrm(ks[16], (DEPTH, d, MOE_EXPERTS), d),
        'router_fine_b': bias(ks[17], (DEPTH, MOE_EXPERTS)),
        'expert_w_gate': nrm(ks[18], (DEPTH, MOE_EXPERTS, d, MOE_D_FF), d),
        'expert_w_up': nrm(ks[19], (DEPTH, MOE_EXPERTS, d, MOE_D_FF), d),
        'expert_w_down': nrm(ks[20], (DEPTH, MOE_EXPERTS, MOE_D_FF, d), MOE_D_FF),
        'final_norm': gain(ks[21], (d,)),
    }

def reference(x, gla_norm, gla_w_in, gla_w_a2, gla_b_a, gla_out_norm, gla_w_out,
              kv_norm, kv_w, kv_b_f, fox_norm, fox_w_in, fox_w_out,
              ffn_norm, router_coarse_w, router_coarse_b, router_fine_w, router_fine_b,
              expert_w_gate, expert_w_up, expert_w_down, final_norm):
    h = x
    k_sh = v_sh = c_sh = None
    for layer in range(DEPTH):
        if layer < N_A_LAYERS:
            i = layer
            h = h + gla_mixer(rmsnorm(h, gla_norm[i]), gla_w_in[i], gla_w_a2[i], gla_b_a[i],
                              gla_out_norm[i], gla_w_out[i])
        else:
            if layer == N_A_LAYERS:
                k_sh, v_sh, c_sh = shared_kv(h, kv_norm, kv_w, kv_b_f)
            i = layer - N_A_LAYERS
            h = h + fox_mixer(rmsnorm(h, fox_norm[i]), k_sh, v_sh, c_sh, fox_w_in[i], fox_w_out[i])
        h = h + hier_moe(rmsnorm(h, ffn_norm[layer]), router_coarse_w[layer], router_coarse_b[layer],
                         router_fine_w[layer], router_fine_b[layer], expert_w_gate[layer],
                         expert_w_up[layer], expert_w_down[layer])
    return rmsnorm(h, final_norm)


_drawn_inputs = setup_inputs


def setup_inputs(seed=0):
    import zlib

    import numpy as np

    out = dict(_drawn_inputs(seed))
    spreads = {}
    factors = {'gla_b_a': 5.326,
     'kv_norm': 5.459,
     'kv_b_f': 8.0,
     'fox_norm': 6.928,
     'router_coarse_b': 16.973,
     'router_fine_b': 2.781,
     'final_norm': 7.565}
    for name, (base, spread) in spreads.items():
        noise = np.random.default_rng([zlib.crc32(name.encode()), seed]).standard_normal(out[name].shape)
        drawn = base * np.exp(spread * noise) if base else spread * noise
        out[name] = jnp.asarray(drawn.astype(out[name].dtype))
    for name, factor in factors.items():
        out[name] = (out[name] * factor).astype(out[name].dtype)
    return out
```

```python
from contextlib import ExitStack

import concourse.bass as bass
from concourse import mybir

F32 = mybir.dt.float32
I32 = mybir.dt.int32
ALU = mybir.AluOpType
ACT = mybir.ActivationFunctionType
AX = mybir.AxisListType.X

P = 128
T = 256
TC = T // P
D = 1024
DC = D // P
HALF = 512
EPS = 1e-6
GH, GDK, GDV, RANK = 4, 128, 256, 16
TAU = 16.0
QKW, VW = GH * GDK, GH * GDV
REF = 17
RB = 32
NRB = T // RB
FH, FD = 16, 64
GROUPS, PER = 4, 8
NE = GROUPS * PER
FF = 512
FC = FF // P
SLOTS = 32
JB = P // SLOTS
ROUNDS = NE // JB
EXTRA = 16
KMAX = T // SLOTS - 1
RING = 8
SLOT = 4096
PIECES = 12
UNROLL = 2
GLA_PIECES, FOX_PIECES = 8, 10
MOE_BASE = [GLA_PIECES, GLA_PIECES + ROUNDS * PIECES + FOX_PIECES]
FOX_BASE = GLA_PIECES + ROUNDS * PIECES
NEG = -1e30


def bank_jobs():
    order = []

    def add(names, banks):
        order.extend(zip(names, banks))

    def router(l):
        add([f"m{l}_xT{i}" for i in range(4)], [0, 1, 2, 3])
        add([f"m{l}_logT", f"m{l}_log", f"m{l}_pos"], [4, 5, 6])

    add([f"g_xT{i}" for i in range(4)], [0, 1, 2, 3])
    add(["g_a"], [4])
    add(["g_q0", "g_q1", "g_k0", "g_k1"], [5, 6, 7, 0])
    add(["g_z0", "g_z1"], [1, 2])
    add(["g_v00", "g_v01", "g_v10", "g_v11"], [3, 4, 5, 6])
    add(["g_cum0", "g_cum1"], [7, 0])
    add(["g_r00", "g_r01", "g_r10", "g_r11"], [1, 2, 3, 0])
    add([f"g_s{h}" for h in range(GH)], [4, 5, 6, 7])
    add([f"g_sT{h}" for h in range(GH)], [0, 1, 2, 3])
    add([f"g_o{h}" for h in range(GH)], [4, 5, 6, 7])
    add([f"g_oT{i}" for i in range(4)], [0, 1, 2, 3])
    add(["g_y00", "g_y01", "g_y10", "g_y11"], [4, 5, 6, 7])
    router(0)
    add([f"f_xT{i}" for i in range(4)], [0, 1, 2, 3])
    add(["f_f"], [4])
    add([f"f_k{i}" for i in range(4)], [5, 6, 7, 4])
    add(["f_lf", "f_c"], [5, 6])
    add(["f_v00", "f_v01", "f_v10", "f_v11"], [7, 4, 5, 6])
    add([f"f_q{i}" for i in range(4)], [7, 0, 1, 2])
    add([f"f_g{i}" for i in range(4)], [3, 4, 5, 6])
    for i in range(FH + 2):
        if i < FH:
            add([f"f_s{i}"], [i % 2])
        if 1 <= i <= FH:
            add([f"f_pT{i - 1}"], [2 + (i - 1) % 2])
        if i >= 2 and i % 2 == 1:
            add([f"f_o{(i - 3) // 2}"], [4 + ((i - 3) // 2) % 2])
    add(["f_y00", "f_y01", "f_y10", "f_y11"], [6, 7, 0, 1])
    router(1)
    used, table = [0] * 8, {}
    for name, bank in order:
        used[bank] += 1
        table[name] = (bank, used[bank])
    return table


JOBS = bank_jobs()
PIECE_JOB = {0: "g_q1", 1: "g_k1", 2: "g_v01", 3: "g_v11", 4: "g_r01", 5: "g_r11", 6: "g_y11", 7: "g_y11"}
PIECE_JOB.update({FOX_BASE + i: n for i, n in enumerate(
    ["f_k1", "f_k3", "f_v01", "f_v11", "f_q1", "f_q3", "f_g1", "f_g3", "f_y11", "f_y11"])})


NORMS = {"g": 1, "go": 2, "m0": 3, "f": 4, "m1": 5, "last": 6}
XN = {"g": 1, "m0": 2, "f": 3, "m1": 4}


class Steps:

    def __init__(self, eng, sem, base=0):
        self.eng, self.sem, self.base, self.n = eng, sem, base, 0

    def __call__(self, ins):
        self.n += 1
        ins.then_inc(self.sem, 1)
        self.eng.wait_ge(self.sem, self.base + self.n)


def trunk(nc, x, gla_norm, gla_w_in, gla_w_a2, gla_b_a, gla_out_norm, gla_w_out, kv_norm, kv_w, kv_b_f,
          fox_norm, fox_w_in, fox_w_out, ffn_norm, router_coarse_w, router_coarse_b, router_fine_w,
          router_fine_b, expert_w_gate, expert_w_up, expert_w_down, final_norm, out):
    with ExitStack() as ctx:
        def sb(name, shape, dt=F32):
            return ctx.enter_context(nc.sbuf_tensor(name, shape, dt))

        made = {}

        def sem(name):
            if name not in made:
                made[name] = ctx.enter_context(nc.semaphore(name))
            return made[name]

        ring = sb("ring", [P, RING, SLOT])
        h = sb("h", [P, TC, D])
        xn = sb("xn", [P, TC, DC, P])
        xT = sb("xT", [P, DC, T])
        area = sb("area", [P, 12800])
        ident = sb("ident", [P, P])
        upto = sb("upto", [P, 2 * P])
        lower = sb("lower", [P, P])
        causal = sb("causal", [P, 3 * P])
        iota = sb("iota", [P, NE])
        iota_i = sb("iota_i", [P, NE], I32)
        limits = sb("limits", [P, KMAX])
        gains = sb("gains", [P, 6, DC])
        wa = sb("wa", [P, DC, RANK])
        wf = sb("wf", [P, DC, FH])
        wa2 = sb("wa2", [RANK + 1, QKW])
        aT = sb("aT", [RANK + 1, T])
        bf = sb("bf", [FH, 1])
        wr = sb("wr", [P, 2, DC, GROUPS + NE])
        br = sb("br", [GROUPS + NE, 2])
        stat = sb("stat", [P, 3, 8])
        ovb_seen = sb("ovb_seen", [P, 1])
        ids = sb("ids", [1, EXTRA], I32)
        flag = sb("flag", [1, 1], I32)
        PS = ctx.enter_context(nc.psum_tensor("ps", [P, 8, HALF], F32))

        def carve(at, *shape):
            n = 1
            for s in shape:
                n *= s
            assert at + n <= 12800, (at, n)
            v = area[:, at:at + n]
            if len(shape) == 2:
                v = v.rearrange("p (a b) -> p a b", a=shape[0])
            if len(shape) == 3:
                v = v.rearrange("p (a b c) -> p a b c", a=shape[0], b=shape[1])
            return v

        qT, kT = carve(0, GH, T), carve(1024, GH, T)
        v_g = carve(2048, TC, D)
        gate_r = carve(4096, TC, D)
        la = carve(6144, TC, QKW)
        cumT = carve(7168, GH, T)
        qs = carve(8192, GH, T)
        kb56 = carve(9216, 4 * 13 * RB)
        sS = carve(10880, GH, 3 * P)
        sT = carve(9216, GH, 3 * P)
        xflat = xn[:].rearrange("p a b c -> p (a b c)")
        lflat = la.rearrange("p a b -> p (a b)")
        kb, at = [], 0
        for b in range(NRB):
            n = GH * RB * (b + 1)
            if b <= 4:
                src, at0 = xflat, at
            elif b <= 6:
                src, at0 = kb56, 0 if b == 5 else GH * RB * 6
            else:
                src, at0 = lflat, 0
            kb.append(src[:, at0:at0 + n].rearrange("p (a b) -> p a b", a=GH))
            at += n
        o_g = xn
        oT_g = xT
        q_f, k_f = carve(0, FH, T), carve(4096, FH, T)
        v_f = carve(8192, TC, D)
        kvT = carve(10240, DC, T)
        s_f, p_f = carve(10240, 2, 3 * P), carve(11008, 2, 3 * P)
        pT_f = carve(11776, 2, 3 * P)
        gT_f = xn[:].rearrange("p t a b -> p (t a b)").rearrange("p (m t) -> p m t", m=DC)
        lfT = carve(12544, T)[0:FH]
        mx_f = sb("mx_f", [P, FH, 2])
        nm_f = sb("nm_f", [P, FH, 2])
        sum_f = sb("sum_f", [P, FH, 2])
        inv_f = sb("inv_f", [P, FH, 2])
        lf_n = sb("lf_n", [P, TC, FH])
        c_neg = sb("c_neg", [FH, T])
        xgT = carve(8192, DC, P)
        silu_g = carve(9216, FF)
        hid = carve(9728, FF)
        hidT = carve(10240, FC, P)
        y_e = carve(10752, D)
        sel = carve(11776, TC, JB * SLOTS)
        wsel = carve(12032, TC, JB * SLOTS)
        wselT = carve(12288, T)
        logT = sb("logT", [GROUPS + NE, T])
        logs = sb("logs", [P, TC, GROUPS + NE])
        small = sb("small", [P, 4, TC, NE])
        place = sb("place", [P, TC, NE + EXTRA])
        gates = sb("gates", [P, TC, NE + EXTRA])
        member = sb("member", [P, TC, NE])
        counts = sb("counts", [P, NE])
        xTf = xT[:].rearrange("p a b -> p (a b)")
        t_a = xTf[:, 0:EXTRA * NE].rearrange("p (b e) -> p b e", b=EXTRA)
        t_hot = xTf[:, 512:1024].rearrange("p (b e) -> p b e", b=EXTRA)
        t_k = xTf[:, 1024:1536].rearrange("p (b e) -> p b e", b=EXTRA)
        ovr = sb("ovr", [P, 4, NE])
        ovb = sb("ovb", [P, 2, EXTRA])
        final_g = area[:, 8192:8192 + D]
        y_out = xn[:].rearrange("p t a b -> p t (a b)")

        landed = [sem(f"landed{s}") for s in range(RING)]
        bank_full = [sem(f"bank_full{b}") for b in range(8)]
        bank_free = [sem(f"bank_free{b}") for b in range(8)]

        def bank(name):
            return PS[:, JOBS[name][0], :]

        def await_full(eng, *names):
            for n in names:
                eng.wait_ge(bank_full[JOBS[n][0]], JOBS[n][1])

        def await_evacuated(eng, *names):
            for n in names:
                eng.wait_ge(bank_free[JOBS[n][0]], JOBS[n][1])

        def freed(ins, name):
            ins.then_inc(bank_free[JOBS[name][0]], 1)

        class Phase:

            def __init__(self, tag, n_iter, layer, base, overflow):
                self.tag, self.n_iter, self.layer, self.base, self.overflow = tag, n_iter, layer, base, overflow
                self.sel_ready = sem(f"{tag}_sel_ready")
                self.gathered = sem(f"{tag}_gathered")
                self.xg_ready = sem(f"{tag}_xg_ready")
                self.wsel_turned = sem(f"{tag}_wsel_turned")
                self.wselT_ready = sem(f"{tag}_wselT_ready")
                self.silu_done = sem(f"{tag}_silu_done")
                self.hid_ready = sem(f"{tag}_hid_ready")
                self.hid_turned = sem(f"{tag}_hid_turned")
                self.hidT_ready = sem(f"{tag}_hidT_ready")
                self.y_ready = sem(f"{tag}_y_ready")
                self.combined = sem(f"{tag}_combined")
                self.h_added = sem(f"{tag}_h_added")
                self.pieces_used = sem(f"{tag}_pieces_used")
                self.steps = sem(f"{tag}_steps")
                self.before = 0 if overflow else layer * ROUNDS
                self.landed = [sem(f"{tag}_landed{s}") for s in range(RING)] if overflow else landed
                self.col0 = NE if overflow else 0

            def slot(self, k):
                return (self.base + k) % RING

            def landed_at(self, it, k):
                inc = 16 * JB if self.overflow else 16
                return inc * (3 * it + (self.base + k) // RING + 1)

        main = [Phase("moe", ROUNDS // UNROLL, l, MOE_BASE[l], False) for l in range(2)]
        over = [Phase(f"ovf{l}", EXTRA // JB // UNROLL, l, 0, True) for l in range(2)]

        block = ctx.enter_context(nc.Block())

        @block.sync
        def _(sp):
            def small_load(dst, src, name):
                sp.dma_start(dst, src).then_inc(sem(name), 16)

            def piece(i, dst, src):
                if i >= RING:
                    await_used(i - RING)
                sp.dma_start(dst, src).then_inc(landed[i % RING], 16)

            def await_used(i):
                if i in PIECE_JOB:
                    await_full(sp, PIECE_JOB[i])
                    return
                l = 0 if i < MOE_BASE[1] else 1
                sp.wait_ge(main[l].pieces_used, l * ROUNDS * PIECES + i - MOE_BASE[l] + 1)

            def cols(i, w, n0):
                piece(i, ring[:, i % RING, :].rearrange("p (c n) -> p c n", c=DC),
                      w.rearrange("(p c) n -> p c n", c=DC)[:, :, n0:n0 + HALF])

            def rows(i, w, c0, order):
                piece(i, ring[:, i % RING, :].rearrange("p (c n) -> p c n", c=4),
                      w.rearrange(f"({order}) n -> p c n", p=P)[:, c0:c0 + 4, :])

            def expert_piece(ph, it, k, ids_of_round=None):
                r, k12 = UNROLL * it + k // PIECES, k % PIECES
                dst = ring[:, ph.slot(k), :].rearrange("p (j n) -> p j n", j=JB)
                if ph.overflow:
                    for j, e in enumerate(ids_of_round):
                        sp.dma_start(dst[:, j:j + 1, :], expert_source(ph.layer, e, 1, k12)).then_inc(
                            ph.landed[ph.slot(k)], 16)
                else:
                    sp.dma_start(dst, expert_source(ph.layer, JB * r, JB, k12)).then_inc(
                        ph.landed[ph.slot(k)], 16)

            def expert_source(layer, e, n, k12):
                if k12 < 8:
                    w = expert_w_gate if k12 % 2 == 0 else expert_w_up
                    cc = k12 // 2
                    return w[layer].rearrange("e (p c) f -> p e (c f)", c=DC)[
                        :, bass.ds(e, n), 2 * cc * FF:2 * (cc + 1) * FF]
                f = k12 - 8
                return expert_w_down[layer].rearrange("e (c p) d -> p e c d", p=P)[
                    :, bass.ds(e, n), f, :]

            def experts(l):
                ph = main[l]
                used0 = ph.before * PIECES
                for k in range(RING):
                    await_used(ph.base + k - RING)
                    expert_piece(ph, 0, k)
                span = UNROLL * PIECES
                with sp.Fori(0, ph.n_iter - 1) as it:
                    for k in range(RING, RING + span):
                        sp.wait_ge(ph.pieces_used, used0 + span * it + k - RING + 1)
                        expert_piece(ph, it, k)
                for k in range(RING, span):
                    sp.wait_ge(ph.pieces_used, used0 + span * (ph.n_iter - 1) + k - RING + 1)
                    expert_piece(ph, ph.n_iter - 1, k)

            def overflow(l):
                ph = over[l]
                span = UNROLL * PIECES
                sp.wait_ge(sem("tables_ready"), l + 1)
                need = sp.value_load(flag[0:1, 0:1], min_val=0, max_val=EXTRA)
                with sp.If(need > 0):
                    sp.wait_ge(main[l].pieces_used, (l + 1) * ROUNDS * PIECES)
                    with sp.Fori(0, ph.n_iter) as it:
                        for k in range(span):
                            if k % PIECES == 0:
                                first = JB * (UNROLL * it + k // PIECES)
                                held = [sp.value_load(ids[0:1, bass.ds(first + j, 1)], min_val=0, max_val=NE - 1)
                                        for j in range(JB)]
                            sp.wait_ge(ph.pieces_used, span * it + max(k - RING + 1, 0))
                            expert_piece(ph, it, k, held)
                    sp.wait_ge(ph.pieces_used, span * ph.n_iter)

            for t in range(TC):
                small_load(h[:, t, :], x[0, t * P:(t + 1) * P, :], f"x_in{t}")
            small_load(gains[:, 0, :], gla_norm[0].rearrange("(p c) -> p c", c=DC), "gains_in")
            small_load(wa[:], gla_w_in[0].rearrange("(p c) n -> p c n", c=DC)[:, :, 2 * QKW + 2 * VW:], "wa_in")
            cols(0, gla_w_in[0], 0)
            small_load(wa2[0:RANK, :], gla_w_a2[0], "wa2_in")
            small_load(wa2[RANK:RANK + 1, :], gla_b_a, "wa2_in")
            cols(1, gla_w_in[0], QKW)
            for i in range(4):
                cols(2 + i, gla_w_in[0], 2 * QKW + i * HALF)
            small_load(gains[:, 5, :], gla_out_norm[0].rearrange("h (q c) -> (h q) c", c=DC), "outg_in")
            for i, g in ((1, ffn_norm[0]), (2, kv_norm), (3, fox_norm[0]), (4, ffn_norm[1])):
                small_load(gains[:, i, :], g.rearrange("(p c) -> p c", c=DC), "gains2_in")
            for l in range(2):
                small_load(wr[:, l, :, 0:GROUPS], router_coarse_w[l].rearrange("(p c) g -> p c g", c=DC), "wr_in")
                small_load(wr[:, l, :, GROUPS:], router_fine_w[l].rearrange("(p c) g -> p c g", c=DC), "wr_in")
                small_load(br[0:GROUPS, l:l + 1], router_coarse_b[l].rearrange("(g a) -> g a", a=1), "wr_in")
                small_load(br[GROUPS:, l:l + 1], router_fine_b[l].rearrange("(g a) -> g a", a=1), "wr_in")
            small_load(wf[:], kv_w.rearrange("(p c) n -> p c n", c=DC)[:, :, 2 * D:], "wf_in")
            small_load(bf[:], kv_b_f.rearrange("(g a) -> g a", a=1), "wf_in")
            rows(6, gla_w_out[0], 0, "p c")
            rows(7, gla_w_out[0], 4, "p c")
            experts(0)
            overflow(0)
            for i, (w, n0) in enumerate([(kv_w, 0), (kv_w, HALF), (kv_w, D), (kv_w, D + HALF), (fox_w_in[0], 0),
                                         (fox_w_in[0], HALF), (fox_w_in[0], D), (fox_w_in[0], D + HALF)]):
                cols(FOX_BASE + i, w, n0)
            rows(FOX_BASE + 8, fox_w_out[0], 0, "c p")
            rows(FOX_BASE + 9, fox_w_out[0], 4, "c p")
            experts(1)
            overflow(1)
            sp.wait_ge(sem("last_h"), 1)
            small_load(final_g, final_norm.rearrange("(a d) -> a d", a=1).to_broadcast([P, D]), "final_in")
            for t in range(TC):
                sp.wait_ge(sem("out_ready"), t + 1)
                sp.dma_start(out[0, t * P:(t + 1) * P, :], y_out[:, t, :]).then_inc(sem("stored"), 16)
            sp.wait_ge(sem("stored"), 16 * TC)

        @block.gpsimd
        def _(pool):
            g = nc.gpsimd
            step = Steps(pool, sem("pool_steps"))
            step(g.memset(ident[:], 0.0))
            g.affine_select(out=ident[:], in_=ident[:], compare_op=ALU.not_equal, fill=1.0, base=0,
                            pattern=[[-1, P]], channel_multiplier=1).then_inc(sem("ident_ready"), 1)
            g.memset(aT[:], 1.0).then_inc(sem("aT_ones"), 1)
            step(g.memset(upto[:], 1.0))
            g.affine_select(out=upto[:, 0:P], in_=upto[:, 0:P], compare_op=ALU.is_ge, fill=0.0, base=0,
                            pattern=[[1, P]], channel_multiplier=-1)
            step(g.memset(lower[:], 1.0))
            step(g.affine_select(out=lower[:], in_=lower[:], compare_op=ALU.is_ge, fill=0.0, base=0,
                                 pattern=[[-1, P]], channel_multiplier=1))
            step(g.memset(causal[:], 0.0))
            for c0 in (0, 2 * P):
                g.affine_select(out=causal[:, c0:c0 + P], in_=causal[:, c0:c0 + P], compare_op=ALU.is_ge,
                                fill=NEG, base=0, pattern=[[-1, P]], channel_multiplier=1)
            step(g.iota(iota_i[:], pattern=[[1, NE]], base=0, channel_multiplier=0))
            step(g.tensor_copy(iota[:], iota_i[:]))
            g.tensor_scalar(limits[:], iota[:, 0:KMAX], float(SLOTS), float(SLOTS), ALU.mult,
                            ALU.add).then_inc(sem("consts_ready"), 1)
            pool.wait_ge(sem("consts_ready"), 1)

            def tables(l):
                pool.wait_ge(sem("routed"), l + 1)
                more, start, end, tmp = (ovr[:, i, :] for i in range(4))
                over_k = t_a.rearrange("p b e -> p (b e)")[:, 0:NE * KMAX].rearrange("p (e k) -> p e k", k=KMAX)
                step(g.tensor_tensor(over_k, counts[:].unsqueeze(2).to_broadcast([P, NE, KMAX]),
                                     limits[:].unsqueeze(1).to_broadcast([P, NE, KMAX]), ALU.subtract))
                step(g.tensor_scalar(over_k, over_k, 0.0, None, ALU.is_gt))
                step(g.tensor_copy(more, over_k[:, :, 0]))
                for k in range(1, KMAX):
                    step(g.tensor_tensor(more, more, over_k[:, :, k], ALU.add))
                src = more
                d = 1
                step(g.tensor_copy(end, more))
                while d < NE:
                    step(g.tensor_copy(tmp, end))
                    step(g.tensor_tensor(end[:, d:NE], tmp[:, d:NE], tmp[:, 0:NE - d], ALU.add))
                    d *= 2
                step(g.tensor_tensor(start, end, more, ALU.subtract))
                b_bc = iota[:, 0:EXTRA].unsqueeze(2).to_broadcast([P, EXTRA, NE])

                def bc(v):
                    return v.unsqueeze(1).to_broadcast([P, EXTRA, NE])

                step(g.tensor_tensor(t_k, b_bc, bc(start), ALU.subtract))
                step(g.tensor_scalar(t_hot, t_k, 0.0, None, ALU.is_ge))
                step(g.tensor_tensor(t_a, b_bc, bc(end), ALU.subtract))
                step(g.tensor_scalar(t_a, t_a, 0.0, None, ALU.is_lt))
                step(g.tensor_tensor(t_hot, t_hot, t_a, ALU.mult))
                step(g.tensor_scalar(t_k, t_k, float(SLOTS), float(SLOTS), ALU.mult, ALU.add))

                def over_experts(dst):
                    n = NE
                    while n > 1:
                        n //= 2
                        o = dst if n == 1 else t_a[:, :, 0:n]
                        i0, i1 = t_a[:, :, 0:n], t_a[:, :, n:2 * n]
                        if n == 1:
                            o = dst.unsqueeze(2)
                        step(g.tensor_tensor(o, i0, i1, ALU.add))

                for t in range(TC):
                    step(g.tensor_scalar(tmp, place[:, t, 0:NE], 1.0, None, ALU.add))
                    step(g.tensor_tensor(t_a, bc(tmp), t_k, ALU.subtract))
                    step(g.tensor_tensor(t_a, t_a, t_hot, ALU.mult))
                    over_experts(ovb[:, 0, :])
                    step(g.tensor_scalar(place[:, t, NE:], ovb[:, 0, :], -1.0, None, ALU.add))
                    step(g.tensor_tensor(t_a, bc(gates[:, t, 0:NE]), t_hot, ALU.mult))
                    over_experts(gates[:, t, NE:])
                step(g.tensor_tensor(t_a, bc(iota[:]), t_hot, ALU.mult))
                over_experts(ovb[:, 1, :])
                step(g.tensor_copy(ids[:], ovb[0:1, 1, :]))
                g.tensor_copy(flag[:], end[0:1, NE - 1:NE]).then_inc(sem("tables_ready"), 1)

            tables(0)
            pool.wait_ge(sem("tables_ready"), 1)
            pool.wait_ge(main[0].pieces_used, 1)
            step(g.memset(k_f[FD:P], 0.0))
            step(g.memset(q_f[FD:P], 0.0))
            g.memset(q_f[FD:FD + 1], 1.0).then_inc(sem("qk_halves"), 1)
            pool.wait_ge(sem("qk_halves"), 1)
            tables(1)
            pool.wait_ge(sem("tables_ready"), 2)

        @block.tensor
        def _(pe):
            def fill(name):
                b, use = JOBS[name]
                if use > 1:
                    pe.wait_ge(bank_free[b], use - 1)
                return PS[:, b, :]

            def full(mm, name):
                mm.then_inc(bank_full[JOBS[name][0]], 1)

            def await_piece(i):
                pe.wait_ge(landed[i % RING], 16 * (i // RING + 1))

            def turn_x(tag):
                for i in range(4):
                    b = fill(f"{tag}_xT{i}")
                    if i == 0:
                        pe.wait_ge(sem("xn_ready"), TC * XN[tag])
                    for c in (2 * i, 2 * i + 1):
                        for t in range(TC):
                            at = (c % 2) * T + t * P
                            mm = pe.transpose(b[:, at:at + P], xn[:, t, c, :], ident[:])
                    full(mm, f"{tag}_xT{i}")

            def down_cols(names, i, src, n_per=2):
                await_piece(i)
                w = ring[:, i % RING, :].rearrange("p (c n) -> p c n", c=DC)
                for a, name in enumerate(names):
                    b = fill(name)
                    for u in range(2):
                        n0 = (2 * a + u) * P
                        for c in range(DC):
                            mm = pe.matmul(b[:, u * T:(u + 1) * T], w[:, c, n0:n0 + P], src[:, c, :],
                                           start=(c == 0), stop=(c == DC - 1))
                    full(mm, name)

            def along_cols(names, i, src):
                await_piece(i)
                w = ring[:, i % RING, :].rearrange("p (c n) -> p c n", c=DC)
                for t, name in enumerate(names):
                    b = fill(name)
                    for c in range(DC):
                        mm = pe.matmul(b[:, :], src[:, c, t * P:(t + 1) * P], w[:, c, :],
                                       start=(c == 0), stop=(c == DC - 1))
                    full(mm, name)

            def out_proj(tag, i, src):
                bs = [[fill(f"{tag}_y{t}{u}") for u in range(2)] for t in range(TC)]
                for half in range(2):
                    await_piece(i + half)
                    w = ring[:, (i + half) % RING, :].rearrange("p (c n) -> p c n", c=4)
                    for t in range(TC):
                        for u in range(2):
                            for c in range(4):
                                cc = 4 * half + c
                                mm = pe.matmul(bs[t][u], src[:, cc, t * P:(t + 1) * P],
                                               w[:, c, u * HALF:(u + 1) * HALF], start=(cc == 0),
                                               stop=(cc == DC - 1))
                            if half == 1:
                                full(mm, f"{tag}_y{t}{u}")

            pe.wait_ge(sem("ident_ready"), 1)
            turn_x("g")
            b = fill("g_a")
            await_evacuated(pe, *[f"g_xT{i}" for i in range(4)])
            pe.wait_ge(sem("wa_in"), 16)
            for c in range(DC):
                mm = pe.matmul(b[0:RANK, 0:T], wa[:, c, :], xT[:, c, :], start=(c == 0), stop=(c == DC - 1))
            full(mm, "g_a")
            down_cols(["g_q0", "g_q1"], 0, xT)
            down_cols(["g_k0", "g_k1"], 1, xT)
            await_evacuated(pe, "g_a")
            pe.wait_ge(sem("wa2_in"), 32)
            for t in range(TC):
                b = fill(f"g_z{t}")
                full(pe.matmul(b, aT[:, t * P:(t + 1) * P], wa2[:], start=True, stop=True), f"g_z{t}")
            along_cols(["g_v00", "g_v01"], 2, xT)
            along_cols(["g_v10", "g_v11"], 3, xT)
            pe.wait_ge(sem("consts_ready"), 1)
            await_evacuated(pe, "g_z0", "g_z1")
            for i in range(2):
                b = fill(f"g_cum{i}")
                for u in range(2):
                    hc = slice((2 * i + u) * P, (2 * i + u + 1) * P)
                    pe.matmul(b[:, u * T:(u + 1) * T], la[:, 0, hc], upto[:], start=True, stop=False)
                    mm = pe.matmul(b[:, u * T + P:(u + 1) * T], la[:, 1, hc], upto[:, 0:P], start=False, stop=True)
                full(mm, f"g_cum{i}")
            along_cols(["g_r00", "g_r01"], 4, xT)
            along_cols(["g_r10", "g_r11"], 5, xT)
            bs = [fill(f"g_s{hh}") for hh in range(GH)]
            pe.wait_ge(sem("qs_ready"), 1)
            for b in range(NRB):
                pe.wait_ge(sem("kb_ready"), b + 1)
                c0 = 0 if b < 4 else P
                q0 = RB * (b % 4)
                for hh in range(GH):
                    mm = pe.matmul(bs[hh][q0:q0 + RB, c0:c0 + RB * (b + 1)], qs[:, hh, RB * b:RB * (b + 1)],
                                   kb[b][:, hh, :], start=True, stop=True)
                    if b == NRB - 1:
                        full(mm, f"g_s{hh}")
            await_evacuated(pe, *[f"g_s{hh}" for hh in range(GH)])
            for hh in range(GH):
                b = fill(f"g_sT{hh}")
                for i in range(3):
                    mm = pe.transpose(b[:, i * P:(i + 1) * P], sS[:, hh, i * P:(i + 1) * P], ident[:])
                full(mm, f"g_sT{hh}")
            for hh in range(GH):
                b = fill(f"g_o{hh}")
                await_evacuated(pe, f"g_sT{hh}")
                vc = slice(hh * GDV, (hh + 1) * GDV)
                pe.matmul(b[:, 0:GDV], sT[:, hh, 0:P], v_g[:, 0, vc], start=True, stop=True)
                pe.matmul(b[:, GDV:], sT[:, hh, P:2 * P], v_g[:, 0, vc], start=True, stop=False)
                full(pe.matmul(b[:, GDV:], sT[:, hh, 2 * P:], v_g[:, 1, vc], start=False, stop=True), f"g_o{hh}")
            await_evacuated(pe, *[f"g_o{hh}" for hh in range(GH)])
            for i in range(4):
                b = fill(f"g_oT{i}")
                for c in (2 * i, 2 * i + 1):
                    for t in range(TC):
                        at = (c % 2) * T + t * P
                        mm = pe.transpose(b[:, at:at + P], o_g[:, t, c, :], ident[:])
                full(mm, f"g_oT{i}")
            await_evacuated(pe, *[f"g_oT{i}" for i in range(4)])
            out_proj("g", 6, oT_g)

            def router(l):
                turn_x(f"m{l}")
                await_evacuated(pe, *[f"m{l}_xT{i}" for i in range(4)])
                b = fill(f"m{l}_logT")
                pe.wait_ge(sem("wr_in"), 8 * 16)
                for c in range(DC):
                    mm = pe.matmul(b[0:GROUPS + NE, 0:T], wr[:, l, c, :], xT[:, c, :], start=(c == 0),
                                   stop=(c == DC - 1))
                full(mm, f"m{l}_logT")
                await_evacuated(pe, f"m{l}_logT")
                b = fill(f"m{l}_log")
                for t in range(TC):
                    mm = pe.transpose(b[:, t * P:t * P + GROUPS + NE], logT[:, t * P:(t + 1) * P],
                                      ident[0:GROUPS + NE, 0:GROUPS + NE])
                full(mm, f"m{l}_log")
                b = fill(f"m{l}_pos")
                pe.wait_ge(sem("member"), l + 1)
                ones = upto[:, P:2 * P]
                pe.matmul(b[:, 0:NE], upto[:, 0:P], member[:, 0, :], start=True, stop=True)
                pe.matmul(b[:, NE:2 * NE], ones, member[:, 0, :], start=True, stop=False)
                pe.matmul(b[:, NE:2 * NE], upto[:, 0:P], member[:, 1, :], start=False, stop=True)
                pe.matmul(b[:, 2 * NE:3 * NE], ones, member[:, 0, :], start=True, stop=False)
                full(pe.matmul(b[:, 2 * NE:3 * NE], ones, member[:, 1, :], start=False, stop=True), f"m{l}_pos")

            def rounds(ph):
                span = UNROLL * PIECES
                with pe.Fori(0, ph.n_iter) as it:
                    for u in range(UNROLL):
                        r = UNROLL * it + u + ph.before
                        pe.wait_ge(ph.sel_ready, r + 1)
                        pe.wait_ge(ph.h_added, 2 * r)
                        for c in range(DC):
                            b = PS[:, 4 + c // 4, (c % 4) * P:(c % 4 + 1) * P]
                            for t in range(TC):
                                mm = pe.matmul(b, xn[:, t, c, :], sel[:, t, :], start=(t == 0), stop=(t == TC - 1))
                        mm.then_inc(ph.gathered, 1)
                        for t in range(TC):
                            mm = pe.transpose(PS[:, 6, t * P:(t + 1) * P], wsel[:, t, :], ident[:])
                        mm.then_inc(ph.wsel_turned, 1)
                        pe.wait_ge(ph.xg_ready, r + 1)
                        pe.wait_ge(ph.hid_ready, r)
                        for k in range(8):
                            kk = u * PIECES + k
                            pe.wait_ge(ph.landed[ph.slot(kk)], ph.landed_at(it, kk))
                            w = ring[:, ph.slot(kk), :].rearrange("p (j c f) -> p j c f", j=JB, c=2)
                            for c2 in range(2):
                                c = 2 * (k // 2) + c2
                                for j in range(JB):
                                    js = slice(SLOTS * j, SLOTS * (j + 1))
                                    mm = pe.matmul(PS[js, k % 2, :], xgT[:, c, js], w[:, j, c2, :],
                                                   start=(c == 0), stop=(c == DC - 1))
                            mm.then_inc(ph.pieces_used, 1)
                        pe.wait_ge(ph.hid_ready, r + 1)
                        pe.wait_ge(ph.wselT_ready, r + 1)
                        for f in range(FC):
                            mm = pe.transpose(PS[:, 6, f * P:(f + 1) * P], hid[:, f * P:(f + 1) * P], ident[:])
                        mm.then_inc(ph.hid_turned, 1)
                        pe.wait_ge(ph.hidT_ready, r + 1)
                        pe.wait_ge(ph.y_ready, r)
                        for f in range(FC):
                            kk = u * PIECES + 8 + f
                            pe.wait_ge(ph.landed[ph.slot(kk)], ph.landed_at(it, kk))
                            w = ring[:, ph.slot(kk), :].rearrange("p (j d) -> p j d", j=JB)
                            for half in range(2):
                                for j in range(JB):
                                    js = slice(SLOTS * j, SLOTS * (j + 1))
                                    mm = pe.matmul(PS[js, 2 + half, :], hidT[:, f, js],
                                                   w[:, j, half * HALF:(half + 1) * HALF],
                                                   start=(f == 0), stop=(f == FC - 1))
                            mm.then_inc(ph.pieces_used, 1)
                        pe.wait_ge(ph.y_ready, r + 1)
                        for t in range(TC):
                            for half in range(2):
                                mm = pe.matmul(PS[:, 4 + 2 * t + half, :], wselT[:, t * P:(t + 1) * P],
                                               y_e[:, half * HALF:(half + 1) * HALF], start=True, stop=True)
                            mm.then_inc(ph.combined, 1)

            def moe(l):
                router(l)
                await_evacuated(pe, f"m{l}_pos")
                rounds(main[l])
                pe.wait_ge(sem("tables_ready"), l + 1)
                need = pe.value_load(flag[0:1, 0:1], min_val=0, max_val=EXTRA)
                with pe.If(need > 0):
                    rounds(over[l])
                    pe.wait_ge(over[l].h_added, EXTRA // JB * 2)
                pe.wait_ge(main[l].h_added, (l + 1) * ROUNDS * TC)

            moe(0)
            turn_x("f")
            b = fill("f_f")
            await_evacuated(pe, *[f"f_xT{i}" for i in range(4)])
            pe.wait_ge(sem("wf_in"), 32)
            for c in range(DC):
                mm = pe.matmul(b[0:FH, 0:T], wf[:, c, :], kvT[:, c, :], start=(c == 0), stop=(c == DC - 1))
            full(mm, "f_f")
            down_cols(["f_k0", "f_k1"], FOX_BASE, kvT)
            down_cols(["f_k2", "f_k3"], FOX_BASE + 1, kvT)
            b = fill("f_lf")
            pe.wait_ge(sem("lfT_ready"), 1)
            for t in range(TC):
                mm = pe.transpose(b[:, t * FH:(t + 1) * FH], lfT[:, t * P:(t + 1) * P], ident[0:FH, 0:FH])
            full(mm, "f_lf")
            await_evacuated(pe, "f_lf")
            b = fill("f_c")
            pe.matmul(b[0:FH, 0:T], lf_n[:, 0, :], upto[:], start=True, stop=False)
            full(pe.matmul(b[0:FH, P:T], lf_n[:, 1, :], upto[:, 0:P], start=False, stop=True), "f_c")
            along_cols(["f_v00", "f_v01"], FOX_BASE + 2, kvT)
            along_cols(["f_v10", "f_v11"], FOX_BASE + 3, kvT)
            pe.wait_ge(sem("foxT_ready"), 4)
            down_cols(["f_q0", "f_q1"], FOX_BASE + 4, xT)
            down_cols(["f_q2", "f_q3"], FOX_BASE + 5, xT)
            down_cols(["f_g0", "f_g1"], FOX_BASE + 6, xT)
            down_cols(["f_g2", "f_g3"], FOX_BASE + 7, xT)
            await_evacuated(pe, *[f"f_{n}{i}" for n in "kq" for i in range(4)])
            await_evacuated(pe, *[f"f_v{i}{t}" for i in range(2) for t in range(TC)])
            pe.wait_ge(sem("c_row"), 16 * FH)
            for i in range(FH + 2):
                if i < FH:
                    b = fill(f"f_s{i}")
                    pe.matmul(b[:, 0:P], q_f[:, i, 0:P], k_f[:, i, 0:P], start=True, stop=True)
                    full(pe.matmul(b[:, P:3 * P], q_f[:, i, P:T], k_f[:, i, :], start=True, stop=True), f"f_s{i}")
                if 1 <= i <= FH:
                    n = i - 1
                    b = fill(f"f_pT{n}")
                    pe.wait_ge(sem("p_ready"), n + 1)
                    for a in range(3):
                        mm = pe.transpose(b[:, a * P:(a + 1) * P], p_f[:, n % 2, a * P:(a + 1) * P], ident[:])
                    full(mm, f"f_pT{n}")
                if i >= 2:
                    n = i - 2
                    o_bank = bank(f"f_o{n // 2}")
                    if n % 2 == 0:
                        fill(f"f_o{n // 2}")
                    await_evacuated(pe, f"f_pT{n}")
                    rs = slice(FD * (n % 2), FD * (n % 2 + 1))
                    hc = slice(FD * n, FD * (n + 1))
                    pe.matmul(o_bank[rs, 0:T], v_f[:, 0, hc], pT_f[:, n % 2, 0:2 * P], start=True, stop=False)
                    mm = pe.matmul(o_bank[rs, P:T], v_f[:, 1, hc], pT_f[:, n % 2, 2 * P:], start=False, stop=True)
                    if n % 2 == 0:
                        mm.then_inc(sem("pv_even"), 1)
                    else:
                        full(mm, f"f_o{n // 2}")
            await_evacuated(pe, *[f"f_o{m}" for m in range(FH // 2)])
            out_proj("f", FOX_BASE + 8, gT_f)
            moe(1)


        @block.scalar
        def _(act):
            a = nc.scalar
            step = Steps(act, sem("act_steps"))

            def root(tag, n):
                act.wait_ge(sem("mean_ready"), NORMS[tag])
                a.activation(stat[:, 2, 0:n], stat[:, 1, 0:n], ACT.Sqrt).then_inc(sem("rstd_ready"), 1)

            def softplus_minus(dst, src):
                step(a.activation(dst, src, ACT.Abs))
                step(a.activation(dst, dst, ACT.Exp, scale=-1.0))
                return a.activation(dst, dst, ACT.Ln, bias=1.0)

            root("g", TC)
            await_full(act, "g_a")
            act.wait_ge(sem("aT_ones"), 1)
            freed(a.copy(aT[0:RANK, :], bank("g_a")[0:RANK, 0:T]), "g_a")
            for dst, n in ((qT, "q"), (kT, "k")):
                for i in range(2):
                    await_full(act, f"g_{n}{i}")
                    freed(a.copy(dst[:, 2 * i:2 * i + 2, :], bank(f"g_{n}{i}").rearrange("p (u t) -> p u t", u=2)),
                          f"g_{n}{i}")
            for t in range(TC):
                await_full(act, f"g_z{t}")
                softplus_minus(la[:, t, :], bank(f"g_z{t}")).then_inc(sem("z_soft"), 1)
            for i in range(2):
                await_full(act, f"g_cum{i}")
                freed(a.mul(cumT[:, 2 * i:2 * i + 2, :], bank(f"g_cum{i}").rearrange("p (u t) -> p u t", u=2), 1 / TAU),
                      f"g_cum{i}")
            act.wait_ge(sem("qs_rel"), 1)
            a.activation(qs, qs, ACT.Exp).then_inc(sem("qs_exp"), 1)
            for b in range(NRB):
                ref = RB * b + REF
                for hh in range(GH):
                    a.activation(kb[b][:, hh, :], cumT[:, hh, 0:RB * (b + 1)], ACT.Exp, scale=-1.0,
                                 bias=cumT[:, hh, ref:ref + 1]).then_inc(sem("kb_exp"), 1)
            for i in range(2):
                for t in range(TC):
                    await_full(act, f"g_r{i}{t}")
                    freed(a.activation(gate_r[:, t, i * HALF:(i + 1) * HALF], bank(f"g_r{i}{t}"), ACT.Silu), f"g_r{i}{t}")
            for hh in range(GH):
                await_full(act, f"g_sT{hh}")
                freed(a.copy(sT[:, hh, :], bank(f"g_sT{hh}")[:, 0:3 * P]), f"g_sT{hh}")
            squares = carve(0, GH * TC, GDV)
            for hh in range(GH):
                await_full(act, f"g_o{hh}")
                for t in range(TC):
                    k = TC * hh + t
                    a.activation(squares[:, k, :], bank(f"g_o{hh}")[:, t * GDV:(t + 1) * GDV], ACT.Square,
                                 accum_out=stat[:, 0, k:k + 1]).then_inc(sem("o_squares"), 1)
            root("go", GH * TC)

            def router(l):
                root(f"m{l}", TC)
                await_full(act, f"m{l}_logT")
                act.wait_ge(sem("wr_in"), 8 * 16)
                freed(a.activation(logT[:], bank(f"m{l}_logT")[0:GROUPS + NE, 0:T], ACT.Identity,
                                   bias=br[:, l:l + 1]), f"m{l}_logT")
                act.wait_ge(sem("coarse_rel"), l + 1)
                coarse = small[:, 0, :, 0:GROUPS]
                a.activation(coarse, coarse, ACT.Exp).then_inc(sem("coarse_exp"), 1)
                act.wait_ge(sem("second_rel"), l + 1)
                second = small[:, 3, :, 8:9]
                a.activation(second, second, ACT.Exp).then_inc(sem("second_exp"), 1)

            def rounds(ph):
                span, used0 = UNROLL * PIECES, ph.before * PIECES
                with act.Fori(0, ph.n_iter) as it:
                    for u in range(UNROLL):
                        r = UNROLL * it + u + ph.before
                        act.wait_ge(ph.wsel_turned, r + 1)
                        act.wait_ge(ph.combined, 2 * r)
                        a.copy(wselT, PS[:, 6, 0:T]).then_inc(ph.wselT_ready, 1)
                        act.wait_ge(ph.pieces_used, used0 + span * it + u * PIECES + 8)
                        act.wait_ge(ph.hid_ready, r)
                        a.activation(silu_g, PS[:, 0, :], ACT.Silu).then_inc(ph.silu_done, 1)
                        act.wait_ge(ph.hid_turned, r + 1)
                        a.copy(hidT.rearrange("p a b -> p (a b)"), PS[:, 6, :]).then_inc(ph.hidT_ready, 1)
                        act.wait_ge(ph.pieces_used, used0 + span * it + (u + 1) * PIECES)
                        a.copy(y_e, PS[:, 2:4, :].rearrange("p a b -> p (a b)")).then_inc(ph.y_ready, 1)

            def moe(l):
                router(l)
                rounds(main[l])
                act.wait_ge(sem("tables_ready"), l + 1)
                need = act.value_load(flag[0:1, 0:1], min_val=0, max_val=EXTRA)
                with act.If(need > 0):
                    rounds(over[l])
                    act.wait_ge(over[l].y_ready, EXTRA // JB)
                act.wait_ge(main[l].y_ready, (l + 1) * ROUNDS)

            moe(0)
            root("f", TC)
            act.wait_ge(sem("f_z"), 1)
            softplus_minus(c_neg[:], lfT).then_inc(sem("f_soft"), 1)
            act.wait_ge(sem("qk_halves"), 1)

            def split_heads(dst, n, i):
                src = bank(f"f_{n}{i}").rearrange("p (u t) -> p u t", u=2)
                d4 = dst[0:FD, 4 * i:4 * i + 4, :].rearrange("p (u o) t -> p u o t", o=2)
                return [(d4[:, :, o, :], src[FD * o:FD * (o + 1)]) for o in range(2)]

            for i in range(4):
                await_full(act, f"f_k{i}")
                (d0, s0), (d1, s1) = split_heads(k_f, "k", i)
                a.copy(d0, s0)
                freed(a.copy(d1, s1), f"f_k{i}")
            await_full(act, "f_c")
            freed(a.mul(c_neg[:], bank("f_c")[0:FH, 0:T], -float(FD) ** 0.5), "f_c")
            await_evacuated(act, "f_c")
            for hh in range(FH):
                act.dma_start(k_f[FD:FD + 1, hh, :], c_neg[hh:hh + 1, :]).then_inc(sem("c_row"), 16)
            for i in range(4):
                await_full(act, f"f_g{i}")
                freed(a.activation(gT_f[:, 2 * i:2 * i + 2, :], bank(f"f_g{i}").rearrange("p (u t) -> p u t", u=2),
                                   ACT.Sigmoid), f"f_g{i}")
            for i in range(FH + 1):
                if i < FH:
                    act.wait_ge(sem("nm_ready"), i + 1)
                    if i >= 2:
                        await_full(act, f"f_pT{i - 2}")
                    for t, (c0, c1) in enumerate(((0, P), (P, 3 * P))):
                        ins = a.activation(p_f[:, i % 2, c0:c1], s_f[:, i % 2, c0:c1], ACT.Exp,
                                           bias=nm_f[:, i, t:t + 1], accum_out=sum_f[:, i, t:t + 1])
                    ins.then_inc(sem("exp_done"), 1)
                if i >= 1:
                    n = i - 1
                    await_full(act, f"f_pT{n}")
                    if n >= 2:
                        if n % 2 == 0:
                            act.wait_ge(sem("pv_even"), n // 2)
                        else:
                            await_full(act, f"f_o{(n - 2) // 2}")
                    freed(a.copy(pT_f[:, n % 2, :], bank(f"f_pT{n}")[:, 0:3 * P]), f"f_pT{n}")
            moe(1)
            root("last", TC)

        @block.vector
        def _(dve):
            v = nc.vector
            step = Steps(dve, sem("dve_steps"))
            h8 = h[:].rearrange("p t (q c) -> p t c q", c=DC)

            def mean_squares(tag):
                for t in range(TC):
                    ins = v.tensor_tensor_reduce(out=xn[:, t, :, :].rearrange("p a b -> p (a b)"), in0=h[:, t, :],
                                                 in1=h[:, t, :], scale=1.0, scalar=0.0, op0=ALU.mult, op1=ALU.add,
                                                 accum_out=stat[:, 0, t:t + 1])
                    if tag == "last" and t == 0:
                        ins.then_inc(sem("last_h"), 1)
                step(ins)
                v.tensor_scalar(stat[:, 1, 0:TC], stat[:, 0, 0:TC], 1.0 / D, EPS, ALU.mult,
                                ALU.add).then_inc(sem("mean_ready"), 1)

            def normalise(tag):
                mean_squares(tag)
                dve.wait_ge(sem("rstd_ready"), NORMS[tag])
                step(v.reciprocal(stat[:, 2, 0:TC], stat[:, 2, 0:TC]))
                for t in range(TC):
                    v.tensor_scalar(xn[:, t, :, :], h8[:, t, :, :], stat[:, 2, t:t + 1], None,
                                    ALU.mult).then_inc(sem("xn_ready"), 1)

            def take_turned(job, dst, i, gain):
                return v.tensor_tensor(dst[:, 2 * i:2 * i + 2, :], bank(job).rearrange("p (u t) -> p u t", u=2),
                                       gains[:, gain, 2 * i:2 * i + 2].unsqueeze(2).to_broadcast([P, 2, T]), ALU.mult)

            def add_to_h(tag):
                for t in range(TC):
                    for u in range(2):
                        await_full(dve, f"{tag}_y{t}{u}")
                        hs = h[:, t, u * HALF:(u + 1) * HALF]
                        freed(v.tensor_tensor(hs, hs, bank(f"{tag}_y{t}{u}"), ALU.add), f"{tag}_y{t}{u}")
                for t in range(TC):
                    await_evacuated(dve, f"{tag}_y{t}0", f"{tag}_y{t}1")

            for t in range(TC):
                dve.wait_ge(sem(f"x_in{t}"), 16)
            normalise("g")
            dve.wait_ge(sem("gains_in"), 16)
            for i in range(4):
                await_full(dve, f"g_xT{i}")
                freed(take_turned(f"g_xT{i}", xT, i, 0), f"g_xT{i}")
            for t in range(TC):
                dve.wait_ge(sem("z_soft"), t + 1)
                freed(v.scalar_tensor_tensor(out=la[:, t, :], in0=bank(f"g_z{t}"), scalar=0.0, in1=la[:, t, :],
                                             op0=ALU.min, op1=ALU.subtract), f"g_z{t}")
            for i in range(2):
                for t in range(TC):
                    await_full(dve, f"g_v{i}{t}")
                    freed(v.tensor_copy(v_g[:, t, i * HALF:(i + 1) * HALF], bank(f"g_v{i}{t}")), f"g_v{i}{t}")
            await_evacuated(dve, "g_cum0", "g_cum1", "g_q0", "g_q1", "g_k0", "g_k1")
            c4 = cumT.rearrange("p a (b s) -> p a b s", s=RB)
            q4 = qs.rearrange("p a (b s) -> p a b s", s=RB)
            for hh in range(GH):
                ref = c4[:, hh, :, REF:REF + 1].to_broadcast([P, NRB, RB])
                ins = v.tensor_tensor(q4[:, hh], c4[:, hh], ref, ALU.subtract)
            ins.then_inc(sem("qs_rel"), 1)
            dve.wait_ge(sem("qs_exp"), 1)
            v.scalar_tensor_tensor(out=qs, in0=qs, scalar=float(GDK) ** -0.5, in1=qT, op0=ALU.mult,
                                   op1=ALU.mult).then_inc(sem("qs_ready"), 1)
            for b in range(NRB):
                dve.wait_ge(sem("kb_exp"), GH * (b + 1))
                v.tensor_tensor(kb[b], kb[b], kT[:, :, 0:RB * (b + 1)], ALU.mult).then_inc(sem("kb_ready"), 1)
            await_full(dve, *[f"g_s{hh}" for hh in range(GH)])
            dve.wait_ge(sem("consts_ready"), 1)
            b0 = JOBS["g_s0"][0]
            step(v.memset(sS, 0.0))
            for b in range(NRB):
                q0, n, c0 = RB * (b % 4), RB * (b % 4 + 1), 0 if b < 4 else 2 * P
                v.tensor_tensor(sS[q0:q0 + RB, :, c0:c0 + n], PS[q0:q0 + RB, b0:b0 + GH, c0:c0 + n],
                                lower[q0:q0 + RB, 0:n].unsqueeze(1).to_broadcast([RB, GH, n]), ALU.mult)
            for hh in range(GH):
                freed(v.tensor_copy(sS[:, hh, P:2 * P], bank(f"g_s{hh}")[:, P:2 * P]), f"g_s{hh}")
            dve.wait_ge(sem("o_squares"), GH * TC)
            v.tensor_scalar(stat[:, 1, :], stat[:, 0, :], 1.0 / GDV, EPS, ALU.mult, ALU.add).then_inc(sem("mean_ready"), 1)
            dve.wait_ge(sem("rstd_ready"), NORMS["go"])
            step(v.reciprocal(stat[:, 2, :], stat[:, 2, :]))
            for i in range(2):
                await_evacuated(dve, *[f"g_r{i}{t}" for t in range(TC)])
            for hh in range(GH):
                hc = slice(hh * GDV, (hh + 1) * GDV)
                for t in range(TC):
                    k = TC * hh + t
                    heads_q = slice(hh * GDV // DC, (hh + 1) * GDV // DC)
                    ins = v.scalar_tensor_tensor(out=o_g[:, t, :, heads_q].rearrange("p c q -> p q c"),
                                                 in0=bank(f"g_o{hh}")[:, t * GDV:(t + 1) * GDV].rearrange(
                                                     "p (q c) -> p q c", c=DC),
                                                 scalar=stat[:, 2, k:k + 1],
                                                 in1=gate_r[:, t, hc].rearrange("p (q c) -> p q c", c=DC), op0=ALU.mult,
                                                 op1=ALU.mult)
                freed(ins, f"g_o{hh}")
            dve.wait_ge(sem("outg_in"), 16)
            for i in range(4):
                await_full(dve, f"g_oT{i}")
                freed(take_turned(f"g_oT{i}", oT_g, i, 5), f"g_oT{i}")
            add_to_h("g")

            def first_of(dst, src, top, scratch, n):
                iota_n = iota[:, 0:n].unsqueeze(1).to_broadcast([P, TC, n])
                step(v.tensor_tensor(dst, src, top.to_broadcast([P, TC, n]), ALU.is_equal))
                step(v.scalar_tensor_tensor(out=dst, in0=iota_n, scalar=100.0, in1=dst, op0=ALU.subtract, op1=ALU.mult))
                step(v.tensor_reduce(scratch, dst, AX, ALU.min))
                step(v.scalar_tensor_tensor(out=dst, in0=iota_n, scalar=100.0, in1=scratch.to_broadcast([P, TC, n]),
                                            op0=ALU.subtract, op1=ALU.is_equal))

            def router(l):
                normalise(f"m{l}")
                dve.wait_ge(sem("gains2_in"), 64)
                for i in range(4):
                    await_full(dve, f"m{l}_xT{i}")
                    freed(take_turned(f"m{l}_xT{i}", xT, i, (1, 4)[l]), f"m{l}_xT{i}")
                await_full(dve, f"m{l}_log")
                W = GROUPS + NE
                freed(v.tensor_copy(logs[:], bank(f"m{l}_log")[:, 0:TC * P].rearrange("p (t n) -> p t n", t=TC)[
                    :, :, 0:W]), f"m{l}_log")
                await_evacuated(dve, f"m{l}_log")
                lc, lf = logs[:, :, 0:GROUPS], logs[:, :, GROUPS:]
                rel = small[:, 0, :, 0:GROUPS]
                hot_g = small[:, 0, :, 4:8]
                top, pos1, p_top, total = (small[:, 3, :, i:i + 1] for i in range(4))
                hot_a, hot_b, two, gate8 = (small[:, 2, :, 8 * i:8 * i + 8] for i in range(4))
                fine, rest = small[:, 0, :, 8:16], small[:, 0, :, 16:24]
                m1, m2, g1, g2, second = (small[:, 3, :, i:i + 1] for i in (4, 5, 6, 7, 8))
                step(v.tensor_reduce(top, lc, AX, ALU.max))
                v.tensor_tensor(rel, lc, top.to_broadcast([P, TC, GROUPS]), ALU.subtract).then_inc(
                    sem("coarse_rel"), 1)
                first_of(hot_g, lc, top, pos1, GROUPS)
                pick = small[:, 1, :, :]
                for t in range(TC):
                    ins = v.tensor_tensor(pick[:, t].rearrange("p (g j) -> p g j", g=GROUPS),
                                          lf[:, t].rearrange("p (g j) -> p g j", g=GROUPS),
                                          hot_g[:, t].unsqueeze(2).to_broadcast([P, GROUPS, PER]), ALU.mult)
                step(ins)
                step(v.tensor_reduce(fine, pick.rearrange("p t (g j) -> p t j g", g=GROUPS), AX, ALU.add))
                step(v.tensor_reduce(m1, fine, AX, ALU.max))
                first_of(hot_a, fine, m1, pos1, PER)
                step(v.scalar_tensor_tensor(out=rest, in0=hot_a, scalar=NEG, in1=fine, op0=ALU.mult, op1=ALU.add))
                step(v.tensor_reduce(m2, rest, AX, ALU.max))
                v.tensor_tensor(second, m2, m1, ALU.subtract).then_inc(sem("second_rel"), 1)
                first_of(hot_b, rest, m2, pos1, PER)
                step(v.tensor_tensor(two, hot_a, hot_b, ALU.add))

                def spread(dst, eight):
                    for t in range(TC):
                        ins = v.tensor_tensor(dst[:, t, 0:NE].rearrange("p (g j) -> p g j", g=GROUPS),
                                              hot_g[:, t].unsqueeze(2).to_broadcast([P, GROUPS, PER]),
                                              eight[:, t].unsqueeze(1).to_broadcast([P, GROUPS, PER]), ALU.mult)
                    return ins

                spread(member, two).then_inc(sem("member"), 1)
                dve.wait_ge(sem("coarse_exp"), l + 1)
                step(v.tensor_reduce(total, rel, AX, ALU.add))
                dve.wait_ge(sem("second_exp"), l + 1)
                step(v.tensor_scalar(g2, second, 1.0, None, ALU.add))
                step(v.tensor_tensor(g2, g2, total, ALU.mult))
                step(v.reciprocal(g1, g2))
                step(v.tensor_tensor(g2, g1, second, ALU.mult))
                step(v.tensor_tensor(gate8, hot_a, g1.to_broadcast([P, TC, PER]), ALU.mult))
                step(v.tensor_tensor(rest, hot_b, g2.to_broadcast([P, TC, PER]), ALU.mult))
                step(v.tensor_tensor(gate8, gate8, rest, ALU.add))
                step(spread(gates, gate8))
                await_full(dve, f"m{l}_pos")
                b = bank(f"m{l}_pos")
                step(v.tensor_tensor(place[:, :, 0:NE], b[:, 0:2 * NE].rearrange("p (t e) -> p t e", t=TC), member[:],
                                     ALU.mult))
                step(v.tensor_scalar(place[:, :, 0:NE], place[:, :, 0:NE], -1.0, None, ALU.add))
                freed(v.tensor_copy(counts[:], b[:, 2 * NE:3 * NE]), f"m{l}_pos")
                await_evacuated(dve, f"m{l}_pos")
                v.tensor_copy(ovb_seen[:], stat[:, 0, 0:1]).then_inc(sem("routed"), 1)

            def rounds(ph, gain):
                span, used0 = UNROLL * PIECES, ph.before * PIECES
                steps = 1 * UNROLL
                sel4 = sel.rearrange("p t (j s) -> p t j s", j=JB)
                wsel4 = wsel.rearrange("p t (j s) -> p t j s", j=JB)
                s_bc = iota[:].unsqueeze(1).to_broadcast([P, JB, SLOTS])
                with dve.Fori(0, ph.n_iter) as it:
                    link = Steps(dve, ph.steps, steps * (it * 1 + ph.before // UNROLL))
                    for u in range(UNROLL):
                        r = UNROLL * it + u + ph.before
                        cols = bass.ds(ph.col0 + JB * (UNROLL * it + u), JB)
                        dve.wait_ge(ph.wsel_turned, r)
                        for t in range(TC):
                            ins = v.tensor_tensor(sel4[:, t], s_bc,
                                                  place[:, t, cols].unsqueeze(2).to_broadcast([P, JB, SLOTS]),
                                                  ALU.is_equal)
                        link(ins)
                        for t in range(TC):
                            ins = v.tensor_tensor(wsel4[:, t], sel4[:, t],
                                                  gates[:, t, cols].unsqueeze(2).to_broadcast([P, JB, SLOTS]),
                                                  ALU.mult)
                        ins.then_inc(ph.sel_ready, 1)
                        dve.wait_ge(ph.gathered, r + 1)
                        dve.wait_ge(ph.pieces_used, used0 + span * it + max(u * PIECES - 4, 0))
                        for a in range(2):
                            cs = slice(4 * a, 4 * a + 4)
                            ins = v.tensor_tensor(xgT[:, cs, :], PS[:, 4 + a, :].rearrange("p (c s) -> p c s", c=4),
                                                  gains[:, gain, cs].unsqueeze(2).to_broadcast([P, 4, P]), ALU.mult)
                        ins.then_inc(ph.xg_ready, 1)
                        dve.wait_ge(ph.silu_done, r + 1)
                        dve.wait_ge(ph.hid_turned, r)
                        v.tensor_tensor(hid, silu_g, PS[:, 1, :], ALU.mult).then_inc(ph.hid_ready, 1)
                        for t in range(TC):
                            dve.wait_ge(ph.combined, 2 * r + t + 1)
                            v.tensor_tensor(h[:, t, :], h[:, t, :],
                                            PS[:, 4 + 2 * t:6 + 2 * t, :].rearrange("p a b -> p (a b)"),
                                            ALU.add).then_inc(ph.h_added, 1)
                    assert link.n == steps

            def moe(l):
                router(l)
                rounds(main[l], (1, 4)[l])
                dve.wait_ge(sem("tables_ready"), l + 1)
                need = dve.value_load(flag[0:1, 0:1], min_val=0, max_val=EXTRA)
                with dve.If(need > 0):
                    rounds(over[l], (1, 4)[l])
                    dve.wait_ge(over[l].h_added, EXTRA // JB * TC)
                dve.wait_ge(main[l].h_added, (l + 1) * ROUNDS * TC)

            moe(0)
            normalise("f")
            for i in range(4):
                await_full(dve, f"f_xT{i}")
                take_turned(f"f_xT{i}", xT, i, 3).then_inc(sem("foxT_ready"), 1)
                freed(take_turned(f"f_xT{i}", kvT, i, 2), f"f_xT{i}")
            await_full(dve, "f_f")
            dve.wait_ge(sem("wf_in"), 32)
            freed(v.tensor_scalar(lfT, bank("f_f")[0:FH, 0:T], bf[:, 0:1], None, ALU.add), "f_f")
            await_evacuated(dve, "f_f")
            v.tensor_copy(mx_f[0:FH, 0, 0:1], lfT[:, 0:1]).then_inc(sem("f_z"), 1)
            dve.wait_ge(sem("f_soft"), 1)
            v.scalar_tensor_tensor(out=lfT, in0=lfT, scalar=0.0, in1=c_neg[:], op0=ALU.min,
                                   op1=ALU.subtract).then_inc(sem("lfT_ready"), 1)
            await_full(dve, "f_lf")
            freed(v.tensor_copy(lf_n[:], bank("f_lf")[:, 0:TC * FH].rearrange("p (t n) -> p t n", t=TC)), "f_lf")
            for i in range(2):
                for t in range(TC):
                    await_full(dve, f"f_v{i}{t}")
                    freed(v.tensor_copy(v_f[:, t, i * HALF:(i + 1) * HALF], bank(f"f_v{i}{t}")), f"f_v{i}{t}")
            dve.wait_ge(sem("qk_halves"), 1)
            for i in range(4):
                await_full(dve, f"f_q{i}")
                src = bank(f"f_q{i}").rearrange("p (u t) -> p u t", u=2)
                dst = q_f[0:FD, 4 * i:4 * i + 4, :].rearrange("p (u o) t -> p u o t", o=2)
                v.tensor_copy(dst[:, :, 0, :], src[0:FD])
                freed(v.tensor_copy(dst[:, :, 1, :], src[FD:P]), f"f_q{i}")
            for i in range(FH + 2):
                if i < FH:
                    await_full(dve, f"f_s{i}")
                    if i >= 2:
                        dve.wait_ge(sem("exp_done"), i - 1)
                    b = bank(f"f_s{i}")
                    for t, (c0, c1) in enumerate(((0, P), (P, 3 * P))):
                        ins = v.tensor_tensor_reduce(out=s_f[:, i % 2, c0:c1], in0=b[:, c0:c1], in1=causal[:, c0:c1],
                                                     scale=float(FD) ** -0.5, scalar=NEG, op0=ALU.add, op1=ALU.max,
                                                     accum_out=mx_f[:, i, t:t + 1])
                    freed(ins, f"f_s{i}")
                    await_evacuated(dve, f"f_s{i}")
                    v.tensor_scalar(nm_f[:, i, :], mx_f[:, i, :], -1.0, None, ALU.mult).then_inc(sem("nm_ready"), 1)
                if 1 <= i <= FH:
                    n = i - 1
                    dve.wait_ge(sem("exp_done"), n + 1)
                    step(v.reciprocal(inv_f[:, n, :], sum_f[:, n, :]))
                    v.tensor_scalar(p_f[:, n % 2, 0:P], p_f[:, n % 2, 0:P], inv_f[:, n, 0:1], None, ALU.mult)
                    v.tensor_scalar(p_f[:, n % 2, P:], p_f[:, n % 2, P:], inv_f[:, n, 1:2], None,
                                    ALU.mult).then_inc(sem("p_ready"), 1)
                if i >= 3 and i % 2 == 1:
                    m = (i - 3) // 2
                    if m == 0:
                        await_evacuated(dve, *[f"f_g{j}" for j in range(4)])
                    await_full(dve, f"f_o{m}")
                    freed(v.tensor_tensor(gT_f[:, m, :], gT_f[:, m, :], bank(f"f_o{m}")[:, 0:T], ALU.mult), f"f_o{m}")
            add_to_h("f")
            moe(1)
            mean_squares("last")
            dve.wait_ge(sem("rstd_ready"), NORMS["last"])
            step(v.reciprocal(stat[:, 2, 0:TC], stat[:, 2, 0:TC]))
            dve.wait_ge(sem("final_in"), 16)
            for t in range(TC):
                v.scalar_tensor_tensor(out=y_out[:, t, :], in0=h[:, t, :], scalar=stat[:, 2, t:t + 1], in1=final_g,
                                       op0=ALU.mult, op1=ALU.mult).then_inc(sem("out_ready"), 1)


_INS = ['x', 'gla_norm', 'gla_w_in', 'gla_w_a2', 'gla_b_a', 'gla_out_norm', 'gla_w_out', 'kv_norm', 'kv_w',
        'kv_b_f', 'fox_norm', 'fox_w_in', 'fox_w_out', 'ffn_norm', 'router_coarse_w', 'router_coarse_b',
        'router_fine_w', 'router_fine_b', 'expert_w_gate', 'expert_w_up', 'expert_w_down', 'final_norm']


def kernel(**inputs):
    import numpy as _np
    import concourse.bacc as _bacc
    from concourse.bass_utils import run_bass_kernel_spmd as _run

    nc = _bacc.Bacc("TRN2", target_bir_lowering=False, num_devices=1, dynamic_dma_scratch_size=1024)
    arrays, args = {}, []
    for name in _INS:
        a = _np.ascontiguousarray(inputs[name])
        arrays[f"in_{name}_dram"] = a
        args.append(nc.dram_tensor(f"in_{name}_dram", a.shape, mybir.dt.from_np(a.dtype), kind="ExternalInput").ap())
    out = nc.dram_tensor("out_0_dram", (1, T, D), F32, kind="ExternalOutput").ap()
    trunk(nc, *args, out)
    r = _run(nc, [arrays], core_ids=[0])
    return r.results[0]["out_0_dram"]
```

```python
from contextlib import ExitStack

import concourse.bass as bass
from concourse import mybir

F32 = mybir.dt.float32
I32 = mybir.dt.int32
ALU = mybir.AluOpType
ACT = mybir.ActivationFunctionType
AX = mybir.AxisListType.X

P = 128
T = 256
TC = T // P
D = 1024
DC = D // P
HALF = 512
EPS = 1e-6
GH, GDK, GDV, RANK = 4, 128, 256, 16
TAU = 16.0
QKW, VW = GH * GDK, GH * GDV
REF = 17
RB = 32
NRB = T // RB
FH, FD = 16, 64
GROUPS, PER = 4, 8
NE = GROUPS * PER
FF = 512
FC = FF // P
SLOTS = 32
JB = P // SLOTS
ROUNDS = NE // JB
EXTRA = 16
KMAX = T // SLOTS - 1
RING = 8
SLOT = 4096
PIECES = 12
UNROLL = 2
GLA_PIECES, FOX_PIECES = 8, 10
ANNEX = (6, 7)
RING_FILLS = ROUNDS * PIECES - len(ANNEX)
FOX_BASE = GLA_PIECES + RING_FILLS
MOE_BASE = [GLA_PIECES, FOX_BASE + FOX_PIECES]
START = 1
NEG = -1e30


def bank_jobs():
    order = []

    def add(names, banks):
        order.extend(zip(names, banks))

    def router(l):
        add([f"m{l}_xT{i}" for i in range(4)], [0, 1, 2, 3])
        add([f"m{l}_logT", f"m{l}_log", f"m{l}_pos"], [4, 5, 6])

    add([f"g_xT{i}" for i in range(4)], [0, 1, 2, 3])
    add(["g_a", "g_gain"], [4, 5])
    add(["g_q0", "g_q1", "g_k0", "g_k1"], [6, 7, 0, 1])
    add(["g_z0", "g_z1"], [2, 3])
    add(["g_v00", "g_v01", "g_v10", "g_v11"], [4, 5, 6, 7])
    add(["g_cum0", "g_cum1", "g_r00"], [0, 1, 2])
    add([f"g_s{h}" for h in range(GH)], [4, 5, 6, 7])
    add(["g_r01"], [3])
    add([f"g_sT{h}" for h in range(GH)], [0, 1, 2, 3])
    add([f"g_o{h}" for h in range(GH)], [4, 5, 6, 7])
    add(["g_r10", "g_r11"], [0, 1])
    add(["g_oT0", "g_oT1", "g_y00", "g_y01"], [2, 3, 4, 5])
    add(["g_oT2", "g_oT3", "g_y10", "g_y11"], [0, 1, 6, 7])
    router(0)
    add([f"f_xT{i}" for i in range(4)], [0, 1, 2, 3])
    add(["f_f"], [4])
    add([f"f_k{i}" for i in range(4)], [5, 6, 7, 4])
    add(["f_lf", "f_c"], [5, 6])
    add(["f_v00", "f_v01", "f_v10", "f_v11"], [7, 4, 5, 6])
    add([f"f_q{i}" for i in range(4)], [7, 0, 1, 2])
    add([f"f_g{i}" for i in range(4)], [3, 4, 5, 6])
    for i in range(FH + 3):
        if i < FH:
            add([f"f_s{i}"], [i % 2])
        if 2 <= i <= FH + 1:
            add([f"f_pT{i - 2}"], [2 + (i - 2) % 2])
        if i >= 3 and i % 2 == 1:
            add([f"f_o{(i - 3) // 2}"], [4 + ((i - 3) // 2) % 2])
    add(["f_y00", "f_y01", "f_y10", "f_y11"], [6, 7, 0, 1])
    router(1)
    used, table = [0] * 8, {}
    for name, bank in order:
        used[bank] += 1
        table[name] = (bank, used[bank])
    return table


JOBS = bank_jobs()
PIECE_JOB = {0: "g_q1", 1: "g_k1", 2: "g_v01", 3: "g_v11", 4: "g_r01", 5: "g_r11", 6: "g_y11", 7: "g_y11"}
PIECE_JOB.update({FOX_BASE + i: n for i, n in enumerate(
    ["f_k1", "f_k3", "f_v01", "f_v11", "f_q1", "f_q3", "f_g1", "f_g3", "f_y11", "f_y11"])})


NORMS = {"g": 0, "go": 2, "m0": 6, "f": 8, "m1": 10, "last": 12}
XN = {"g": 1, "m0": 2, "f": 3, "m1": 4}


class Steps:

    def __init__(self, eng, sem, base=0):
        self.eng, self.sem, self.base, self.n = eng, sem, base, 0

    def __call__(self, ins):
        self.n += 1
        ins.then_inc(self.sem, 1)
        self.eng.wait_ge(self.sem, self.base + self.n)


def trunk(nc, x, gla_norm, gla_w_in, gla_w_a2, gla_b_a, gla_out_norm, gla_w_out, kv_norm, kv_w, kv_b_f,
          fox_norm, fox_w_in, fox_w_out, ffn_norm, router_coarse_w, router_coarse_b, router_fine_w,
          router_fine_b, expert_w_gate, expert_w_up, expert_w_down, final_norm, out):
    with ExitStack() as ctx:
        def sb(name, shape, dt=F32):
            return ctx.enter_context(nc.sbuf_tensor(name, shape, dt))

        made = {}

        def sem(name):
            if name not in made:
                made[name] = ctx.enter_context(nc.semaphore(name))
            return made[name]

        ring = sb("ring", [P, RING, SLOT])
        h = sb("h", [P, TC, D])
        xn = sb("xn", [P, TC, DC, P])
        xT = sb("xT", [P, DC, T])
        area = sb("area", [P, 12800])
        ident = sb("ident", [P, P])
        upto = sb("upto", [P, 2 * P])
        lower = sb("lower", [P, P])
        causal = sb("causal", [P, 3 * P])
        iota = sb("iota", [P, NE])
        iota_i = sb("iota_i", [P, NE], I32)
        limits = sb("limits", [P, KMAX])
        gains = sb("gains", [P, 6, DC])
        wa = sb("wa", [P, DC, RANK])
        wf = sb("wf", [P, DC, FH])
        wa2 = sb("wa2", [RANK + 1, QKW])
        aT = sb("aT", [RANK + 1, T])
        bf = sb("bf", [FH, 1])
        wr = sb("wr", [P, 2, DC, GROUPS + NE])
        br = sb("br", [GROUPS + NE, 2])
        stat = sb("stat", [P, 3, 8])
        ovb_seen = sb("ovb_seen", [P, 1])
        out_gain = sb("out_gain", [DC, P])
        ids = sb("ids", [1, EXTRA], I32)
        flag = sb("flag", [1, 1], I32)
        PS = ctx.enter_context(nc.psum_tensor("ps", [P, 8, HALF], F32))

        def carve(at, *shape):
            n = 1
            for s in shape:
                n *= s
            assert at + n <= 12800, (at, n)
            v = area[:, at:at + n]
            if len(shape) == 2:
                v = v.rearrange("p (a b) -> p a b", a=shape[0])
            if len(shape) == 3:
                v = v.rearrange("p (a b c) -> p a b c", a=shape[0], b=shape[1])
            return v

        qT, kT = carve(0, GH, T), carve(1024, GH, T)
        v_g = carve(2048, TC, D)
        gate_r = carve(4096, TC, D)
        la = carve(6144, TC, QKW)
        cumT = carve(7168, GH, T)
        qs = carve(8192, GH, T)
        kb56 = carve(9216, 4 * 13 * RB)
        sS = carve(10880, GH, 3 * P)
        sT = carve(9216, GH, 3 * P)
        xflat = xn[:].rearrange("p a b c -> p (a b c)")
        lflat = la.rearrange("p a b -> p (a b)")
        kb, at = [], 0
        for b in range(NRB):
            n = GH * RB * (b + 1)
            if b <= 4:
                src, at0 = xflat, at
            elif b <= 6:
                src, at0 = kb56, 0 if b == 5 else GH * RB * 6
            else:
                src, at0 = lflat, 0
            kb.append(src[:, at0:at0 + n].rearrange("p (a b) -> p a b", a=GH))
            at += n
        o_g = xn[:].rearrange("p t a b -> p t (a b)")
        oT_g = xT
        q_f, k_f = carve(0, FH, T), carve(4096, FH, T)
        v_f = carve(8192, TC, D)
        kvT = carve(10240, DC, T)
        s_f = xT[:].rearrange("p a b -> p (a b)")[:, 0:9 * P].rearrange("p (a b) -> p a b", a=3)
        p_f, pT_f = carve(10240, 3, 3 * P), carve(11392, 2, 3 * P)
        gT_f = xn[:].rearrange("p t a b -> p (t a b)").rearrange("p (m t) -> p m t", m=DC)
        lfT = carve(12544, T)[0:FH]
        mx_f = sb("mx_f", [P, FH, 2])
        nm_f = sb("nm_f", [P, FH, 2])
        sum_f = sb("sum_f", [P, FH, 2])
        inv_f = sb("inv_f", [P, FH, 2])
        lf_n = sb("lf_n", [P, TC, FH])
        c_neg = sb("c_neg", [FH, T])
        xgT = carve(8192, DC, P)
        silu_g = carve(9216, FF)
        hid = carve(9728, FF)
        hidT = carve(10240, FC, P)
        y_e = carve(10752, D)
        sel = carve(11776, TC, JB * SLOTS)
        wsel = carve(12032, TC, JB * SLOTS)
        wselT = carve(12288, T)
        logT = sb("logT", [GROUPS + NE, T])
        logs = sb("logs", [P, TC, GROUPS + NE])
        small = sb("small", [P, 4, TC, NE])
        place = sb("place", [P, TC, NE + EXTRA])
        gates = sb("gates", [P, TC, NE + EXTRA])
        member = sb("member", [P, TC, NE])
        counts = sb("counts", [P, NE])
        xTf = xT[:].rearrange("p a b -> p (a b)")
        t_a = xTf[:, 0:EXTRA * NE].rearrange("p (b e) -> p b e", b=EXTRA)
        t_hot = xTf[:, 512:1024].rearrange("p (b e) -> p b e", b=EXTRA)
        t_k = xTf[:, 1024:1536].rearrange("p (b e) -> p b e", b=EXTRA)
        ovr = sb("ovr", [P, 4, NE])
        ovb = sb("ovb", [P, 2, EXTRA])
        annex = [carve(SLOT * i, SLOT) for i in range(2)]
        final_g = carve(0, D)
        y_out = xn[:].rearrange("p t a b -> p t (a b)")

        landed = [sem(f"landed{s}") for s in range(RING)]
        annex_landed = [sem(f"annex_landed{i}") for i in range(2)]
        bank_full = [sem(f"bank_full{b}") for b in range(8)]
        bank_free = [sem(f"bank_free{b}") for b in range(8)]

        def bank(name):
            return PS[:, JOBS[name][0], :]

        def await_full(eng, *names):
            for n in names:
                eng.wait_ge(bank_full[JOBS[n][0]], JOBS[n][1])

        def await_evacuated(eng, *names):
            for n in names:
                eng.wait_ge(bank_free[JOBS[n][0]], JOBS[n][1])

        def freed(ins, name):
            ins.then_inc(bank_free[JOBS[name][0]], 1)

        class Phase:

            def __init__(self, tag, n_iter, layer, base, overflow):
                self.tag, self.n_iter, self.layer, self.base, self.overflow = tag, n_iter, layer, base, overflow
                self.sel_ready = sem(f"{tag}_sel_ready")
                self.gathered = sem(f"{tag}_gathered")
                self.xg_ready = sem(f"{tag}_xg_ready")
                self.wsel_turned = sem(f"{tag}_wsel_turned")
                self.wselT_ready = sem(f"{tag}_wselT_ready")
                self.silu_done = sem(f"{tag}_silu_done")
                self.hid_ready = sem(f"{tag}_hid_ready")
                self.hid_turned = sem(f"{tag}_hid_turned")
                self.hidT_ready = sem(f"{tag}_hidT_ready")
                self.y_ready = sem(f"{tag}_y_ready")
                self.combined = sem(f"{tag}_combined")
                self.h_added = sem(f"{tag}_h_added")
                self.pieces_used = sem(f"{tag}_pieces_used")
                self.steps = sem(f"{tag}_steps")
                self.before = 0 if overflow else layer * ROUNDS
                self.landed = [sem(f"{tag}_landed{s}") for s in range(RING)] if overflow else landed
                self.col0 = NE if overflow else 0

            def home(self, it, k):
                if self.overflow:
                    return ring[:, k % RING, :], self.landed[k % RING], 16 * JB * (3 * it + k // RING + 1)
                peeled = isinstance(it, int)
                if peeled and k in ANNEX:
                    return annex[k - ANNEX[0]], annex_landed[k - ANNEX[0]], 16 * (self.layer + 1)
                fill = self.base + (k if peeled and k < ANNEX[0] else k - len(ANNEX))
                return ring[:, fill % RING, :], landed[fill % RING], 16 * (3 * it + fill // RING + 1)

            def iterations(self, eng, body):
                first = 0 if self.overflow else 1
                if first:
                    body(0)
                with eng.Fori(first, self.n_iter) as it:
                    body(it)

            def used(self, n):
                return n + self.before * PIECES + START

        main = [Phase("moe", ROUNDS // UNROLL, l, MOE_BASE[l], False) for l in range(2)]
        over = [Phase(f"ovf{l}", EXTRA // JB // UNROLL, l, 0, True) for l in range(2)]

        block = ctx.enter_context(nc.Block())

        @block.sync
        def _(sp):
            def small_load(dst, src, name):
                sp.dma_start(dst, src).then_inc(sem(name), 16)

            def piece(i, dst, src):
                if i >= RING:
                    await_used(i - RING)
                sp.dma_start(dst, src).then_inc(landed[i % RING], 16)

            def await_used(i):
                if i in PIECE_JOB:
                    await_full(sp, PIECE_JOB[i])
                    return
                l = 0 if i < FOX_BASE else 1
                n = i - MOE_BASE[l]
                sp.wait_ge(main[l].pieces_used, main[l].used(n + 1 if n < ANNEX[0] else n + 1 + len(ANNEX)))

            def cols(i, w, n0):
                piece(i, ring[:, i % RING, :].rearrange("p (c n) -> p c n", c=DC),
                      w.rearrange("(p c) n -> p c n", c=DC)[:, :, n0:n0 + HALF])

            def rows(i, w, c0, order):
                piece(i, ring[:, i % RING, :].rearrange("p (c n) -> p c n", c=4),
                      w.rearrange(f"({order}) n -> p c n", p=P)[:, c0:c0 + 4, :])

            def expert_piece(ph, it, k, experts_of_round=None):
                r, k12 = UNROLL * it + k // PIECES, k % PIECES
                dst, arrived, _ = ph.home(it, k)
                dst = dst.rearrange("p (j n) -> p j n", j=JB)
                if ph.overflow:
                    for j, e in enumerate(experts_of_round):
                        sp.dma_start(dst[:, j:j + 1, :], expert_source(ph.layer, e, 1, k12)).then_inc(arrived, 16)
                else:
                    sp.dma_start(dst, expert_source(ph.layer, JB * r, JB, k12)).then_inc(arrived, 16)

            def expert_source(layer, e, n, k12):
                if k12 < 8:
                    w = expert_w_gate if k12 % 2 == 0 else expert_w_up
                    cc = k12 // 2
                    return w[layer].rearrange("e (p c) f -> p e (c f)", c=DC)[
                        :, bass.ds(e, n), 2 * cc * FF:2 * (cc + 1) * FF]
                f = k12 - 8
                return expert_w_down[layer].rearrange("e (c p) d -> p e c d", p=P)[
                    :, bass.ds(e, n), f, :]

            def experts(l):
                ph = main[l]
                span = UNROLL * PIECES
                for k in range(span):
                    if k in ANNEX:
                        if l == 0:
                            await_evacuated(sp, *[f"g_o{hh}" for hh in range(GH)])
                        else:
                            await_full(sp, f"f_s{FH - 2}", f"f_s{FH - 1}")
                    else:
                        await_used(ph.base + (k if k < ANNEX[0] else k - len(ANNEX)) - RING)
                    expert_piece(ph, 0, k)
                with sp.Fori(1, ph.n_iter) as it:
                    for k in range(span):
                        sp.wait_ge(ph.pieces_used, ph.used(span * it + k - RING + 1))
                        expert_piece(ph, it, k)

            def overflow(l):
                ph = over[l]
                span = UNROLL * PIECES
                sp.wait_ge(sem("tables_ready"), l + 1)
                need = sp.value_load(flag[0:1, 0:1], min_val=0, max_val=EXTRA)
                with sp.If(need > 0):
                    sp.wait_ge(main[l].pieces_used, main[l].used(ROUNDS * PIECES))
                    with sp.Fori(0, ph.n_iter) as it:
                        for k in range(span):
                            if k % PIECES == 0:
                                first = JB * (UNROLL * it + k // PIECES)
                                held = [sp.value_load(ids[0:1, bass.ds(first + j, 1)], min_val=0, max_val=NE - 1)
                                        for j in range(JB)]
                            sp.wait_ge(ph.pieces_used, ph.used(span * it + max(k - RING + 1, 0)))
                            expert_piece(ph, it, k, held)
                    sp.wait_ge(ph.pieces_used, ph.used(span * ph.n_iter))

            for t in range(TC):
                small_load(h[:, t, :], x[0, t * P:(t + 1) * P, :], f"x_in{t}")
            small_load(gains[:, 0, :], gla_norm[0].rearrange("(p c) -> p c", c=DC), "gains_in")
            small_load(out_gain[:], gla_out_norm[0].rearrange("h (u p) -> (h u) p", p=P), "outg_in")
            small_load(wa[:], gla_w_in[0].rearrange("(p c) n -> p c n", c=DC)[:, :, 2 * QKW + 2 * VW:], "wa_in")
            cols(0, gla_w_in[0], 0)
            small_load(wa2[0:RANK, :], gla_w_a2[0], "wa2_in")
            small_load(wa2[RANK:RANK + 1, :], gla_b_a, "wa2_in")
            cols(1, gla_w_in[0], QKW)
            for i in range(4):
                cols(2 + i, gla_w_in[0], 2 * QKW + i * HALF)
            for i, g in ((1, ffn_norm[0]), (2, kv_norm), (3, fox_norm[0]), (4, ffn_norm[1])):
                small_load(gains[:, i, :], g.rearrange("(p c) -> p c", c=DC), "gains2_in")
            for l in range(2):
                small_load(wr[:, l, :, 0:GROUPS], router_coarse_w[l].rearrange("(p c) g -> p c g", c=DC), "wr_in")
                small_load(wr[:, l, :, GROUPS:], router_fine_w[l].rearrange("(p c) g -> p c g", c=DC), "wr_in")
                small_load(br[0:GROUPS, l:l + 1], router_coarse_b[l].rearrange("(g a) -> g a", a=1), "wr_in")
                small_load(br[GROUPS:, l:l + 1], router_fine_b[l].rearrange("(g a) -> g a", a=1), "wr_in")
            small_load(wf[:], kv_w.rearrange("(p c) n -> p c n", c=DC)[:, :, 2 * D:], "wf_in")
            small_load(bf[:], kv_b_f.rearrange("(g a) -> g a", a=1), "wf_in")
            rows(6, gla_w_out[0], 0, "c p")
            rows(7, gla_w_out[0], 4, "c p")
            experts(0)
            overflow(0)
            for i, (w, n0) in enumerate([(kv_w, 0), (kv_w, HALF), (kv_w, D), (kv_w, D + HALF), (fox_w_in[0], 0),
                                         (fox_w_in[0], HALF), (fox_w_in[0], D), (fox_w_in[0], D + HALF)]):
                cols(FOX_BASE + i, w, n0)
            rows(FOX_BASE + 8, fox_w_out[0], 0, "c p")
            rows(FOX_BASE + 9, fox_w_out[0], 4, "c p")
            experts(1)
            overflow(1)
            sp.wait_ge(main[1].pieces_used, main[1].used(ROUNDS * PIECES - RING))
            small_load(final_g, final_norm.rearrange("(a d) -> a d", a=1).to_broadcast([P, D]), "final_in")
            for t in range(TC):
                sp.wait_ge(sem("out_ready"), t + 1)
                sp.dma_start(out[0, t * P:(t + 1) * P, :], y_out[:, t, :]).then_inc(sem("stored"), 16)
            sp.wait_ge(sem("stored"), 16 * TC)

        @block.gpsimd
        def _(pool):
            g = nc.gpsimd
            step = Steps(pool, sem("pool_steps"))
            step(g.memset(ident[:], 0.0))
            g.affine_select(out=ident[:], in_=ident[:], compare_op=ALU.not_equal, fill=1.0, base=0,
                            pattern=[[-1, P]], channel_multiplier=1).then_inc(sem("ident_ready"), 1)
            g.memset(aT[:], 1.0).then_inc(sem("aT_ones"), 1)
            step(g.memset(upto[:], 1.0))
            g.affine_select(out=upto[:, 0:P], in_=upto[:, 0:P], compare_op=ALU.is_ge, fill=0.0, base=0,
                            pattern=[[1, P]], channel_multiplier=-1)
            step(g.memset(lower[:], 1.0))
            step(g.affine_select(out=lower[:], in_=lower[:], compare_op=ALU.is_ge, fill=0.0, base=0,
                                 pattern=[[-1, P]], channel_multiplier=1))
            step(g.memset(causal[:], 0.0))
            for c0 in (0, 2 * P):
                g.affine_select(out=causal[:, c0:c0 + P], in_=causal[:, c0:c0 + P], compare_op=ALU.is_ge,
                                fill=NEG, base=0, pattern=[[-1, P]], channel_multiplier=1)
            step(g.iota(iota_i[:], pattern=[[1, NE]], base=0, channel_multiplier=0))
            step(g.tensor_copy(iota[:], iota_i[:]))
            g.tensor_scalar(limits[:], iota[:, 0:KMAX], float(SLOTS), float(SLOTS), ALU.mult,
                            ALU.add).then_inc(sem("consts_ready"), 1)
            pool.wait_ge(sem("consts_ready"), 1)

            def tables(l):
                pool.wait_ge(sem("routed"), l + 1)
                more, start, end, tmp = (ovr[:, i, :] for i in range(4))
                over_k = t_a.rearrange("p b e -> p (b e)")[:, 0:NE * KMAX].rearrange("p (e k) -> p e k", k=KMAX)
                step(g.tensor_tensor(over_k, counts[:].unsqueeze(2).to_broadcast([P, NE, KMAX]),
                                     limits[:].unsqueeze(1).to_broadcast([P, NE, KMAX]), ALU.subtract))
                step(g.tensor_scalar(over_k, over_k, 0.0, None, ALU.is_gt))
                step(g.tensor_copy(more, over_k[:, :, 0]))
                for k in range(1, KMAX):
                    step(g.tensor_tensor(more, more, over_k[:, :, k], ALU.add))
                src = more
                d = 1
                step(g.tensor_copy(end, more))
                while d < NE:
                    step(g.tensor_copy(tmp, end))
                    step(g.tensor_tensor(end[:, d:NE], tmp[:, d:NE], tmp[:, 0:NE - d], ALU.add))
                    d *= 2
                step(g.tensor_tensor(start, end, more, ALU.subtract))
                b_bc = iota[:, 0:EXTRA].unsqueeze(2).to_broadcast([P, EXTRA, NE])

                def bc(v):
                    return v.unsqueeze(1).to_broadcast([P, EXTRA, NE])

                step(g.tensor_tensor(t_k, b_bc, bc(start), ALU.subtract))
                step(g.tensor_scalar(t_hot, t_k, 0.0, None, ALU.is_ge))
                step(g.tensor_tensor(t_a, b_bc, bc(end), ALU.subtract))
                step(g.tensor_scalar(t_a, t_a, 0.0, None, ALU.is_lt))
                step(g.tensor_tensor(t_hot, t_hot, t_a, ALU.mult))
                step(g.tensor_scalar(t_k, t_k, float(SLOTS), float(SLOTS), ALU.mult, ALU.add))

                def over_experts(dst):
                    n = NE
                    while n > 1:
                        n //= 2
                        o = dst if n == 1 else t_a[:, :, 0:n]
                        i0, i1 = t_a[:, :, 0:n], t_a[:, :, n:2 * n]
                        if n == 1:
                            o = dst.unsqueeze(2)
                        step(g.tensor_tensor(o, i0, i1, ALU.add))

                for t in range(TC):
                    step(g.tensor_scalar(tmp, place[:, t, 0:NE], 1.0, None, ALU.add))
                    step(g.tensor_tensor(t_a, bc(tmp), t_k, ALU.subtract))
                    step(g.tensor_tensor(t_a, t_a, t_hot, ALU.mult))
                    over_experts(ovb[:, 0, :])
                    step(g.tensor_scalar(place[:, t, NE:], ovb[:, 0, :], -1.0, None, ALU.add))
                    step(g.tensor_tensor(t_a, bc(gates[:, t, 0:NE]), t_hot, ALU.mult))
                    over_experts(gates[:, t, NE:])
                step(g.tensor_tensor(t_a, bc(iota[:]), t_hot, ALU.mult))
                over_experts(ovb[:, 1, :])
                step(g.tensor_copy(ids[:], ovb[0:1, 1, :]))
                g.tensor_copy(flag[:], end[0:1, NE - 1:NE]).then_inc(sem("tables_ready"), 1)

            tables(0)
            pool.wait_ge(sem("tables_ready"), 1)
            pool.wait_ge(main[0].pieces_used, main[0].used(PIECES))
            step(g.memset(k_f[FD:P], 0.0))
            step(g.memset(q_f[FD:P], 0.0))
            g.memset(q_f[FD:FD + 1], 1.0).then_inc(sem("qk_halves"), 1)
            pool.wait_ge(sem("qk_halves"), 1)
            tables(1)
            pool.wait_ge(sem("tables_ready"), 2)

        @block.tensor
        def _(pe):
            for ph in (main[0], *over):
                for counter in (ph.gathered, ph.wsel_turned, ph.hid_turned, ph.combined, ph.pieces_used):
                    pe.sem_inc(counter, START)
            def fill(name):
                b, use = JOBS[name]
                if use > 1:
                    pe.wait_ge(bank_free[b], use - 1)
                return PS[:, b, :]

            def full(mm, name):
                mm.then_inc(bank_full[JOBS[name][0]], 1)

            def await_piece(i):
                pe.wait_ge(landed[i % RING], 16 * (i // RING + 1))

            def turn_x(tag):
                bs = [fill(f"{tag}_xT{i}") for i in range(4)]
                for t in range(TC):
                    pe.wait_ge(sem("xn_ready"), TC * (XN[tag] - 1) + t + 1)
                    for i in range(4):
                        for c in (2 * i, 2 * i + 1):
                            at = (c % 2) * T + t * P
                            mm = pe.transpose(bs[i][:, at:at + P], xn[:, t, c, :], ident[:])
                        if t == TC - 1:
                            full(mm, f"{tag}_xT{i}")

            def down_cols(names, i, src, n_per=2):
                await_piece(i)
                w = ring[:, i % RING, :].rearrange("p (c n) -> p c n", c=DC)
                for a, name in enumerate(names):
                    b = fill(name)
                    for u in range(2):
                        n0 = (2 * a + u) * P
                        for c in range(DC):
                            mm = pe.matmul(b[:, u * T:(u + 1) * T], w[:, c, n0:n0 + P], src[:, c, :],
                                           start=(c == 0), stop=(c == DC - 1))
                    full(mm, name)

            def along_cols(names, i, src):
                await_piece(i)
                w = ring[:, i % RING, :].rearrange("p (c n) -> p c n", c=DC)
                for name in names:
                    t = int(name[-1])
                    b = fill(name)
                    for c in range(DC):
                        mm = pe.matmul(b[:, :], src[:, c, t * P:(t + 1) * P], w[:, c, :],
                                       start=(c == 0), stop=(c == DC - 1))
                    full(mm, name)

            def out_part(tag, i, src, half, t):
                await_piece(i + half)
                w = ring[:, (i + half) % RING, :].rearrange("p (c n) -> p c n", c=4)
                for u in range(2):
                    name = f"{tag}_y{t}{u}"
                    b = fill(name) if half == 0 else bank(name)
                    for c in range(4):
                        cc = 4 * half + c
                        mm = pe.matmul(b, src[:, cc, t * P:(t + 1) * P], w[:, c, u * HALF:(u + 1) * HALF],
                                       start=(cc == 0), stop=(cc == DC - 1))
                    if half == 1:
                        full(mm, name)

            pe.wait_ge(sem("ident_ready"), 1)
            turn_x("g")
            b = fill("g_a")
            await_evacuated(pe, *[f"g_xT{i}" for i in range(4)])
            pe.wait_ge(sem("wa_in"), 16)
            for c in range(DC):
                mm = pe.matmul(b[0:RANK, 0:T], wa[:, c, :], xT[:, c, :], start=(c == 0), stop=(c == DC - 1))
            full(mm, "g_a")
            b = fill("g_gain")
            pe.wait_ge(sem("outg_in"), 16)
            full(pe.transpose(b[:, 0:DC], out_gain[:], ident[0:DC, 0:DC]), "g_gain")
            down_cols(["g_q0", "g_q1"], 0, xT)
            down_cols(["g_k0", "g_k1"], 1, xT)
            await_evacuated(pe, "g_a")
            pe.wait_ge(sem("wa2_in"), 32)
            for t in range(TC):
                b = fill(f"g_z{t}")
                full(pe.matmul(b, aT[:, t * P:(t + 1) * P], wa2[:], start=True, stop=True), f"g_z{t}")
            along_cols(["g_v00", "g_v01"], 2, xT)
            along_cols(["g_v10", "g_v11"], 3, xT)
            pe.wait_ge(sem("consts_ready"), 1)
            await_evacuated(pe, "g_z0", "g_z1")
            for i in range(2):
                b = fill(f"g_cum{i}")
                for u in range(2):
                    hc = slice((2 * i + u) * P, (2 * i + u + 1) * P)
                    pe.matmul(b[:, u * T:(u + 1) * T], la[:, 0, hc], upto[:], start=True, stop=False)
                    mm = pe.matmul(b[:, u * T + P:(u + 1) * T], la[:, 1, hc], upto[:, 0:P], start=False, stop=True)
                full(mm, f"g_cum{i}")
            along_cols(["g_r00"], 4, xT)
            bs = [fill(f"g_s{hh}") for hh in range(GH)]
            pe.wait_ge(sem("qs_ready"), 1)
            for b in range(NRB):
                pe.wait_ge(sem("kb_ready"), b + 1)
                c0 = 0 if b < 4 else P
                q0 = RB * (b % 4)
                for hh in range(GH):
                    mm = pe.matmul(bs[hh][q0:q0 + RB, c0:c0 + RB * (b + 1)], qs[:, hh, RB * b:RB * (b + 1)],
                                   kb[b][:, hh, :], start=True, stop=True)
                    if b == NRB - 1:
                        full(mm, f"g_s{hh}")
            along_cols(["g_r01"], 4, xT)
            await_evacuated(pe, *[f"g_s{hh}" for hh in range(GH)])
            for hh in range(GH):
                b = fill(f"g_sT{hh}")
                for i in range(3):
                    mm = pe.transpose(b[:, i * P:(i + 1) * P], sS[:, hh, i * P:(i + 1) * P], ident[:])
                full(mm, f"g_sT{hh}")
            for hh in range(GH):
                b = fill(f"g_o{hh}")
                await_evacuated(pe, f"g_sT{hh}")
                vc = slice(hh * GDV, (hh + 1) * GDV)
                pe.matmul(b[:, 0:GDV], sT[:, hh, 0:P], v_g[:, 0, vc], start=True, stop=True)
                pe.matmul(b[:, GDV:], sT[:, hh, P:2 * P], v_g[:, 0, vc], start=True, stop=False)
                full(pe.matmul(b[:, GDV:], sT[:, hh, 2 * P:], v_g[:, 1, vc], start=False, stop=True), f"g_o{hh}")
            along_cols(["g_r10", "g_r11"], 5, xT)

            def turn_o(i):
                b = fill(f"g_oT{i}")
                await_evacuated(pe, f"g_o{i}")
                for c in (2 * i, 2 * i + 1):
                    for t in range(TC):
                        at = (c % 2) * T + t * P
                        mm = pe.transpose(b[:, at:at + P], o_g[:, t, c * P:(c + 1) * P], ident[:])
                full(mm, f"g_oT{i}")

            turn_o(0)
            turn_o(1)
            await_evacuated(pe, "g_oT0", "g_oT1")
            out_part("g", 6, oT_g, 0, 0)
            turn_o(2)
            turn_o(3)
            out_part("g", 6, oT_g, 0, 1)
            await_evacuated(pe, "g_oT2", "g_oT3")
            out_part("g", 6, oT_g, 1, 0)
            out_part("g", 6, oT_g, 1, 1)

            def router(l):
                turn_x(f"m{l}")
                await_evacuated(pe, *[f"m{l}_xT{i}" for i in range(4)])
                b = fill(f"m{l}_logT")
                pe.wait_ge(sem("wr_in"), 8 * 16)
                for c in range(DC):
                    mm = pe.matmul(b[0:GROUPS + NE, 0:T], wr[:, l, c, :], xT[:, c, :], start=(c == 0),
                                   stop=(c == DC - 1))
                full(mm, f"m{l}_logT")
                await_evacuated(pe, f"m{l}_logT")
                b = fill(f"m{l}_log")
                for t in range(TC):
                    mm = pe.transpose(b[:, t * P:t * P + GROUPS + NE], logT[:, t * P:(t + 1) * P],
                                      ident[0:GROUPS + NE, 0:GROUPS + NE])
                full(mm, f"m{l}_log")
                b = fill(f"m{l}_pos")
                pe.wait_ge(sem("member"), l + 1)
                ones = upto[:, P:2 * P]
                pe.matmul(b[:, 0:NE], upto[:, 0:P], member[:, 0, :], start=True, stop=True)
                pe.matmul(b[:, NE:2 * NE], ones, member[:, 0, :], start=True, stop=False)
                pe.matmul(b[:, NE:2 * NE], upto[:, 0:P], member[:, 1, :], start=False, stop=True)
                pe.matmul(b[:, 2 * NE:3 * NE], ones, member[:, 0, :], start=True, stop=False)
                full(pe.matmul(b[:, 2 * NE:3 * NE], ones, member[:, 1, :], start=False, stop=True), f"m{l}_pos")

            def rounds(ph):
                def body(it):
                    for u in range(UNROLL):
                        r = UNROLL * it + u + ph.before + START
                        pe.wait_ge(ph.sel_ready, r + 1)
                        pe.wait_ge(ph.h_added, TC * (r - START) + START)
                        for c in range(DC):
                            b = PS[:, 4 + c // 4, (c % 4) * P:(c % 4 + 1) * P]
                            for t in range(TC):
                                mm = pe.matmul(b, xn[:, t, c, :], sel[:, t, :], start=(t == 0), stop=(t == TC - 1))
                        mm.then_inc(ph.gathered, 1)
                        for t in range(TC):
                            mm = pe.transpose(PS[:, 6, t * P:(t + 1) * P], wsel[:, t, :], ident[:])
                        mm.then_inc(ph.wsel_turned, 1)
                        pe.wait_ge(ph.xg_ready, r + 1)
                        pe.wait_ge(ph.hid_ready, r)
                        for k in range(8):
                            home, arrived, value = ph.home(it, u * PIECES + k)
                            pe.wait_ge(arrived, value)
                            w = home.rearrange("p (j c f) -> p j c f", j=JB, c=2)
                            for c2 in range(2):
                                c = 2 * (k // 2) + c2
                                for j in range(JB):
                                    js = slice(SLOTS * j, SLOTS * (j + 1))
                                    mm = pe.matmul(PS[js, k % 2, :], xgT[:, c, js], w[:, j, c2, :],
                                                   start=(c == 0), stop=(c == DC - 1))
                            mm.then_inc(ph.pieces_used, 1)
                        pe.wait_ge(ph.hid_ready, r + 1)
                        pe.wait_ge(ph.wselT_ready, r + 1)
                        for f in range(FC):
                            mm = pe.transpose(PS[:, 6, f * P:(f + 1) * P], hid[:, f * P:(f + 1) * P], ident[:])
                        mm.then_inc(ph.hid_turned, 1)
                        pe.wait_ge(ph.hidT_ready, r + 1)
                        pe.wait_ge(ph.y_ready, r)
                        for f in range(FC):
                            home, arrived, value = ph.home(it, u * PIECES + 8 + f)
                            pe.wait_ge(arrived, value)
                            w = home.rearrange("p (j d) -> p j d", j=JB)
                            for half in range(2):
                                for j in range(JB):
                                    js = slice(SLOTS * j, SLOTS * (j + 1))
                                    mm = pe.matmul(PS[js, 2 + half, :], hidT[:, f, js],
                                                   w[:, j, half * HALF:(half + 1) * HALF],
                                                   start=(f == 0), stop=(f == FC - 1))
                            mm.then_inc(ph.pieces_used, 1)
                        pe.wait_ge(ph.y_ready, r + 1)
                        for t in range(TC):
                            for half in range(2):
                                mm = pe.matmul(PS[:, 4 + 2 * t + half, :], wselT[:, t * P:(t + 1) * P],
                                               y_e[:, half * HALF:(half + 1) * HALF], start=True, stop=True)
                            mm.then_inc(ph.combined, 1)

                ph.iterations(pe, body)

            def moe(l):
                router(l)
                await_evacuated(pe, f"m{l}_pos")
                rounds(main[l])
                pe.wait_ge(sem("tables_ready"), l + 1)
                need = pe.value_load(flag[0:1, 0:1], min_val=0, max_val=EXTRA)
                with pe.If(need > 0):
                    rounds(over[l])
                    pe.wait_ge(over[l].h_added, EXTRA // JB * TC + START)
                pe.wait_ge(main[l].h_added, (l + 1) * ROUNDS * TC + START)

            moe(0)
            turn_x("f")
            b = fill("f_f")
            await_evacuated(pe, *[f"f_xT{i}" for i in range(4)])
            pe.wait_ge(sem("wf_in"), 32)
            for c in range(DC):
                mm = pe.matmul(b[0:FH, 0:T], wf[:, c, :], kvT[:, c, :], start=(c == 0), stop=(c == DC - 1))
            full(mm, "f_f")
            down_cols(["f_k0", "f_k1"], FOX_BASE, kvT)
            down_cols(["f_k2", "f_k3"], FOX_BASE + 1, kvT)
            b = fill("f_lf")
            pe.wait_ge(sem("lfT_ready"), 1)
            for t in range(TC):
                mm = pe.transpose(b[:, t * FH:(t + 1) * FH], lfT[:, t * P:(t + 1) * P], ident[0:FH, 0:FH])
            full(mm, "f_lf")
            await_evacuated(pe, "f_lf")
            b = fill("f_c")
            pe.matmul(b[0:FH, 0:T], lf_n[:, 0, :], upto[:], start=True, stop=False)
            full(pe.matmul(b[0:FH, P:T], lf_n[:, 1, :], upto[:, 0:P], start=False, stop=True), "f_c")
            along_cols(["f_v00", "f_v01"], FOX_BASE + 2, kvT)
            along_cols(["f_v10", "f_v11"], FOX_BASE + 3, kvT)
            pe.wait_ge(sem("foxT_ready"), 4)
            down_cols(["f_q0", "f_q1"], FOX_BASE + 4, xT)
            down_cols(["f_q2", "f_q3"], FOX_BASE + 5, xT)
            down_cols(["f_g0", "f_g1"], FOX_BASE + 6, xT)
            down_cols(["f_g2", "f_g3"], FOX_BASE + 7, xT)
            await_evacuated(pe, *[f"f_{n}{i}" for n in "kq" for i in range(4)])
            await_evacuated(pe, *[f"f_v{i}{t}" for i in range(2) for t in range(TC)])
            pe.wait_ge(sem("c_row"), 16 * FH)
            for i in range(FH + 3):
                if i < FH:
                    b = fill(f"f_s{i}")
                    pe.matmul(b[:, 0:P], q_f[:, i, 0:P], k_f[:, i, 0:P], start=True, stop=True)
                    full(pe.matmul(b[:, P:3 * P], q_f[:, i, P:T], k_f[:, i, :], start=True, stop=True), f"f_s{i}")
                if 2 <= i <= FH + 1:
                    n = i - 2
                    b = fill(f"f_pT{n}")
                    pe.wait_ge(sem("p_ready"), n + 1)
                    for a in range(3):
                        mm = pe.transpose(b[:, a * P:(a + 1) * P], p_f[:, n % 3, a * P:(a + 1) * P], ident[:])
                    full(mm, f"f_pT{n}")
                if i >= 3:
                    n = i - 3
                    o_bank = bank(f"f_o{n // 2}")
                    if n % 2 == 0:
                        fill(f"f_o{n // 2}")
                    await_evacuated(pe, f"f_pT{n}")
                    rs = slice(FD * (n % 2), FD * (n % 2 + 1))
                    hc = slice(FD * n, FD * (n + 1))
                    pe.matmul(o_bank[rs, 0:T], v_f[:, 0, hc], pT_f[:, n % 2, 0:2 * P], start=True, stop=False)
                    mm = pe.matmul(o_bank[rs, P:T], v_f[:, 1, hc], pT_f[:, n % 2, 2 * P:], start=False, stop=True)
                    if n % 2 == 0:
                        mm.then_inc(sem("pv_even"), 1)
                    else:
                        full(mm, f"f_o{n // 2}")
            await_evacuated(pe, *[f"f_o{m}" for m in range(FH // 2)])
            for half in range(2):
                for t in range(TC):
                    out_part("f", FOX_BASE + 8, gT_f, half, t)
            moe(1)


        @block.scalar
        def _(act):
            a = nc.scalar
            for ph in (main[0], *over):
                for counter in (ph.wselT_ready, ph.silu_done, ph.hidT_ready, ph.y_ready):
                    act.sem_inc(counter, START)
            step = Steps(act, sem("act_steps"))

            def root(tag, i, cols):
                act.wait_ge(sem("mean_ready"), NORMS[tag] + i + 1)
                a.activation(stat[:, 2, cols], stat[:, 1, cols], ACT.Sqrt).then_inc(sem("rstd_ready"), 1)

            def roots(tag):
                for t in range(TC):
                    root(tag, t, slice(t, t + 1))

            def take_turned(tag, dst, gain):
                for i in (1, 3):
                    job = f"{tag}_xT{i}"
                    await_full(act, job)
                    for u in range(2):
                        ins = a.activation(dst[:, 2 * i + u, :], bank(job)[:, u * T:(u + 1) * T], ACT.Copy,
                                           scale=gains[:, gain, 2 * i + u:2 * i + u + 1])
                    freed(ins, job)

            def softplus_minus(dst, src):
                step(a.activation(dst, src, ACT.Abs))
                step(a.activation(dst, dst, ACT.Exp, scale=-1.0))
                return a.activation(dst, dst, ACT.Ln, bias=1.0)

            roots("g")
            act.wait_ge(sem("gains_in"), 16)
            take_turned("g", xT, 0)
            await_full(act, "g_a")
            act.wait_ge(sem("aT_ones"), 1)
            freed(a.copy(aT[0:RANK, :], bank("g_a")[0:RANK, 0:T]), "g_a")
            for dst, n in ((qT, "q"), (kT, "k")):
                for i in range(2):
                    await_full(act, f"g_{n}{i}")
                    freed(a.copy(dst[:, 2 * i:2 * i + 2, :], bank(f"g_{n}{i}").rearrange("p (u t) -> p u t", u=2)),
                          f"g_{n}{i}")
            for t in range(TC):
                await_full(act, f"g_z{t}")
                softplus_minus(la[:, t, :], bank(f"g_z{t}")).then_inc(sem("z_soft"), 1)
            for i in range(2):
                await_full(act, f"g_cum{i}")
                freed(a.mul(cumT[:, 2 * i:2 * i + 2, :], bank(f"g_cum{i}").rearrange("p (u t) -> p u t", u=2), 1 / TAU),
                      f"g_cum{i}")
            act.wait_ge(sem("qs_rel"), 1)
            a.activation(qs, qs, ACT.Exp).then_inc(sem("qs_exp"), 1)
            for b in range(NRB):
                ref = RB * b + REF
                for hh in range(GH):
                    a.activation(kb[b][:, hh, :], cumT[:, hh, 0:RB * (b + 1)], ACT.Exp, scale=-1.0,
                                 bias=cumT[:, hh, ref:ref + 1]).then_inc(sem("kb_exp"), 1)

            def gate(i):
                for t in range(TC):
                    await_full(act, f"g_r{i}{t}")
                    freed(a.activation(gate_r[:, t, i * HALF:(i + 1) * HALF], bank(f"g_r{i}{t}"), ACT.Silu), f"g_r{i}{t}")

            gate(0)
            for hh in range(GH):
                await_full(act, f"g_sT{hh}")
                freed(a.copy(sT[:, hh, :], bank(f"g_sT{hh}")[:, 0:3 * P]), f"g_sT{hh}")
            squares = carve(0, GH * TC, GDV)
            for hh in range(GH):
                await_full(act, f"g_o{hh}")
                for t in range(TC):
                    k = TC * hh + t
                    a.activation(squares[:, k, :], bank(f"g_o{hh}")[:, t * GDV:(t + 1) * GDV], ACT.Square,
                                 accum_out=stat[:, 0, k:k + 1]).then_inc(sem("o_squares"), 1)
                if hh % 2 == 1:
                    for i in (hh - 1, hh):
                        root("go", i, slice(TC * i, TC * (i + 1)))
            gate(1)

            def router(l):
                roots(f"m{l}")
                act.wait_ge(sem("gains2_in"), 64)
                take_turned(f"m{l}", xT, (1, 4)[l])
                await_full(act, f"m{l}_logT")
                act.wait_ge(sem("wr_in"), 8 * 16)
                freed(a.activation(logT[:], bank(f"m{l}_logT")[0:GROUPS + NE, 0:T], ACT.Identity,
                                   bias=br[:, l:l + 1]), f"m{l}_logT")
                act.wait_ge(sem("coarse_rel"), l + 1)
                coarse = small[:, 0, :, 0:GROUPS]
                a.activation(coarse, coarse, ACT.Exp).then_inc(sem("coarse_exp"), 1)
                act.wait_ge(sem("second_rel"), l + 1)
                second = small[:, 3, :, 8:9]
                a.activation(second, second, ACT.Exp).then_inc(sem("second_exp"), 1)

            def rounds(ph):
                span = UNROLL * PIECES
                with act.Fori(0, ph.n_iter) as it:
                    for u in range(UNROLL):
                        r = UNROLL * it + u + ph.before + START
                        act.wait_ge(ph.wsel_turned, r + 1)
                        act.wait_ge(ph.combined, TC * (r - START) + START)
                        a.copy(wselT, PS[:, 6, 0:T]).then_inc(ph.wselT_ready, 1)
                        act.wait_ge(ph.pieces_used, ph.used(span * it + u * PIECES + 8))
                        act.wait_ge(ph.hid_ready, r)
                        a.activation(silu_g, PS[:, 0, :], ACT.Silu).then_inc(ph.silu_done, 1)
                        act.wait_ge(ph.hid_turned, r + 1)
                        a.copy(hidT.rearrange("p a b -> p (a b)"), PS[:, 6, :]).then_inc(ph.hidT_ready, 1)
                        act.wait_ge(ph.pieces_used, ph.used(span * it + (u + 1) * PIECES))
                        a.copy(y_e, PS[:, 2:4, :].rearrange("p a b -> p (a b)")).then_inc(ph.y_ready, 1)

            def moe(l):
                router(l)
                rounds(main[l])
                act.wait_ge(sem("tables_ready"), l + 1)
                need = act.value_load(flag[0:1, 0:1], min_val=0, max_val=EXTRA)
                with act.If(need > 0):
                    rounds(over[l])
                    act.wait_ge(over[l].y_ready, EXTRA // JB + START)
                act.wait_ge(main[l].y_ready, (l + 1) * ROUNDS + START)

            moe(0)
            roots("f")
            act.wait_ge(sem("f_z"), 1)
            softplus_minus(c_neg[:], lfT).then_inc(sem("f_soft"), 1)
            act.wait_ge(sem("qk_halves"), 1)

            def split_heads(dst, n, i):
                src = bank(f"f_{n}{i}").rearrange("p (u t) -> p u t", u=2)
                d4 = dst[0:FD, 4 * i:4 * i + 4, :].rearrange("p (u o) t -> p u o t", o=2)
                return [(d4[:, :, o, :], src[FD * o:FD * (o + 1)]) for o in range(2)]

            for i in range(4):
                await_full(act, f"f_k{i}")
                (d0, s0), (d1, s1) = split_heads(k_f, "k", i)
                a.copy(d0, s0)
                freed(a.copy(d1, s1), f"f_k{i}")
            await_full(act, "f_c")
            freed(a.mul(c_neg[:], bank("f_c")[0:FH, 0:T], -float(FD) ** 0.5), "f_c")
            await_evacuated(act, "f_c")
            for hh in range(FH):
                act.dma_start(k_f[FD:FD + 1, hh, :], c_neg[hh:hh + 1, :]).then_inc(sem("c_row"), 16)
            for i in range(4):
                await_full(act, f"f_g{i}")
                freed(a.activation(gT_f[:, 2 * i:2 * i + 2, :], bank(f"f_g{i}").rearrange("p (u t) -> p u t", u=2),
                                   ACT.Sigmoid), f"f_g{i}")
            for i in range(FH + 2):
                if i < FH:
                    act.wait_ge(sem("nm_ready"), i + 1)
                    if i >= 3:
                        await_full(act, f"f_pT{i - 3}")
                    for t, (c0, c1) in enumerate(((0, P), (P, 3 * P))):
                        ins = a.activation(p_f[:, i % 3, c0:c1], s_f[:, i % 3, c0:c1], ACT.Exp,
                                           bias=nm_f[:, i, t:t + 1], accum_out=sum_f[:, i, t:t + 1])
                    ins.then_inc(sem("exp_done"), 1)
                if i >= 2:
                    n = i - 2
                    await_full(act, f"f_pT{n}")
                    if n >= 2:
                        if n % 2 == 0:
                            act.wait_ge(sem("pv_even"), n // 2)
                        else:
                            await_full(act, f"f_o{(n - 2) // 2}")
                    freed(a.copy(pT_f[:, n % 2, :], bank(f"f_pT{n}")[:, 0:3 * P]), f"f_pT{n}")
            moe(1)
            roots("last")

        @block.vector
        def _(dve):
            v = nc.vector
            for ph in (main[0], *over):
                for counter in (ph.sel_ready, ph.xg_ready, ph.hid_ready, ph.h_added):
                    dve.sem_inc(counter, START)
            step = Steps(dve, sem("dve_steps"))
            h8 = h[:].rearrange("p t (q c) -> p t c q", c=DC)

            def mean_square(tag, t):
                ins = v.tensor_tensor_reduce(out=xn[:, t, :, :].rearrange("p a b -> p (a b)"), in0=h[:, t, :],
                                             in1=h[:, t, :], scale=1.0, scalar=0.0, op0=ALU.mult, op1=ALU.add,
                                             accum_out=stat[:, 0, t:t + 1])
                step(ins)
                v.tensor_scalar(stat[:, 1, t:t + 1], stat[:, 0, t:t + 1], 1.0 / D, EPS, ALU.mult,
                                ALU.add).then_inc(sem("mean_ready"), 1)

            def inverse(tag, t):
                dve.wait_ge(sem("rstd_ready"), NORMS[tag] + t + 1)
                step(v.reciprocal(stat[:, 2, t:t + 1], stat[:, 2, t:t + 1]))

            def normalise(tag, t):
                mean_square(tag, t)
                inverse(tag, t)
                v.tensor_scalar(xn[:, t, :, :], h8[:, t, :, :], stat[:, 2, t:t + 1], None,
                                ALU.mult).then_inc(sem("xn_ready"), 1)

            def take_turned(job, dst, i, gain):
                return v.tensor_tensor(dst[:, 2 * i:2 * i + 2, :], bank(job).rearrange("p (u t) -> p u t", u=2),
                                       gains[:, gain, 2 * i:2 * i + 2].unsqueeze(2).to_broadcast([P, 2, T]), ALU.mult)

            def add_to_h(tag, then):
                for t in range(TC):
                    for u in range(2):
                        await_full(dve, f"{tag}_y{t}{u}")
                        hs = h[:, t, u * HALF:(u + 1) * HALF]
                        freed(v.tensor_tensor(hs, hs, bank(f"{tag}_y{t}{u}"), ALU.add), f"{tag}_y{t}{u}")
                    await_evacuated(dve, f"{tag}_y{t}0", f"{tag}_y{t}1")
                    normalise(then, t)

            for t in range(TC):
                dve.wait_ge(sem(f"x_in{t}"), 16)
                normalise("g", t)
            dve.wait_ge(sem("gains_in"), 16)
            for i in (0, 2):
                await_full(dve, f"g_xT{i}")
                freed(take_turned(f"g_xT{i}", xT, i, 0), f"g_xT{i}")
            await_full(dve, "g_gain")
            freed(v.tensor_copy(gains[:, 5, :], bank("g_gain")[:, 0:DC]), "g_gain")
            for t in range(TC):
                dve.wait_ge(sem("z_soft"), t + 1)
                freed(v.scalar_tensor_tensor(out=la[:, t, :], in0=bank(f"g_z{t}"), scalar=0.0, in1=la[:, t, :],
                                             op0=ALU.min, op1=ALU.subtract), f"g_z{t}")
            for i in range(2):
                for t in range(TC):
                    await_full(dve, f"g_v{i}{t}")
                    freed(v.tensor_copy(v_g[:, t, i * HALF:(i + 1) * HALF], bank(f"g_v{i}{t}")), f"g_v{i}{t}")
            await_evacuated(dve, "g_cum0", "g_cum1", "g_q0", "g_q1", "g_k0", "g_k1")
            c4 = cumT.rearrange("p a (b s) -> p a b s", s=RB)
            q4 = qs.rearrange("p a (b s) -> p a b s", s=RB)
            for hh in range(GH):
                ref = c4[:, hh, :, REF:REF + 1].to_broadcast([P, NRB, RB])
                ins = v.tensor_tensor(q4[:, hh], c4[:, hh], ref, ALU.subtract)
            ins.then_inc(sem("qs_rel"), 1)
            dve.wait_ge(sem("qs_exp"), 1)
            v.scalar_tensor_tensor(out=qs, in0=qs, scalar=float(GDK) ** -0.5, in1=qT, op0=ALU.mult,
                                   op1=ALU.mult).then_inc(sem("qs_ready"), 1)
            for b in range(NRB):
                dve.wait_ge(sem("kb_exp"), GH * (b + 1))
                v.tensor_tensor(kb[b], kb[b], kT[:, :, 0:RB * (b + 1)], ALU.mult).then_inc(sem("kb_ready"), 1)
            step(v.memset(sS, 0.0))
            await_full(dve, *[f"g_s{hh}" for hh in range(GH)])
            dve.wait_ge(sem("consts_ready"), 1)
            b0 = JOBS["g_s0"][0]
            for b in range(NRB):
                q0, n, c0 = RB * (b % 4), RB * (b % 4 + 1), 0 if b < 4 else 2 * P
                v.tensor_tensor(sS[q0:q0 + RB, :, c0:c0 + n], PS[q0:q0 + RB, b0:b0 + GH, c0:c0 + n],
                                lower[q0:q0 + RB, 0:n].unsqueeze(1).to_broadcast([RB, GH, n]), ALU.mult)
            for hh in range(GH):
                freed(v.tensor_copy(sS[:, hh, P:2 * P], bank(f"g_s{hh}")[:, P:2 * P]), f"g_s{hh}")

            def head_mean(hh):
                dve.wait_ge(sem("o_squares"), TC * (hh + 1))
                ks = slice(TC * hh, TC * (hh + 1))
                v.tensor_scalar(stat[:, 1, ks], stat[:, 0, ks], 1.0 / GDV, EPS, ALU.mult,
                                ALU.add).then_inc(sem("mean_ready"), 1)

            def head_inverse(hh):
                dve.wait_ge(sem("rstd_ready"), NORMS["go"] + hh + 1)
                ks = slice(TC * hh, TC * (hh + 1))
                step(v.reciprocal(stat[:, 2, ks], stat[:, 2, ks]))

            def gated(hh):
                hc = slice(hh * GDV, (hh + 1) * GDV)
                for t in range(TC):
                    await_evacuated(dve, f"g_r{hh // 2}{t}")
                    k = TC * hh + t
                    ins = v.scalar_tensor_tensor(out=o_g[:, t, hc], in0=bank(f"g_o{hh}")[:, t * GDV:(t + 1) * GDV],
                                                 scalar=stat[:, 2, k:k + 1], in1=gate_r[:, t, hc], op0=ALU.mult,
                                                 op1=ALU.mult)
                freed(ins, f"g_o{hh}")

            for pair in ((0, 1), (2, 3)):
                for hh in pair:
                    head_mean(hh)
                for hh in pair:
                    head_inverse(hh)
                if pair[0] == 0:
                    gated(0)
                    gated(1)
            for i in (0, 1):
                await_full(dve, f"g_oT{i}")
                freed(take_turned(f"g_oT{i}", oT_g, i, 5), f"g_oT{i}")
            gated(2)
            gated(3)
            for i in (2, 3):
                await_full(dve, f"g_oT{i}")
                freed(take_turned(f"g_oT{i}", oT_g, i, 5), f"g_oT{i}")
            add_to_h("g", "m0")

            def first_of(dst, src, top, scratch, n):
                iota_n = iota[:, 0:n].unsqueeze(1).to_broadcast([P, TC, n])
                step(v.tensor_tensor(dst, src, top.to_broadcast([P, TC, n]), ALU.is_equal))
                step(v.scalar_tensor_tensor(out=dst, in0=iota_n, scalar=100.0, in1=dst, op0=ALU.subtract, op1=ALU.mult))
                step(v.tensor_reduce(scratch, dst, AX, ALU.min))
                step(v.scalar_tensor_tensor(out=dst, in0=iota_n, scalar=100.0, in1=scratch.to_broadcast([P, TC, n]),
                                            op0=ALU.subtract, op1=ALU.is_equal))

            def router(l):
                dve.wait_ge(sem("gains2_in"), 64)
                for i in (0, 2):
                    await_full(dve, f"m{l}_xT{i}")
                    freed(take_turned(f"m{l}_xT{i}", xT, i, (1, 4)[l]), f"m{l}_xT{i}")
                await_full(dve, f"m{l}_log")
                W = GROUPS + NE
                freed(v.tensor_copy(logs[:], bank(f"m{l}_log")[:, 0:TC * P].rearrange("p (t n) -> p t n", t=TC)[
                    :, :, 0:W]), f"m{l}_log")
                await_evacuated(dve, f"m{l}_log")
                lc, lf = logs[:, :, 0:GROUPS], logs[:, :, GROUPS:]
                rel = small[:, 0, :, 0:GROUPS]
                hot_g = small[:, 0, :, 4:8]
                top, pos1, p_top, total = (small[:, 3, :, i:i + 1] for i in range(4))
                hot_a, hot_b, two, gate8 = (small[:, 2, :, 8 * i:8 * i + 8] for i in range(4))
                fine, rest = small[:, 0, :, 8:16], small[:, 0, :, 16:24]
                m1, m2, g1, g2, second = (small[:, 3, :, i:i + 1] for i in (4, 5, 6, 7, 8))
                step(v.tensor_reduce(top, lc, AX, ALU.max))
                v.tensor_tensor(rel, lc, top.to_broadcast([P, TC, GROUPS]), ALU.subtract).then_inc(
                    sem("coarse_rel"), 1)
                first_of(hot_g, lc, top, pos1, GROUPS)
                pick = small[:, 1, :, :]
                for t in range(TC):
                    ins = v.tensor_tensor(pick[:, t].rearrange("p (g j) -> p g j", g=GROUPS),
                                          lf[:, t].rearrange("p (g j) -> p g j", g=GROUPS),
                                          hot_g[:, t].unsqueeze(2).to_broadcast([P, GROUPS, PER]), ALU.mult)
                step(ins)
                step(v.tensor_reduce(fine, pick.rearrange("p t (g j) -> p t j g", g=GROUPS), AX, ALU.add))
                step(v.tensor_reduce(m1, fine, AX, ALU.max))
                first_of(hot_a, fine, m1, pos1, PER)
                step(v.scalar_tensor_tensor(out=rest, in0=hot_a, scalar=NEG, in1=fine, op0=ALU.mult, op1=ALU.add))
                step(v.tensor_reduce(m2, rest, AX, ALU.max))
                v.tensor_tensor(second, m2, m1, ALU.subtract).then_inc(sem("second_rel"), 1)
                first_of(hot_b, rest, m2, pos1, PER)
                step(v.tensor_tensor(two, hot_a, hot_b, ALU.add))

                def spread(dst, eight):
                    for t in range(TC):
                        ins = v.tensor_tensor(dst[:, t, 0:NE].rearrange("p (g j) -> p g j", g=GROUPS),
                                              hot_g[:, t].unsqueeze(2).to_broadcast([P, GROUPS, PER]),
                                              eight[:, t].unsqueeze(1).to_broadcast([P, GROUPS, PER]), ALU.mult)
                    return ins

                spread(member, two).then_inc(sem("member"), 1)
                dve.wait_ge(sem("coarse_exp"), l + 1)
                step(v.tensor_reduce(total, rel, AX, ALU.add))
                dve.wait_ge(sem("second_exp"), l + 1)
                step(v.tensor_scalar(g2, second, 1.0, None, ALU.add))
                step(v.tensor_tensor(g2, g2, total, ALU.mult))
                step(v.reciprocal(g1, g2))
                step(v.tensor_tensor(g2, g1, second, ALU.mult))
                step(v.tensor_tensor(gate8, hot_a, g1.to_broadcast([P, TC, PER]), ALU.mult))
                step(v.tensor_tensor(rest, hot_b, g2.to_broadcast([P, TC, PER]), ALU.mult))
                step(v.tensor_tensor(gate8, gate8, rest, ALU.add))
                step(spread(gates, gate8))
                await_full(dve, f"m{l}_pos")
                b = bank(f"m{l}_pos")
                step(v.tensor_tensor(place[:, :, 0:NE], b[:, 0:2 * NE].rearrange("p (t e) -> p t e", t=TC), member[:],
                                     ALU.mult))
                step(v.tensor_scalar(place[:, :, 0:NE], place[:, :, 0:NE], -1.0, None, ALU.add))
                freed(v.tensor_copy(counts[:], b[:, 2 * NE:3 * NE]), f"m{l}_pos")
                await_evacuated(dve, f"m{l}_pos")
                v.tensor_copy(ovb_seen[:], stat[:, 0, 0:1]).then_inc(sem("routed"), 1)

            def rounds(ph, gain):
                span = UNROLL * PIECES
                steps = 1 * UNROLL
                sel4 = sel.rearrange("p t (j s) -> p t j s", j=JB)
                wsel4 = wsel.rearrange("p t (j s) -> p t j s", j=JB)
                s_bc = iota[:].unsqueeze(1).to_broadcast([P, JB, SLOTS])
                with dve.Fori(0, ph.n_iter) as it:
                    link = Steps(dve, ph.steps, steps * (it + ph.before // UNROLL))
                    for u in range(UNROLL):
                        r = UNROLL * it + u + ph.before + START
                        cols = bass.ds(ph.col0 + JB * (UNROLL * it + u), JB)
                        dve.wait_ge(ph.wsel_turned, r)
                        for t in range(TC):
                            ins = v.tensor_tensor(sel4[:, t], s_bc,
                                                  place[:, t, cols].unsqueeze(2).to_broadcast([P, JB, SLOTS]),
                                                  ALU.is_equal)
                        link(ins)
                        for t in range(TC):
                            ins = v.tensor_tensor(wsel4[:, t], sel4[:, t],
                                                  gates[:, t, cols].unsqueeze(2).to_broadcast([P, JB, SLOTS]),
                                                  ALU.mult)
                        ins.then_inc(ph.sel_ready, 1)
                        dve.wait_ge(ph.gathered, r + 1)
                        dve.wait_ge(ph.pieces_used, ph.used(span * it + max(u * PIECES - 4, 0)))
                        for a in range(2):
                            cs = slice(4 * a, 4 * a + 4)
                            ins = v.tensor_tensor(xgT[:, cs, :], PS[:, 4 + a, :].rearrange("p (c s) -> p c s", c=4),
                                                  gains[:, gain, cs].unsqueeze(2).to_broadcast([P, 4, P]), ALU.mult)
                        ins.then_inc(ph.xg_ready, 1)
                        dve.wait_ge(ph.silu_done, r + 1)
                        dve.wait_ge(ph.hid_turned, r)
                        v.tensor_tensor(hid, silu_g, PS[:, 1, :], ALU.mult).then_inc(ph.hid_ready, 1)
                        for t in range(TC):
                            dve.wait_ge(ph.combined, TC * (r - START) + t + 1 + START)
                            v.tensor_tensor(h[:, t, :], h[:, t, :],
                                            PS[:, 4 + 2 * t:6 + 2 * t, :].rearrange("p a b -> p (a b)"),
                                            ALU.add).then_inc(ph.h_added, 1)
                    assert link.n == steps

            def moe(l):
                router(l)
                rounds(main[l], (1, 4)[l])
                dve.wait_ge(sem("tables_ready"), l + 1)
                need = dve.value_load(flag[0:1, 0:1], min_val=0, max_val=EXTRA)
                with dve.If(need > 0):
                    rounds(over[l], (1, 4)[l])
                    dve.wait_ge(over[l].h_added, EXTRA // JB * TC + START)
                dve.wait_ge(main[l].h_added, (l + 1) * ROUNDS * TC + START)

            moe(0)
            for t in range(TC):
                normalise("f", t)
            for i in range(4):
                await_full(dve, f"f_xT{i}")
                take_turned(f"f_xT{i}", xT, i, 3).then_inc(sem("foxT_ready"), 1)
                freed(take_turned(f"f_xT{i}", kvT, i, 2), f"f_xT{i}")
            await_full(dve, "f_f")
            dve.wait_ge(sem("wf_in"), 32)
            freed(v.tensor_scalar(lfT, bank("f_f")[0:FH, 0:T], bf[:, 0:1], None, ALU.add), "f_f")
            await_evacuated(dve, "f_f")
            v.tensor_copy(mx_f[0:FH, 0, 0:1], lfT[:, 0:1]).then_inc(sem("f_z"), 1)
            dve.wait_ge(sem("f_soft"), 1)
            v.scalar_tensor_tensor(out=lfT, in0=lfT, scalar=0.0, in1=c_neg[:], op0=ALU.min,
                                   op1=ALU.subtract).then_inc(sem("lfT_ready"), 1)
            await_full(dve, "f_lf")
            freed(v.tensor_copy(lf_n[:], bank("f_lf")[:, 0:TC * FH].rearrange("p (t n) -> p t n", t=TC)), "f_lf")
            for i in range(2):
                for t in range(TC):
                    await_full(dve, f"f_v{i}{t}")
                    freed(v.tensor_copy(v_f[:, t, i * HALF:(i + 1) * HALF], bank(f"f_v{i}{t}")), f"f_v{i}{t}")
            dve.wait_ge(sem("qk_halves"), 1)
            for i in range(4):
                await_full(dve, f"f_q{i}")
                src = bank(f"f_q{i}").rearrange("p (u t) -> p u t", u=2)
                dst = q_f[0:FD, 4 * i:4 * i + 4, :].rearrange("p (u o) t -> p u o t", o=2)
                v.tensor_copy(dst[:, :, 0, :], src[0:FD])
                freed(v.tensor_copy(dst[:, :, 1, :], src[FD:P]), f"f_q{i}")
            for i in range(FH + 3):
                if i < FH:
                    await_full(dve, f"f_s{i}")
                    if i >= 3:
                        dve.wait_ge(sem("exp_done"), i - 2)
                    b = bank(f"f_s{i}")
                    for t, (c0, c1) in enumerate(((0, P), (P, 3 * P))):
                        ins = v.tensor_tensor_reduce(out=s_f[:, i % 3, c0:c1], in0=b[:, c0:c1], in1=causal[:, c0:c1],
                                                     scale=float(FD) ** -0.5, scalar=NEG, op0=ALU.add, op1=ALU.max,
                                                     accum_out=mx_f[:, i, t:t + 1])
                    freed(ins, f"f_s{i}")
                    await_evacuated(dve, f"f_s{i}")
                    v.tensor_scalar(nm_f[:, i, :], mx_f[:, i, :], -1.0, None, ALU.mult).then_inc(sem("nm_ready"), 1)
                if 1 <= i <= FH:
                    n = i - 1
                    dve.wait_ge(sem("exp_done"), n + 1)
                    step(v.reciprocal(inv_f[:, n, :], sum_f[:, n, :]))
                    v.tensor_scalar(p_f[:, n % 3, 0:P], p_f[:, n % 3, 0:P], inv_f[:, n, 0:1], None, ALU.mult)
                    v.tensor_scalar(p_f[:, n % 3, P:], p_f[:, n % 3, P:], inv_f[:, n, 1:2], None,
                                    ALU.mult).then_inc(sem("p_ready"), 1)
                if i >= 4 and i % 2 == 0:
                    m = (i - 4) // 2
                    if m == 0:
                        await_evacuated(dve, *[f"f_g{j}" for j in range(4)])
                    await_full(dve, f"f_o{m}")
                    freed(v.tensor_tensor(gT_f[:, m, :], gT_f[:, m, :], bank(f"f_o{m}")[:, 0:T], ALU.mult), f"f_o{m}")
            add_to_h("f", "m1")
            moe(1)
            dve.wait_ge(sem("final_in"), 16)
            for t in range(TC):
                mean_square("last", t)
                inverse("last", t)
                v.scalar_tensor_tensor(out=y_out[:, t, :], in0=h[:, t, :], scalar=stat[:, 2, t:t + 1], in1=final_g,
                                       op0=ALU.mult, op1=ALU.mult).then_inc(sem("out_ready"), 1)


_INS = ['x', 'gla_norm', 'gla_w_in', 'gla_w_a2', 'gla_b_a', 'gla_out_norm', 'gla_w_out', 'kv_norm', 'kv_w',
        'kv_b_f', 'fox_norm', 'fox_w_in', 'fox_w_out', 'ffn_norm', 'router_coarse_w', 'router_coarse_b',
        'router_fine_w', 'router_fine_b', 'expert_w_gate', 'expert_w_up', 'expert_w_down', 'final_norm']


def kernel(**inputs):
    import numpy as _np
    import concourse.bacc as _bacc
    from concourse.bass_utils import run_bass_kernel_spmd as _run

    nc = _bacc.Bacc("TRN2", target_bir_lowering=False, num_devices=1, dynamic_dma_scratch_size=1024)
    arrays, args = {}, []
    for name in _INS:
        a = _np.ascontiguousarray(inputs[name])
        arrays[f"in_{name}_dram"] = a
        args.append(nc.dram_tensor(f"in_{name}_dram", a.shape, mybir.dt.from_np(a.dtype), kind="ExternalInput").ap())
    out = nc.dram_tensor("out_0_dram", (1, T, D), F32, kind="ExternalOutput").ap()
    trunk(nc, *args, out)
    r = _run(nc, [arrays], core_ids=[0])
    return r.results[0]["out_0_dram"]
```

```python
from contextlib import ExitStack

import concourse.bass as bass
from concourse import mybir

F32 = mybir.dt.float32
I32 = mybir.dt.int32
ALU = mybir.AluOpType
ACT = mybir.ActivationFunctionType
AX = mybir.AxisListType.X

P = 128
T = 256
TC = T // P
D = 1024
DC = D // P
HALF = 512
EPS = 1e-6
GH, GDK, GDV, RANK = 4, 128, 256, 16
TAU = 16.0
QKW, VW = GH * GDK, GH * GDV
RB = 32
REF = 17
NRB = T // RB
FH, FD = 16, 64
GROUPS, PER = 4, 8
NE = GROUPS * PER
FF = 512
FC = FF // P
SLOTS = 32
JB = P // SLOTS
ROUNDS = NE // JB
EXTRA = 16
KMAX = T // SLOTS - 1
RING = 8
SLOT = 4096
PIECES = 12
UNROLL = 2
GLA_PIECES, FOX_PIECES = 8, 10
ANNEX = (6, 7)
RING_FILLS = ROUNDS * PIECES - len(ANNEX)
FOX_BASE = GLA_PIECES + RING_FILLS
MOE_BASE = [GLA_PIECES, FOX_BASE + FOX_PIECES]
START = 1
NEG = -1e30


X_JOBS = [f"xT{t}{u}" for t in range(TC) for u in range(2)]


EARLY = 3
PBUF = 4
OUT_BETWEEN = {13: (0, 0), 15: (0, 1), 16: (1, 0), 18: (1, 1)}


def bank_jobs():
    order = []

    def add(names, banks):
        order.extend(zip(names, banks))

    def router(l):
        add([f"m{l}_{x}" for x in X_JOBS], ([0, 1, 2, 3], [3, 4, 5, 7])[l])
        add([f"m{l}_log", f"m{l}_pos"], ([4, 5], [6, 1])[l])

    add([f"g_{x}" for x in X_JOBS], [0, 1, 2, 3])
    add(["g_a", "g_gain"], [4, 5])
    add(["g_q0", "g_q1", "g_k0", "g_k1"], [6, 7, 0, 1])
    add(["g_z0", "g_z1"], [2, 3])
    add(["g_v00", "g_v01", "g_cum0", "g_cum1", "g_v10", "g_v11"], [4, 5, 6, 7, 0, 1])
    add([f"g_s{h}" for h in range(GH)], [2, 3, 4, 5])
    add(["g_r00", "g_r01"], [6, 7])
    add([f"g_sT{h}" for h in range(GH)], [0, 1, 2, 3])
    add([f"g_o{h}" for h in range(GH)], [4, 5, 6, 7])
    add(["g_r10", "g_oT0", "g_oT1", "g_r11", "g_y00", "g_y01"], [0, 2, 3, 1, 4, 5])
    add(["g_oT2", "g_oT3", "g_y10", "g_y11"], [0, 1, 6, 7])
    router(0)
    add([f"f_{x}" for x in X_JOBS], [0, 1, 2, 3])
    add(["f_f"], [4])
    add([f"f_k{i}" for i in range(4)], [5, 6, 7, 4])
    add(["f_lf", "f_c"], [5, 6])
    add(["f_v00", "f_v01", "f_v10", "f_v11"], [7, 4, 5, 6])
    add([f"f_q{i}" for i in range(4)], [7, 0, 1, 2])
    add(["f_g0", "f_g1"], [3, 4])
    for i in range(FH + 4):
        if i == EARLY:
            add(["f_g2", "f_g3"], [5, 6])
        if i < FH:
            add([f"f_s{i}"], [i % 3])
        if 3 <= i <= FH + 2:
            add([f"f_pT{i - 3}"], [(7, 3)[(i - 3) % 2]])
        if i >= 5 and i % 2 == 1:
            add([f"f_o{(i - 5) // 2}"], [4 + ((i - 5) // 2) % 2])
        if i in OUT_BETWEEN:
            add(["f_y%d%d" % OUT_BETWEEN[i]], [{(0, 0): 6, (0, 1): 1, (1, 0): 2, (1, 1): 0}[OUT_BETWEEN[i]]])
    router(1)
    used, table = [0] * 8, {}
    for name, bank in order:
        used[bank] += 1
        table[name] = (bank, used[bank])
    return table


JOBS = bank_jobs()
PIECE_JOB = {0: "g_q1", 1: "g_k1", 2: "g_v01", 3: "g_v11", 4: "g_r01", 5: "g_r11", 7: "g_y11"}
PIECE_JOB.update({FOX_BASE + i: n for i, n in enumerate(
    ["f_k1", "f_k3", "f_v01", "f_v11", "f_q1", "f_q3", "f_g1", "f_g3"])})
PIECE_JOB[FOX_BASE + 9] = "f_y11"
W_OUT_LEFT = {6: 1, FOX_BASE + 8: 2}


NORMS = {"g": 0, "go": 2, "m0": 6, "f": 8, "m1": 10, "last": 12}
XN = {"g": 1, "m0": 2, "f": 3, "m1": 4}


WAKE = {"start": 12, "router": 16, "down": 10, "boundary": 8}


class Steps:

    def __init__(self, eng, sem, base=0):
        self.eng, self.sem, self.base, self.n = eng, sem, base, 0

    def mark(self, ins):
        self.n += 1
        ins.then_inc(self.sem, 1)
        return self.n

    def reach(self, n):
        self.eng.wait_ge(self.sem, self.base + n)

    def __call__(self, ins):
        self.reach(self.mark(ins))


def trunk(nc, x, gla_norm, gla_w_in, gla_w_a2, gla_b_a, gla_out_norm, gla_w_out, kv_norm, kv_w, kv_b_f,
          fox_norm, fox_w_in, fox_w_out, ffn_norm, router_coarse_w, router_coarse_b, router_fine_w,
          router_fine_b, expert_w_gate, expert_w_up, expert_w_down, final_norm, out):
    with ExitStack() as ctx:
        def sb(name, shape, dt=F32):
            return ctx.enter_context(nc.sbuf_tensor(name, shape, dt))

        made = {}

        def sem(name):
            if name not in made:
                made[name] = ctx.enter_context(nc.semaphore(name))
            return made[name]

        ring = sb("ring", [P, RING, SLOT])
        h = sb("h", [P, TC, D])
        h8 = h[:].rearrange("p t (q c) -> p t c q", c=DC)
        xn = sb("xn", [P, TC, DC, P])
        xT = sb("xT", [P, DC, T])
        area = sb("area", [P, 12800])
        ident = sb("ident", [P, P])
        upto = sb("upto", [P, 2 * P])
        lower = sb("lower", [P, P])
        causal = sb("causal", [P, 3 * P])
        iota = sb("iota", [P, NE])
        iota_i = sb("iota_i", [P, NE], I32)
        slot = sb("slot", [P, SLOTS])
        limits = sb("limits", [P, KMAX])
        gains = sb("gains", [P, 6, DC])
        wa = sb("wa", [P, DC, RANK])
        wf = sb("wf", [P, DC, FH])
        wa2 = sb("wa2", [RANK + 1, QKW])
        aT = sb("aT", [RANK + 1, T])
        bf = sb("bf", [FH, 1])
        wr = sb("wr", [P, 2, DC, GROUPS + NE])
        br = sb("br", [P, 2, GROUPS + NE])
        stat = sb("stat", [P, 3, 8])
        out_gain = sb("out_gain", [DC, P])
        ids = sb("ids", [1, EXTRA], I32)
        flag = sb("flag", [1, 1], I32)
        PS = ctx.enter_context(nc.psum_tensor("ps", [P, 8, HALF], F32))

        def carve(at, *shape):
            n = 1
            for s in shape:
                n *= s
            assert at + n <= 12800, (at, n)
            v = area[:, at:at + n]
            if len(shape) == 2:
                v = v.rearrange("p (a b) -> p a b", a=shape[0])
            if len(shape) == 3:
                v = v.rearrange("p (a b c) -> p a b c", a=shape[0], b=shape[1])
            return v

        qT, kT = carve(0, GH, T), carve(1024, GH, T)
        v_g = carve(2048, TC, D)
        gate_r = carve(4096, TC, D)
        la = carve(6144, TC, QKW)
        cumT = carve(7168, GH, T)
        qs = carve(8192, GH, T)
        kb56 = carve(9216, 4 * 13 * RB)
        sS = carve(10880, GH, 3 * P)
        sT = carve(9216, GH, 3 * P)
        xflat = xn[:].rearrange("p a b c -> p (a b c)")
        lflat = la.rearrange("p a b -> p (a b)")
        kb, at = [], 0
        for b in range(NRB):
            n = GH * RB * (b + 1)
            if b <= 4:
                src, at0 = xflat, at
            elif b <= 6:
                src, at0 = kb56, 0 if b == 5 else GH * RB * 6
            else:
                src, at0 = lflat, 0
            kb.append(src[:, at0:at0 + n].rearrange("p (a b) -> p a b", a=GH))
            at += n
        o_g = xn[:].rearrange("p t a b -> p t (a b)")
        oT_g = [carve(8192, 4, T)[:, c, :] for c in range(4)] + [xT[:, c, :] for c in range(4, DC)]
        q_f, k_f = carve(0, FH, T), carve(4096, FH, T)
        v_f = carve(8192, TC, D)
        kvT = carve(10240, DC, T)
        p_f = carve(10240, PBUF, 3 * P)
        pT_f = xT[:].rearrange("p a b -> p (a b)")[:, 0:PBUF * 3 * P].rearrange("p (a b) -> p a b", a=PBUF)
        gT_f = xn[:].rearrange("p t a b -> p (t a b)").rearrange("p (m t) -> p m t", m=DC)
        lfT = carve(12544, T)[0:FH]
        mx_f = sb("mx_f", [P, FH, 2])
        nm_f = sb("nm_f", [P, FH, 2])
        sum_f = sb("sum_f", [P, FH, 2])
        inv_f = sb("inv_f", [P, FH, 2])
        lf_n = sb("lf_n", [P, TC, FH])
        c_neg = sb("c_neg", [FH, T])
        xgT = carve(8192, DC, P)
        silu_g = carve(9216, FF)
        hid = carve(9728, FF)
        hidT = carve(10240, FC, P)
        y_e = carve(10752, D)
        sel = carve(11776, TC, JB * SLOTS)
        wsel = carve(12032, TC, JB * SLOTS)
        wselT = carve(12288, T)
        lc = sb("lc", [P, TC, GROUPS])
        rel = sb("rel", [P, TC, GROUPS])
        hot_g = sb("hot_g", [P, TC, GROUPS])
        best_g = sb("best_g", [P, 3, TC])
        lf = sb("lf", [P, TC * GROUPS, PER])
        hot_a = sb("hot_a", [P, TC * GROUPS, PER])
        rest = sb("rest", [P, TC * GROUPS, PER])
        hot_b = sb("hot_b", [P, TC * GROUPS, PER])
        best_f = sb("best_f", [P, 6, TC * GROUPS])
        place = sb("place", [P, TC, NE + EXTRA])
        gates = sb("gates", [P, TC, NE + EXTRA])
        member = sb("member", [P, TC, NE])
        counts = sb("counts", [P, NE])
        xTf = xT[:].rearrange("p a b -> p (a b)")
        t_a = xTf[:, 0:EXTRA * NE].rearrange("p (b e) -> p b e", b=EXTRA)
        t_hot = xTf[:, 512:1024].rearrange("p (b e) -> p b e", b=EXTRA)
        t_k = xTf[:, 1024:1536].rearrange("p (b e) -> p b e", b=EXTRA)
        ovr = sb("ovr", [P, 4, NE])
        ovb = sb("ovb", [P, EXTRA])
        annex = [carve(SLOT * i, SLOT) for i in range(2)]
        final_g = carve(0, D)
        y_out = xn[:].rearrange("p t a b -> p t (a b)")

        landed = [sem(f"landed{s}") for s in range(RING)]
        annex_landed = [sem(f"annex_landed{i}") for i in range(2)]
        bank_full = [sem(f"bank_full{b}") for b in range(8)]
        bank_free = [sem(f"bank_free{b}") for b in range(8)]

        out_ready = [sem(f"out_ready{t}") for t in range(TC)]

        def bank(name):
            return PS[:, JOBS[name][0], :]

        def await_full(eng, *names):
            for n in names:
                eng.wait_ge(bank_full[JOBS[n][0]], JOBS[n][1])

        def await_evacuated(eng, *names):
            for n in names:
                eng.wait_ge(bank_free[JOBS[n][0]], JOBS[n][1])

        def freed(ins, name):
            ins.then_inc(bank_free[JOBS[name][0]], 1)

        class Phase:

            def __init__(self, tag, n_iter, layer, base, overflow):
                self.tag, self.n_iter, self.layer, self.base, self.overflow = tag, n_iter, layer, base, overflow
                self.sel_ready = sem(f"{tag}_sel_ready")
                self.wsel_ready = sem(f"{tag}_wsel_ready")
                self.gathered = sem(f"{tag}_gathered")
                self.xg_ready = sem(f"{tag}_xg_ready")
                self.wsel_turned = sem(f"{tag}_wsel_turned")
                self.wselT_ready = sem(f"{tag}_wselT_ready")
                self.silu_done = sem(f"{tag}_silu_done")
                self.hid_ready = sem(f"{tag}_hid_ready")
                self.hid_turned = sem(f"{tag}_hid_turned")
                self.hidT_ready = sem(f"{tag}_hidT_ready")
                self.y_left_full = sem(f"{tag}_y_left_full")
                self.y_ready = sem(f"{tag}_y_ready")
                self.combined = sem(f"{tag}_combined")
                self.h_added = sem(f"{tag}_h_added")
                self.pieces_used = sem(f"{tag}_pieces_used")
                self.before = 0 if overflow else layer * ROUNDS
                self.landed = [sem(f"{tag}_landed{s}") for s in range(RING)] if overflow else landed
                self.col0 = NE if overflow else 0

            def home(self, it, k):
                if self.overflow:
                    return ring[:, k % RING, :], self.landed[k % RING], 16 * JB * (3 * it + k // RING + 1)
                peeled = isinstance(it, int)
                if peeled and k in ANNEX:
                    return annex[k - ANNEX[0]], annex_landed[k - ANNEX[0]], 16 * (self.layer + 1)
                fill = self.base + (k if peeled and k < ANNEX[0] else k - len(ANNEX))
                return ring[:, fill % RING, :], landed[fill % RING], 16 * (3 * it + fill // RING + 1)

            def iterations(self, eng, body):
                first = 0 if self.overflow else 1
                if first:
                    body(0)
                with eng.Fori(first, self.n_iter) as it:
                    body(it)

            def used(self, n):
                return n + self.before * PIECES + START

        main = [Phase("moe", ROUNDS // UNROLL, l, MOE_BASE[l], False) for l in range(2)]
        over = [Phase(f"ovf{l}", EXTRA // JB // UNROLL, l, 0, True) for l in range(2)]

        QUARTERS = 2 * TC

        def at_round(r, per_round, n):
            return per_round * (r - START) + n + START

        block = ctx.enter_context(nc.Block())

        @block.sync
        def _(sp):
            def small_load(dst, src, name):
                sp.dma_start(dst, src).then_inc(sem(name), 16)

            def piece(i, dst, src):
                if i >= RING:
                    await_used(i - RING)
                sp.dma_start(dst, src).then_inc(landed[i % RING], 16)

            def await_used(i):
                if i in W_OUT_LEFT:
                    sp.wait_ge(sem("w_out_used"), W_OUT_LEFT[i])
                    return
                if i in PIECE_JOB:
                    await_full(sp, PIECE_JOB[i])
                    return
                l = 0 if i < FOX_BASE else 1
                n = i - MOE_BASE[l]
                sp.wait_ge(main[l].pieces_used, main[l].used(n + 1 if n < ANNEX[0] else n + 1 + len(ANNEX)))

            def cols(i, w, n0):
                piece(i, ring[:, i % RING, :].rearrange("p (c n) -> p c n", c=DC),
                      w.rearrange("(p c) n -> p c n", c=DC)[:, :, n0:n0 + HALF])

            def rows(i, w, c0, order):
                piece(i, ring[:, i % RING, :].rearrange("p (c n) -> p c n", c=4),
                      w.rearrange(f"({order}) n -> p c n", p=P)[:, c0:c0 + 4, :])

            def expert_piece(ph, it, k, experts_of_round=None):
                r, k12 = UNROLL * it + k // PIECES, k % PIECES
                dst, arrived, _ = ph.home(it, k)
                dst = dst.rearrange("p (j n) -> p j n", j=JB)
                if ph.overflow:
                    for j, e in enumerate(experts_of_round):
                        sp.dma_start(dst[:, j:j + 1, :], expert_source(ph.layer, e, 1, k12)).then_inc(arrived, 16)
                else:
                    sp.dma_start(dst, expert_source(ph.layer, JB * r, JB, k12)).then_inc(arrived, 16)

            def expert_source(layer, e, n, k12):
                if k12 < 8:
                    w = expert_w_gate if k12 % 2 == 0 else expert_w_up
                    cc = k12 // 2
                    return w[layer].rearrange("e (p c) f -> p e (c f)", c=DC)[
                        :, bass.ds(e, n), 2 * cc * FF:2 * (cc + 1) * FF]
                f = k12 - 8
                return expert_w_down[layer].rearrange("e (c p) d -> p e c d", p=P)[
                    :, bass.ds(e, n), f, :]

            def experts(l):
                ph = main[l]
                span = UNROLL * PIECES
                for k in range(span):
                    if k in ANNEX:
                        if l == 0:
                            await_evacuated(sp, *[f"g_o{hh}" for hh in range(GH)])
                        else:
                            await_full(sp, f"f_s{FH - 2}", f"f_s{FH - 1}")
                    else:
                        await_used(ph.base + (k if k < ANNEX[0] else k - len(ANNEX)) - RING)
                    expert_piece(ph, 0, k)
                with sp.Fori(1, ph.n_iter) as it:
                    for k in range(span):
                        sp.wait_ge(ph.pieces_used, ph.used(span * it + k - RING + 1))
                        expert_piece(ph, it, k)

            def overflow(l):
                ph = over[l]
                span = UNROLL * PIECES
                sp.wait_ge(sem("tables_ready"), l + 1)
                need = sp.value_load(flag[0:1, 0:1], min_val=0, max_val=EXTRA)
                with sp.If(need > 0):
                    sp.wait_ge(main[l].pieces_used, main[l].used(ROUNDS * PIECES))
                    with sp.Fori(0, ph.n_iter) as it:
                        for k in range(span):
                            if k % PIECES == 0:
                                first = JB * (UNROLL * it + k // PIECES)
                                held = [sp.value_load(ids[0:1, bass.ds(first + j, 1)], min_val=0, max_val=NE - 1)
                                        for j in range(JB)]
                            sp.wait_ge(ph.pieces_used, ph.used(span * it + max(k - RING + 1, 0)))
                            expert_piece(ph, it, k, held)
                    sp.wait_ge(ph.pieces_used, ph.used(span * ph.n_iter))

            for t in range(TC):
                small_load(h[:, t, :], x[0, t * P:(t + 1) * P, :], f"x_in{t}")
            small_load(gains[:, 0, :], gla_norm[0].rearrange("(p c) -> p c", c=DC), "gains_in")
            small_load(out_gain[:], gla_out_norm[0].rearrange("h (u p) -> (h u) p", p=P), "outg_in")
            small_load(wa[:], gla_w_in[0].rearrange("(p c) n -> p c n", c=DC)[:, :, 2 * QKW + 2 * VW:], "wa_in")
            cols(0, gla_w_in[0], 0)
            small_load(wa2[0:RANK, :], gla_w_a2[0], "wa2_in")
            small_load(wa2[RANK:RANK + 1, :], gla_b_a, "wa2_in")
            cols(1, gla_w_in[0], QKW)
            for i in range(4):
                cols(2 + i, gla_w_in[0], 2 * QKW + i * HALF)
            for i, g in ((1, ffn_norm[0]), (2, kv_norm), (3, fox_norm[0]), (4, ffn_norm[1])):
                small_load(gains[:, i, :], g.rearrange("(p c) -> p c", c=DC), "gains2_in")
            for l in range(2):
                small_load(wr[:, l, :, 0:GROUPS], router_coarse_w[l].rearrange("(p c) g -> p c g", c=DC), "wr_in")
                small_load(wr[:, l, :, GROUPS:], router_fine_w[l].rearrange("(p c) g -> p c g", c=DC), "wr_in")
                small_load(br[:, l, 0:GROUPS], router_coarse_b[l].rearrange("(a g) -> a g", a=1).to_broadcast(
                    [P, GROUPS]), "wr_in")
                small_load(br[:, l, GROUPS:], router_fine_b[l].rearrange("(a e) -> a e", a=1).to_broadcast(
                    [P, NE]), "wr_in")
            small_load(wf[:], kv_w.rearrange("(p c) n -> p c n", c=DC)[:, :, 2 * D:], "wf_in")
            small_load(bf[:], kv_b_f.rearrange("(g a) -> g a", a=1), "wf_in")
            rows(6, gla_w_out[0], 0, "c p")
            rows(7, gla_w_out[0], 4, "c p")
            experts(0)
            overflow(0)
            for i, (w, n0) in enumerate([(kv_w, 0), (kv_w, HALF), (kv_w, D), (kv_w, D + HALF), (fox_w_in[0], 0),
                                         (fox_w_in[0], HALF), (fox_w_in[0], D), (fox_w_in[0], D + HALF)]):
                cols(FOX_BASE + i, w, n0)
            rows(FOX_BASE + 8, fox_w_out[0], 0, "c p")
            rows(FOX_BASE + 9, fox_w_out[0], 4, "c p")
            experts(1)
            overflow(1)
            sp.wait_ge(main[1].pieces_used, main[1].used(ROUNDS * PIECES - RING))
            small_load(final_g, final_norm.rearrange("(a d) -> a d", a=1).to_broadcast([P, D]), "final_in")
            for t in range(TC):
                sp.wait_ge(out_ready[t], 1)
                sp.dma_start(out[0, t * P:(t + 1) * P, :], y_out[:, t, :]).then_inc(sem("stored"), 16)
            sp.wait_ge(sem("stored"), 16 * TC)

        @block.gpsimd
        def _(pool):
            g = nc.gpsimd
            step = Steps(pool, sem("pool_steps"))
            step(g.memset(ident[:], 0.0))
            g.affine_select(out=ident[:], in_=ident[:], compare_op=ALU.not_equal, fill=1.0, base=0,
                            pattern=[[-1, P]], channel_multiplier=1).then_inc(sem("ident_ready"), 1)
            g.memset(aT[:], 1.0).then_inc(sem("aT_ones"), 1)
            step(g.memset(upto[:], 1.0))
            g.affine_select(out=upto[:, 0:P], in_=upto[:, 0:P], compare_op=ALU.is_ge, fill=0.0, base=0,
                            pattern=[[1, P]], channel_multiplier=-1)
            step(g.memset(lower[:], 1.0))
            step(g.affine_select(out=lower[:], in_=lower[:], compare_op=ALU.is_ge, fill=0.0, base=0,
                                 pattern=[[-1, P]], channel_multiplier=1))
            step(g.memset(causal[:], 0.0))
            for c0 in (0, 2 * P):
                g.affine_select(out=causal[:, c0:c0 + P], in_=causal[:, c0:c0 + P], compare_op=ALU.is_ge,
                                fill=NEG, base=0, pattern=[[-1, P]], channel_multiplier=1)
            step(g.iota(iota_i[:], pattern=[[1, NE]], base=0, channel_multiplier=0))
            step(g.tensor_copy(iota[:], iota_i[:]))
            g.tensor_scalar(slot[:], iota[:, 0:SLOTS], 1.0, None, ALU.add)
            g.tensor_scalar(limits[:], iota[:, 0:KMAX], float(SLOTS), float(SLOTS), ALU.mult,
                            ALU.add).then_inc(sem("consts_ready"), 1)
            pool.wait_ge(sem("consts_ready"), 1)

            def tables(l):
                await_evacuated(pool, f"m{l}_pos")
                pool.wait_ge(main[l].wsel_ready, l * ROUNDS + 1 + START)
                more, start, end, tmp = (ovr[:, i, :] for i in range(4))
                over_k = t_a.rearrange("p b e -> p (b e)")[:, 0:NE * KMAX].rearrange("p (e k) -> p e k", k=KMAX)
                step(g.tensor_tensor(over_k, counts[:].unsqueeze(2).to_broadcast([P, NE, KMAX]),
                                     limits[:].unsqueeze(1).to_broadcast([P, NE, KMAX]), ALU.subtract))
                step(g.tensor_scalar(over_k, over_k, 0.0, None, ALU.is_gt))
                step(g.tensor_copy(more, over_k[:, :, 0]))
                for k in range(1, KMAX):
                    step(g.tensor_tensor(more, more, over_k[:, :, k], ALU.add))
                src = more
                d = 1
                step(g.tensor_copy(end, more))
                while d < NE:
                    step(g.tensor_copy(tmp, end))
                    step(g.tensor_tensor(end[:, d:NE], tmp[:, d:NE], tmp[:, 0:NE - d], ALU.add))
                    d *= 2
                step(g.tensor_tensor(start, end, more, ALU.subtract))
                b_bc = iota[:, 0:EXTRA].unsqueeze(2).to_broadcast([P, EXTRA, NE])

                def bc(v):
                    return v.unsqueeze(1).to_broadcast([P, EXTRA, NE])

                step(g.tensor_tensor(t_k, b_bc, bc(start), ALU.subtract))
                step(g.tensor_scalar(t_hot, t_k, 0.0, None, ALU.is_ge))
                step(g.tensor_tensor(t_a, b_bc, bc(end), ALU.subtract))
                step(g.tensor_scalar(t_a, t_a, 0.0, None, ALU.is_lt))
                step(g.tensor_tensor(t_hot, t_hot, t_a, ALU.mult))
                step(g.tensor_scalar(t_k, t_k, float(SLOTS), float(SLOTS), ALU.mult, ALU.add))

                def over_experts(dst):
                    n = NE
                    while n > 1:
                        n //= 2
                        o = dst if n == 1 else t_a[:, :, 0:n]
                        i0, i1 = t_a[:, :, 0:n], t_a[:, :, n:2 * n]
                        if n == 1:
                            o = dst.unsqueeze(2)
                        step(g.tensor_tensor(o, i0, i1, ALU.add))

                for t in range(TC):
                    step(g.tensor_tensor(t_a, bc(place[:, t, 0:NE]), t_k, ALU.subtract))
                    step(g.tensor_tensor(t_a, t_a, t_hot, ALU.mult))
                    over_experts(place[:, t, NE:])
                    step(g.tensor_tensor(t_a, bc(gates[:, t, 0:NE]), t_hot, ALU.mult))
                    over_experts(gates[:, t, NE:])
                step(g.tensor_tensor(t_a, bc(iota[:]), t_hot, ALU.mult))
                over_experts(ovb[:])
                step(g.tensor_copy(ids[:], ovb[0:1, :]))
                g.tensor_copy(flag[:], end[0:1, NE - 1:NE]).then_inc(sem("tables_ready"), 1)

            tables(0)
            pool.wait_ge(sem("tables_ready"), 1)
            pool.wait_ge(main[0].pieces_used, main[0].used(PIECES))
            step(g.memset(k_f[FD:P], 0.0))
            step(g.memset(q_f[FD:P], 0.0))
            g.memset(q_f[FD:FD + 1], 1.0).then_inc(sem("qk_halves"), 1)
            pool.wait_ge(sem("qk_halves"), 1)
            tables(1)
            pool.wait_ge(sem("tables_ready"), 2)

        @block.tensor
        def _(pe):
            for ph in (main[0], *over):
                for counter in (ph.gathered, ph.wsel_turned, ph.hid_turned, ph.y_left_full, ph.combined,
                                ph.pieces_used):
                    pe.sem_inc(counter, START)

            def fill(name):
                b, use = JOBS[name]
                if use > 1:
                    pe.wait_ge(bank_free[b], use - 1)
                return PS[:, b, :]

            def full(mm, name):
                mm.then_inc(bank_full[JOBS[name][0]], 1)

            def await_piece(i):
                pe.wait_ge(landed[i % RING], 16 * (i // RING + 1))

            def stay_awake(b, n):
                for _ in range(n):
                    pe.matmul(b[:, 0:P], ident[:], ident[:], start=True, stop=True)

            def turn(tag, t, src):
                for u in range(2):
                    b = fill(f"{tag}_xT{t}{u}")
                    for c in range(4):
                        mm = pe.transpose(b[:, c * P:(c + 1) * P], src[:, t, 4 * u + c, :], ident[:])
                    full(mm, f"{tag}_xT{t}{u}")

            def turn_x(tag, t):
                pe.wait_ge(sem("xn_ready"), TC * (XN[tag] - 1) + t + 1)
                turn(tag, t, xn)

            def turn_h(tag, l, t):
                await_evacuated(pe, f"{tag}_y{t}0", f"{tag}_y{t}1")
                turn(f"m{l}", t, h8)

            def down_cols(names, i, src):
                await_piece(i)
                w = ring[:, i % RING, :].rearrange("p (c n) -> p c n", c=DC)
                for a, name in enumerate(names):
                    b = fill(name)
                    for u in range(2):
                        n0 = (2 * a + u) * P
                        for c in range(DC):
                            mm = pe.matmul(b[:, u * T:(u + 1) * T], w[:, c, n0:n0 + P], src[:, c, :],
                                           start=(c == 0), stop=(c == DC - 1))
                    full(mm, name)

            def along_cols(names, i, src):
                await_piece(i)
                w = ring[:, i % RING, :].rearrange("p (c n) -> p c n", c=DC)
                for name in names:
                    t = int(name[-1])
                    b = fill(name)
                    for c in range(DC):
                        mm = pe.matmul(b[:, :], src[:, c, t * P:(t + 1) * P], w[:, c, :],
                                       start=(c == 0), stop=(c == DC - 1))
                    full(mm, name)

            def out_part(tag, i, src, half, t, u):
                await_piece(i + half)
                w = ring[:, (i + half) % RING, :].rearrange("p (c n) -> p c n", c=4)
                name = f"{tag}_y{t}{u}"
                b = fill(name) if half == 0 else bank(name)
                for c in range(4):
                    cc = 4 * half + c
                    mm = pe.matmul(b, src[cc][:, t * P:(t + 1) * P], w[:, c, u * HALF:(u + 1) * HALF],
                                   start=(cc == 0), stop=(cc == DC - 1))
                if half == 1:
                    full(mm, name)
                elif (t, u) == (TC - 1, 1):
                    mm.then_inc(sem("w_out_used"), 1)

            def last_out_part(tag, i, src, l):
                out_part(tag, i, src, 1, 0, 0)
                out_part(tag, i, src, 1, 0, 1)
                out_part(tag, i, src, 1, 1, 0)
                turn_h(tag, l, 0)
                out_part(tag, i, src, 1, 1, 1)

            pe.wait_ge(sem("ident_ready"), 1)
            stay_awake(PS[:, 7, :], WAKE["start"])
            for t in range(TC):
                turn_x("g", t)
            b = fill("g_a")
            await_evacuated(pe, *[f"g_{x}" for x in X_JOBS])
            pe.wait_ge(sem("wa_in"), 16)
            for c in range(DC):
                mm = pe.matmul(b[0:RANK, 0:T], wa[:, c, :], xT[:, c, :], start=(c == 0), stop=(c == DC - 1))
            full(mm, "g_a")
            b = fill("g_gain")
            pe.wait_ge(sem("outg_in"), 16)
            full(pe.transpose(b[:, 0:DC], out_gain[:], ident[0:DC, 0:DC]), "g_gain")
            down_cols(["g_q0", "g_q1"], 0, xT)
            down_cols(["g_k0", "g_k1"], 1, xT)
            await_evacuated(pe, "g_a")
            pe.wait_ge(sem("wa2_in"), 32)
            for t in range(TC):
                b = fill(f"g_z{t}")
                full(pe.matmul(b, aT[:, t * P:(t + 1) * P], wa2[:], start=True, stop=True), f"g_z{t}")
            along_cols(["g_v00", "g_v01"], 2, xT)
            pe.wait_ge(sem("consts_ready"), 1)
            await_evacuated(pe, "g_z0", "g_z1")
            for i in range(2):
                b = fill(f"g_cum{i}")
                for u in range(2):
                    hc = slice((2 * i + u) * P, (2 * i + u + 1) * P)
                    pe.matmul(b[:, u * T:(u + 1) * T], la[:, 0, hc], upto[:], start=True, stop=False)
                    mm = pe.matmul(b[:, u * T + P:(u + 1) * T], la[:, 1, hc], upto[:, 0:P], start=False, stop=True)
                full(mm, f"g_cum{i}")
            along_cols(["g_v10", "g_v11"], 3, xT)
            bs = [fill(f"g_s{hh}") for hh in range(GH)]
            pe.wait_ge(sem("qs_ready"), 1)
            for b in range(NRB):
                pe.wait_ge(sem("kb_ready"), b + 1)
                c0 = 0 if b < 4 else P
                q0 = RB * (b % 4)
                for hh in range(GH):
                    mm = pe.matmul(bs[hh][q0:q0 + RB, c0:c0 + RB * (b + 1)], qs[:, hh, RB * b:RB * (b + 1)],
                                   kb[b][:, hh, :], start=True, stop=True)
                    if b == NRB - 1:
                        full(mm, f"g_s{hh}")
            along_cols(["g_r00", "g_r01"], 4, xT)
            await_evacuated(pe, *[f"g_s{hh}" for hh in range(GH)])
            for hh in range(GH):
                b = fill(f"g_sT{hh}")
                for i in range(3):
                    mm = pe.transpose(b[:, i * P:(i + 1) * P], sS[:, hh, i * P:(i + 1) * P], ident[:])
                full(mm, f"g_sT{hh}")
            await_evacuated(pe, "g_v10", "g_v11")
            for hh in range(GH):
                b = fill(f"g_o{hh}")
                await_evacuated(pe, f"g_sT{hh}")
                vc = slice(hh * GDV, (hh + 1) * GDV)
                pe.matmul(b[:, 0:GDV], sT[:, hh, 0:P], v_g[:, 0, vc], start=True, stop=True)
                pe.matmul(b[:, GDV:], sT[:, hh, P:2 * P], v_g[:, 0, vc], start=True, stop=False)
                full(pe.matmul(b[:, GDV:], sT[:, hh, 2 * P:], v_g[:, 1, vc], start=False, stop=True), f"g_o{hh}")
            along_cols(["g_r10"], 5, xT)

            def turn_o(i):
                b = fill(f"g_oT{i}")
                await_evacuated(pe, f"g_o{i}")
                for c in (2 * i, 2 * i + 1):
                    for t in range(TC):
                        at = (c % 2) * T + t * P
                        mm = pe.transpose(b[:, at:at + P], o_g[:, t, c * P:(c + 1) * P], ident[:])
                full(mm, f"g_oT{i}")

            turn_o(0)
            turn_o(1)
            along_cols(["g_r11"], 5, xT)
            await_evacuated(pe, "g_oT0", "g_oT1")
            for u in range(2):
                out_part("g", 6, oT_g, 0, 0, u)
            turn_o(2)
            turn_o(3)
            for u in range(2):
                out_part("g", 6, oT_g, 0, 1, u)
            await_evacuated(pe, "g_oT2", "g_oT3")
            last_out_part("g", 6, oT_g, 0)

            def router(l):
                b = fill(f"m{l}_log")
                pe.wait_ge(sem("wr_in"), 8 * 16)

                def logits(t, chunks):
                    for c in chunks:
                        if c in (0, 4):
                            await_evacuated(pe, f"m{l}_xT{t}{c // 4}")
                        mm = pe.matmul(b[:, t * P:t * P + GROUPS + NE], xT[:, c, t * P:(t + 1) * P], wr[:, l, c, :],
                                       start=(c == 0), stop=(c == DC - 1))
                    return mm

                fill(f"m{l}_pos")
                logits(0, range(0, 4))
                turn_h("gf"[l], l, 1)
                logits(0, range(4, DC))
                full(logits(1, range(DC)), f"m{l}_log")
                b = fill(f"m{l}_pos")
                stay_awake(b, WAKE["router"])
                pe.wait_ge(sem("member"), l + 1)
                both = member[:].rearrange("p t e -> p (t e)")
                ones = upto[:, P:2 * P]
                pe.matmul(b[:, 0:2 * NE], upto[:, 0:P], both, start=True, stop=False)
                pe.matmul(b[:, NE:2 * NE], ones, member[:, 0, :], start=False, stop=True)
                full(pe.matmul(b[:, 2 * NE:4 * NE], ones, both, start=True, stop=True), f"m{l}_pos")

            def rounds(ph):
                def body(it):
                    for u in range(UNROLL):
                        r = UNROLL * it + u + ph.before + START
                        pe.wait_ge(ph.sel_ready, r + 1)
                        pe.wait_ge(ph.h_added, at_round(r, QUARTERS, 0))
                        for c in range(DC):
                            b = PS[:, 4 + c // 4, (c % 4) * P:(c % 4 + 1) * P]
                            for t in range(TC):
                                mm = pe.matmul(b, xn[:, t, c, :], sel[:, t, :], start=(t == 0), stop=(t == TC - 1))
                            if c % 4 == 3:
                                mm.then_inc(ph.gathered, 1)
                        pe.wait_ge(ph.wsel_ready, r + 1)
                        for t in range(TC):
                            mm = pe.transpose(PS[:, 6, t * P:(t + 1) * P], wsel[:, t, :], ident[:])
                        mm.then_inc(ph.wsel_turned, 1)
                        pe.wait_ge(ph.hid_ready, r)
                        for k in range(8):
                            if k % 4 == 0:
                                pe.wait_ge(ph.xg_ready, at_round(r, 2, k // 4 + 1))
                            home, arrived, value = ph.home(it, u * PIECES + k)
                            pe.wait_ge(arrived, value)
                            w = home.rearrange("p (j c f) -> p j c f", j=JB, c=2)
                            for c2 in range(2):
                                c = 2 * (k // 2) + c2
                                for j in range(JB):
                                    js = slice(SLOTS * j, SLOTS * (j + 1))
                                    mm = pe.matmul(PS[js, k % 2, :], xgT[:, c, js], w[:, j, c2, :],
                                                   start=(c == 0), stop=(c == DC - 1))
                            mm.then_inc(ph.pieces_used, 1)
                        pe.wait_ge(ph.hid_ready, r + 1)
                        pe.wait_ge(ph.wselT_ready, r + 1)
                        for f in range(FC):
                            mm = pe.transpose(PS[:, 6, f * P:(f + 1) * P], hid[:, f * P:(f + 1) * P], ident[:])
                        mm.then_inc(ph.hid_turned, 1)
                        pe.wait_ge(ph.hidT_ready, r + 1)
                        pe.wait_ge(ph.y_ready, at_round(r, 2, 0))
                        for f in range(FC):
                            home, arrived, value = ph.home(it, u * PIECES + 8 + f)
                            if f == FC - 1:
                                stay_awake(PS[:, 0, :], WAKE["down"])
                            pe.wait_ge(arrived, value)
                            w = home.rearrange("p (j d) -> p j d", j=JB)
                            for half in range(2):
                                for j in range(JB):
                                    js = slice(SLOTS * j, SLOTS * (j + 1))
                                    mm = pe.matmul(PS[js, 2 + half, :], hidT[:, f, js],
                                                   w[:, j, half * HALF:(half + 1) * HALF],
                                                   start=(f == 0), stop=(f == FC - 1))
                                if f == FC - 1 and half == 0:
                                    mm.then_inc(ph.y_left_full, 1)
                            mm.then_inc(ph.pieces_used, 1)
                        for half in range(2):
                            pe.wait_ge(ph.y_ready, at_round(r, 2, half + 1))
                            for t in range(TC):
                                pe.matmul(PS[:, 4 + 2 * t + half, :], wselT[:, t * P:(t + 1) * P],
                                          y_e[:, half * HALF:(half + 1) * HALF], start=True,
                                          stop=True).then_inc(ph.combined, 1)

                ph.iterations(pe, body)

            def moe(l):
                router(l)
                await_evacuated(pe, f"m{l}_pos")
                rounds(main[l])
                pe.wait_ge(sem("tables_ready"), l + 1)
                need = pe.value_load(flag[0:1, 0:1], min_val=0, max_val=EXTRA)
                with pe.If(need > 0):
                    rounds(over[l])
                    pe.wait_ge(over[l].h_added, EXTRA // JB * QUARTERS + START)
                pe.wait_ge(main[l].h_added, (l + 1) * ROUNDS * QUARTERS + START)

            moe(0)
            stay_awake(bank("f_f"), WAKE["boundary"])
            for t in range(TC):
                turn_x("f", t)
            b = fill("f_f")
            pe.wait_ge(sem("kvT_left"), TC)
            pe.wait_ge(sem("kvT_right"), TC)
            pe.wait_ge(sem("wf_in"), 32)
            for c in range(DC):
                mm = pe.matmul(b[0:FH, 0:T], wf[:, c, :], kvT[:, c, :], start=(c == 0), stop=(c == DC - 1))
            full(mm, "f_f")
            down_cols(["f_k0", "f_k1"], FOX_BASE, kvT)
            down_cols(["f_k2", "f_k3"], FOX_BASE + 1, kvT)
            b = fill("f_lf")
            pe.wait_ge(sem("lfT_ready"), 1)
            for t in range(TC):
                mm = pe.transpose(b[:, t * FH:(t + 1) * FH], lfT[:, t * P:(t + 1) * P], ident[0:FH, 0:FH])
            full(mm, "f_lf")
            await_evacuated(pe, "f_lf")
            b = fill("f_c")
            pe.matmul(b[0:FH, 0:T], lf_n[:, 0, :], upto[:], start=True, stop=False)
            full(pe.matmul(b[0:FH, P:T], lf_n[:, 1, :], upto[:, 0:P], start=False, stop=True), "f_c")
            along_cols(["f_v00", "f_v01"], FOX_BASE + 2, kvT)
            along_cols(["f_v10", "f_v11"], FOX_BASE + 3, kvT)
            await_evacuated(pe, *[f"f_{x}" for x in X_JOBS])
            down_cols(["f_q0", "f_q1"], FOX_BASE + 4, xT)
            down_cols(["f_q2", "f_q3"], FOX_BASE + 5, xT)
            down_cols(["f_g0", "f_g1"], FOX_BASE + 6, xT)
            await_evacuated(pe, *[f"f_{n}{i}" for n in "kq" for i in range(4)])
            await_evacuated(pe, *[f"f_v{i}{t}" for i in range(2) for t in range(TC)])
            pe.wait_ge(sem("c_row"), 16 * FH)
            gated_f = [gT_f[:, c, :] for c in range(DC)]
            for i in range(FH + 4):
                if i == EARLY:
                    down_cols(["f_g2", "f_g3"], FOX_BASE + 7, xT)
                if i < FH:
                    b = fill(f"f_s{i}")
                    pe.matmul(b[:, 0:P], q_f[:, i, 0:P], k_f[:, i, 0:P], start=True, stop=True)
                    full(pe.matmul(b[:, P:3 * P], q_f[:, i, P:T], k_f[:, i, :], start=True, stop=True), f"f_s{i}")
                if 3 <= i <= FH + 2:
                    n = i - 3
                    b = fill(f"f_pT{n}")
                    pe.wait_ge(sem("p_ready"), n + 1)
                    for a in range(3):
                        mm = pe.transpose(b[:, a * P:(a + 1) * P], p_f[:, n % PBUF, a * P:(a + 1) * P], ident[:])
                    full(mm, f"f_pT{n}")
                if i >= 5 and i % 2 == 1:
                    m = (i - 5) // 2
                    o_bank = fill(f"f_o{m}")
                    await_evacuated(pe, f"f_pT{2 * m}", f"f_pT{2 * m + 1}")
                    for t, q0 in ((0, 0), (1, P)):
                        for o in range(2):
                            n = 2 * m + o
                            mm = pe.matmul(o_bank[FD * o:FD * (o + 1), q0:T], v_f[:, t, FD * n:FD * (n + 1)],
                                           pT_f[:, n % PBUF, 2 * q0:2 * P + q0], start=(t == 0), stop=(t == 1))
                    full(mm, f"f_o{m}")
                if i in OUT_BETWEEN:
                    await_evacuated(pe, *[f"f_o{m}" for m in range(4)])
                    out_part("f", FOX_BASE + 8, gated_f, 0, *OUT_BETWEEN[i])
            await_evacuated(pe, *[f"f_o{m}" for m in range(4, FH // 2)])
            last_out_part("f", FOX_BASE + 8, gated_f, 1)
            moe(1)

        @block.scalar
        def _(act):
            a = nc.scalar
            for ph in (main[0], *over):
                for counter in (ph.wselT_ready, ph.silu_done, ph.hidT_ready, ph.y_ready):
                    act.sem_inc(counter, START)
            step = Steps(act, sem("act_steps"))

            def root(tag, i, cols):
                act.wait_ge(sem("mean_ready"), NORMS[tag] + i + 1)
                a.activation(stat[:, 2, cols], stat[:, 1, cols], ACT.Sqrt).then_inc(sem("rstd_ready"), 1)

            def roots(tag):
                for t in range(TC):
                    root(tag, t, slice(t, t + 1))

            def take_turned(tag, t, dst, gain):
                await_full(act, f"{tag}_xT{t}1")
                for c in range(4, DC):
                    ins = a.activation(dst[:, c, t * P:(t + 1) * P], bank(f"{tag}_xT{t}1")[:, (c - 4) * P:(c - 3) * P],
                                       ACT.Copy, scale=gains[:, gain, c:c + 1])
                return ins

            def square_sum(dst, t):
                a.activation(dst, h[:, t, :], ACT.Square, accum_out=stat[:, 0, t:t + 1]).then_inc(sem("squared"), 1)

            def root_table():
                a.activation(stat[:, 2, 7:8], stat[:, 1, 7:8], ACT.Sqrt)

            def softplus_minus(dst, src):
                step(a.activation(dst, src, ACT.Abs))
                step(a.activation(dst, dst, ACT.Exp, scale=-1.0))
                return a.activation(dst, dst, ACT.Ln, bias=1.0)

            roots("g")
            act.wait_ge(sem("gains_in"), 16)
            for t in range(TC):
                freed(take_turned("g", t, xT, 0), f"g_xT{t}1")
            await_full(act, "g_a")
            act.wait_ge(sem("aT_ones"), 1)
            freed(a.copy(aT[0:RANK, :], bank("g_a")[0:RANK, 0:T]), "g_a")
            for dst, n in ((qT, "q"), (kT, "k")):
                for i in range(2):
                    await_full(act, f"g_{n}{i}")
                    freed(a.copy(dst[:, 2 * i:2 * i + 2, :], bank(f"g_{n}{i}").rearrange("p (u t) -> p u t", u=2)),
                          f"g_{n}{i}")
            for t in range(TC):
                await_full(act, f"g_z{t}")
                softplus_minus(la[:, t, :], bank(f"g_z{t}")).then_inc(sem("z_soft"), 1)
            for i in range(2):
                await_full(act, f"g_cum{i}")
                freed(a.mul(cumT[:, 2 * i:2 * i + 2, :], bank(f"g_cum{i}").rearrange("p (u t) -> p u t", u=2), 1 / TAU),
                      f"g_cum{i}")
            act.wait_ge(sem("qs_rel"), 1)
            a.activation(qs, qs, ACT.Exp).then_inc(sem("qs_exp"), 1)
            for b in range(NRB):
                ref = RB * b + REF
                for hh in range(GH):
                    a.activation(kb[b][:, hh, :], cumT[:, hh, 0:RB * (b + 1)], ACT.Exp, scale=-1.0,
                                 bias=cumT[:, hh, ref:ref + 1]).then_inc(sem("kb_exp"), 1)

            def gate(i):
                for t in range(TC):
                    await_full(act, f"g_r{i}{t}")
                    freed(a.activation(gate_r[:, t, i * HALF:(i + 1) * HALF], bank(f"g_r{i}{t}"), ACT.Silu), f"g_r{i}{t}")

            gate(0)
            for hh in range(GH):
                await_full(act, f"g_sT{hh}")
                freed(a.copy(sT[:, hh, :], bank(f"g_sT{hh}")[:, 0:3 * P]), f"g_sT{hh}")
            squares = carve(0, GH * TC, GDV)
            for hh in range(GH):
                await_full(act, f"g_o{hh}")
                for t in range(TC):
                    k = TC * hh + t
                    a.activation(squares[:, k, :], bank(f"g_o{hh}")[:, t * GDV:(t + 1) * GDV], ACT.Square,
                                 accum_out=stat[:, 0, k:k + 1]).then_inc(sem("o_squares"), 1)
                if hh % 2 == 1:
                    for i in (hh - 1, hh):
                        root("go", i, slice(TC * i, TC * (i + 1)))
            gate(1)

            def router(l):
                act.wait_ge(sem("gains2_in"), 64)
                for t in range(TC):
                    await_evacuated(act, f"{'gf'[l]}_y{t}0", f"{'gf'[l]}_y{t}1")
                    square_sum(y_out[:, t, :], t)
                    if t == 0:
                        freed(take_turned(f"m{l}", t, xT, (1, 4)[l]), f"m{l}_xT01")
                    root(f"m{l}", t, slice(t, t + 1))
                act.wait_ge(sem("coarse_rel"), l + 1)
                a.activation(rel[:], rel[:], ACT.Exp).then_inc(sem("coarse_exp"), 1)
                act.wait_ge(sem("second_rel"), l + 1)
                a.activation(best_f[:, 3, :], best_f[:, 3, :], ACT.Exp).then_inc(sem("second_exp"), 1)

            def rounds(ph):
                span = UNROLL * PIECES
                with act.Fori(0, ph.n_iter) as it:
                    for u in range(UNROLL):
                        r = UNROLL * it + u + ph.before + START
                        act.wait_ge(ph.wsel_turned, r + 1)
                        act.wait_ge(ph.combined, at_round(r, QUARTERS, 0))
                        a.copy(wselT, PS[:, 6, 0:T]).then_inc(ph.wselT_ready, 1)
                        act.wait_ge(ph.pieces_used, ph.used(span * it + u * PIECES + 7))
                        act.wait_ge(ph.hid_ready, r)
                        a.activation(silu_g, PS[:, 0, :], ACT.Silu).then_inc(ph.silu_done, 1)
                        act.wait_ge(ph.hid_turned, r + 1)
                        a.copy(hidT.rearrange("p a b -> p (a b)"), PS[:, 6, :]).then_inc(ph.hidT_ready, 1)
                        act.wait_ge(ph.y_left_full, r + 1)
                        a.copy(y_e[:, 0:HALF], PS[:, 2, :]).then_inc(ph.y_ready, 1)
                        act.wait_ge(ph.pieces_used, ph.used(span * it + (u + 1) * PIECES))
                        a.copy(y_e[:, HALF:], PS[:, 3, :]).then_inc(ph.y_ready, 1)

            def moe(l):
                router(l)
                rounds(main[l])
                act.wait_ge(sem("tables_ready"), l + 1)
                need = act.value_load(flag[0:1, 0:1], min_val=0, max_val=EXTRA)
                with act.If(need > 0):
                    rounds(over[l])
                    act.wait_ge(over[l].y_ready, EXTRA // JB * 2 + START)
                    act.wait_ge(over[l].h_added, EXTRA // JB * QUARTERS + START)
                act.wait_ge(main[l].y_ready, (l + 1) * ROUNDS * 2 + START)
                root_table()
                act.wait_ge(main[l].h_added, (l + 1) * ROUNDS * QUARTERS + START)

            moe(0)
            square_sum(y_out[:, 1, :], 1)
            roots("f")
            for t in range(TC):
                take_turned("f", t, kvT, 2).then_inc(sem("kvT_right"), 1)
            for t in range(TC):
                freed(take_turned("f", t, xT, 3), f"f_xT{t}1")
            await_evacuated(act, "f_f")
            softplus_minus(c_neg[:], lfT).then_inc(sem("f_soft"), 1)
            act.wait_ge(sem("qk_halves"), 1)

            def split_heads(dst, n, i):
                src = bank(f"f_{n}{i}").rearrange("p (u t) -> p u t", u=2)
                d4 = dst[0:FD, 4 * i:4 * i + 4, :].rearrange("p (u o) t -> p u o t", o=2)
                return [(d4[:, :, o, :], src[FD * o:FD * (o + 1)]) for o in range(2)]

            for i in range(4):
                await_full(act, f"f_k{i}")
                (d0, s0), (d1, s1) = split_heads(k_f, "k", i)
                a.copy(d0, s0)
                freed(a.copy(d1, s1), f"f_k{i}")
            await_full(act, "f_c")
            freed(a.mul(c_neg[:], bank("f_c")[0:FH, 0:T], -float(FD) ** 0.5), "f_c")
            await_evacuated(act, "f_c")
            for hh in range(FH):
                act.dma_start(k_f[FD:FD + 1, hh, :], c_neg[hh:hh + 1, :]).then_inc(sem("c_row"), 16)

            def gate_f(i):
                await_full(act, f"f_g{i}")
                freed(a.activation(gT_f[:, 2 * i:2 * i + 2, :], bank(f"f_g{i}").rearrange("p (u t) -> p u t", u=2),
                                   ACT.Sigmoid), f"f_g{i}")

            gate_f(0)
            gate_f(1)
            for i in range(FH + 2):
                if i < FH:
                    act.wait_ge(sem("nm_ready"), i + 1)
                    for t, (c0, c1) in enumerate(((0, P), (P, 3 * P))):
                        ins = a.activation(p_f[:, i % PBUF, c0:c1], p_f[:, i % PBUF, c0:c1], ACT.Exp,
                                           bias=nm_f[:, i, t:t + 1], accum_out=sum_f[:, i, t:t + 1])
                    ins.then_inc(sem("exp_done"), 1)
                if i == EARLY - 1:
                    gate_f(2)
                    gate_f(3)
                if i >= 2:
                    n = i - 2
                    await_full(act, f"f_pT{n}")
                    if n >= PBUF:
                        await_full(act, f"f_o{(n - PBUF) // 2}")
                    freed(a.copy(pT_f[:, n % PBUF, :], bank(f"f_pT{n}")[:, 0:3 * P]), f"f_pT{n}")
            moe(1)
            for t in range(TC):
                square_sum(xTf[:, t * D:(t + 1) * D], t)
            roots("last")
            act.wait_ge(sem("last_inverse"), 1)
            a.mul(y_out[:, 1, :], y_out[:, 1, :], stat[:, 2, 1:2]).then_inc(out_ready[1], 1)

        @block.vector
        def _(dve):
            v = nc.vector
            for ph in (main[0], *over):
                for counter in (ph.sel_ready, ph.wsel_ready, ph.xg_ready, ph.hid_ready, ph.h_added):
                    dve.sem_inc(counter, START)
            step = Steps(dve, sem("dve_steps"))

            def mean(t):
                v.tensor_scalar(stat[:, 1, t:t + 1], stat[:, 0, t:t + 1], 1.0 / D, EPS, ALU.mult,
                                ALU.add).then_inc(sem("mean_ready"), 1)

            def mean_square(t):
                ins = v.tensor_tensor_reduce(out=xn[:, t, :, :].rearrange("p a b -> p (a b)"), in0=h[:, t, :],
                                             in1=h[:, t, :], scale=1.0, scalar=0.0, op0=ALU.mult, op1=ALU.add,
                                             accum_out=stat[:, 0, t:t + 1])
                step(ins)
                mean(t)

            def inverse(tag, t):
                dve.wait_ge(sem("rstd_ready"), NORMS[tag] + t + 1)
                step(v.reciprocal(stat[:, 2, t:t + 1], stat[:, 2, t:t + 1]))

            def scale(tag, t):
                inverse(tag, t)
                v.tensor_scalar(xn[:, t, :, :], h8[:, t, :, :], stat[:, 2, t:t + 1], None,
                                ALU.mult).then_inc(sem("xn_ready"), 1)

            def normalise(tag, t):
                mean_square(t)
                scale(tag, t)

            def take_half(tag, t, u, dst, gain):
                await_full(dve, f"{tag}_xT{t}{u}")
                cs = slice(4 * u, 4 * u + 4)
                return v.tensor_tensor(dst[:, cs, t * P:(t + 1) * P],
                                       bank(f"{tag}_xT{t}{u}").rearrange("p (c t) -> p c t", c=4),
                                       gains[:, gain, cs].unsqueeze(2).to_broadcast([P, 4, P]), ALU.mult)

            def take_turned_o(i):
                await_full(dve, f"g_oT{i}")
                for u in range(2):
                    ins = v.tensor_scalar(oT_g[2 * i + u], bank(f"g_oT{i}")[:, u * T:(u + 1) * T],
                                          gains[:, 5, 2 * i + u:2 * i + u + 1], None, ALU.mult)
                freed(ins, f"g_oT{i}")

            def finish_mixer(tag, l):
                def add(t, u):
                    await_full(dve, f"{tag}_y{t}{u}")
                    hs = h[:, t, u * HALF:(u + 1) * HALF]
                    freed(v.tensor_tensor(hs, hs, bank(f"{tag}_y{t}{u}"), ALU.add), f"{tag}_y{t}{u}")

                before = (0, TC + 1)[l]
                dve.wait_ge(sem("gains2_in"), 64)
                add(0, 0)
                add(0, 1)
                dve.wait_ge(sem("squared"), before + 1)
                mean(0)
                add(1, 0)
                freed(take_half(f"m{l}", 0, 0, xT, (1, 4)[l]), f"m{l}_xT00")
                scale(f"m{l}", 0)
                add(1, 1)
                for u in range(2):
                    freed(take_half(f"m{l}", 1, u, xT, (1, 4)[l]), f"m{l}_xT1{u}")
                dve.wait_ge(sem("squared"), before + 2)
                mean(1)
                scale(f"m{l}", 1)

            for t in range(TC):
                dve.wait_ge(sem(f"x_in{t}"), 16)
                normalise("g", t)
            dve.wait_ge(sem("gains_in"), 16)
            for t in range(TC):
                freed(take_half("g", t, 0, xT, 0), f"g_xT{t}0")
            await_full(dve, "g_gain")
            freed(v.tensor_copy(gains[:, 5, :], bank("g_gain")[:, 0:DC]), "g_gain")
            for t in range(TC):
                dve.wait_ge(sem("z_soft"), t + 1)
                freed(v.scalar_tensor_tensor(out=la[:, t, :], in0=bank(f"g_z{t}"), scalar=0.0, in1=la[:, t, :],
                                             op0=ALU.min, op1=ALU.subtract), f"g_z{t}")

            def take_v(i):
                for t in range(TC):
                    await_full(dve, f"g_v{i}{t}")
                    freed(v.tensor_copy(v_g[:, t, i * HALF:(i + 1) * HALF], bank(f"g_v{i}{t}")), f"g_v{i}{t}")

            take_v(0)
            v.memset(sS, 0.0).then_inc(sem("sS_zero"), 1)
            await_evacuated(dve, "g_cum0", "g_cum1", "g_q0", "g_q1", "g_k0", "g_k1")
            c4 = cumT.rearrange("p a (b s) -> p a b s", s=RB)
            q4 = qs.rearrange("p a (b s) -> p a b s", s=RB)
            for hh in range(GH):
                ref = c4[:, hh, :, REF:REF + 1].to_broadcast([P, NRB, RB])
                ins = v.tensor_tensor(q4[:, hh], c4[:, hh], ref, ALU.subtract)
            ins.then_inc(sem("qs_rel"), 1)
            dve.wait_ge(sem("qs_exp"), 1)
            v.scalar_tensor_tensor(out=qs, in0=qs, scalar=float(GDK) ** -0.5, in1=qT, op0=ALU.mult,
                                   op1=ALU.mult).then_inc(sem("qs_ready"), 1)
            for b in range(NRB):
                dve.wait_ge(sem("kb_exp"), GH * (b + 1))
                v.tensor_tensor(kb[b], kb[b], kT[:, :, 0:RB * (b + 1)], ALU.mult).then_inc(sem("kb_ready"), 1)
            take_v(1)
            dve.wait_ge(sem("sS_zero"), 1)
            await_full(dve, *[f"g_s{hh}" for hh in range(GH)])
            dve.wait_ge(sem("consts_ready"), 1)
            b0 = JOBS["g_s0"][0]
            for b in range(NRB):
                q0, n, c0 = RB * (b % 4), RB * (b % 4 + 1), 0 if b < 4 else 2 * P
                v.tensor_tensor(sS[q0:q0 + RB, :, c0:c0 + n], PS[q0:q0 + RB, b0:b0 + GH, c0:c0 + n],
                                lower[q0:q0 + RB, 0:n].unsqueeze(1).to_broadcast([RB, GH, n]), ALU.mult)
            for hh in range(GH):
                freed(v.tensor_copy(sS[:, hh, P:2 * P], bank(f"g_s{hh}")[:, P:2 * P]), f"g_s{hh}")

            def head_mean(hh):
                dve.wait_ge(sem("o_squares"), TC * (hh + 1))
                ks = slice(TC * hh, TC * (hh + 1))
                v.tensor_scalar(stat[:, 1, ks], stat[:, 0, ks], 1.0 / GDV, EPS, ALU.mult,
                                ALU.add).then_inc(sem("mean_ready"), 1)

            def head_inverse(hh):
                dve.wait_ge(sem("rstd_ready"), NORMS["go"] + hh + 1)
                ks = slice(TC * hh, TC * (hh + 1))
                step(v.reciprocal(stat[:, 2, ks], stat[:, 2, ks]))

            def gated(hh):
                hc = slice(hh * GDV, (hh + 1) * GDV)
                for t in range(TC):
                    await_evacuated(dve, f"g_r{hh // 2}{t}")
                    k = TC * hh + t
                    ins = v.scalar_tensor_tensor(out=o_g[:, t, hc], in0=bank(f"g_o{hh}")[:, t * GDV:(t + 1) * GDV],
                                                 scalar=stat[:, 2, k:k + 1], in1=gate_r[:, t, hc], op0=ALU.mult,
                                                 op1=ALU.mult)
                freed(ins, f"g_o{hh}")

            for pair in ((0, 1), (2, 3)):
                for hh in pair:
                    head_mean(hh)
                for hh in pair:
                    head_inverse(hh)
                if pair[0] == 0:
                    gated(0)
                    gated(1)
            for i in (0, 1):
                take_turned_o(i)
            gated(2)
            gated(3)
            for i in (2, 3):
                take_turned_o(i)
            finish_mixer("g", 0)

            def row_max(dst, src):
                return v.tensor_reduce(dst.unsqueeze(2), src, AX, ALU.max)

            def is_top(dst, src, top):
                return v.tensor_tensor(dst, src, top.unsqueeze(2).to_broadcast(list(src.shape)), ALU.is_equal)

            def positions(dst):
                _, rows, n = dst.shape
                return v.scalar_tensor_tensor(out=dst, in0=iota[:, 0:n].unsqueeze(1).to_broadcast([P, rows, n]),
                                              scalar=100.0, in1=dst, op0=ALU.subtract, op1=ALU.mult)

            def least(dst, src):
                return v.tensor_reduce(dst.unsqueeze(2), src, AX, ALU.min)

            def one_hot(dst, where):
                _, rows, n = dst.shape
                return v.scalar_tensor_tensor(out=dst, in0=iota[:, 0:n].unsqueeze(1).to_broadcast([P, rows, n]),
                                              scalar=100.0, in1=where.unsqueeze(2).to_broadcast([P, rows, n]),
                                              op0=ALU.subtract, op1=ALU.is_equal)

            def router(l):
                await_full(dve, f"m{l}_log")
                dve.wait_ge(sem("wr_in"), 8 * 16)
                logs = bank(f"m{l}_log")[:, 0:TC * P].rearrange("p (t n) -> p t n", t=TC)
                flat = lf[:].rearrange("p (t g) j -> p t (g j)", t=TC)
                group_of_row = hot_g[:].rearrange("p t g -> p (t g)")
                top_g, pos_g = (best_g[:, i, :] for i in range(2))
                m1, m2, pos_f, second = (best_f[:, i, :] for i in range(4))
                for t in range(TC):
                    ins = v.scalar_tensor_tensor(out=flat[:, t, :], in0=logs[:, t, GROUPS:GROUPS + NE],
                                                 scalar=stat[:, 2, t:t + 1], in1=br[:, l, GROUPS:], op0=ALU.mult,
                                                 op1=ALU.add)
                fine = step.mark(ins)
                for t in range(TC):
                    ins = v.scalar_tensor_tensor(out=lc[:, t, :], in0=logs[:, t, 0:GROUPS],
                                                 scalar=stat[:, 2, t:t + 1], in1=br[:, l, 0:GROUPS], op0=ALU.mult,
                                                 op1=ALU.add)
                freed(ins, f"m{l}_log")
                step.reach(fine)
                fine = step.mark(row_max(m1, lf[:]))
                await_evacuated(dve, f"m{l}_log")
                group = step.mark(row_max(top_g, lc[:]))
                step.reach(fine)
                fine = step.mark(is_top(hot_a[:], lf[:], m1))
                step.reach(group)
                v.tensor_tensor(rel[:], lc[:], top_g.unsqueeze(2).to_broadcast([P, TC, GROUPS]),
                                ALU.subtract).then_inc(sem("coarse_rel"), 1)
                group = step.mark(is_top(hot_g[:], lc[:], top_g))
                step.reach(fine)
                fine = step.mark(positions(hot_a[:]))
                step.reach(group)
                group = step.mark(positions(hot_g[:]))
                step.reach(fine)
                fine = step.mark(least(pos_f, hot_a[:]))
                step.reach(group)
                group = step.mark(least(pos_g, hot_g[:]))
                step.reach(fine)
                fine = step.mark(one_hot(hot_a[:], pos_f))
                step.reach(group)
                group = step.mark(one_hot(hot_g[:], pos_g))
                step.reach(fine)
                step(v.scalar_tensor_tensor(out=rest[:], in0=hot_a[:], scalar=NEG, in1=lf[:], op0=ALU.mult,
                                            op1=ALU.add))
                step(row_max(m2, rest[:]))
                fine = step.mark(is_top(hot_b[:], rest[:], m2))
                v.tensor_tensor(second, m2, m1, ALU.subtract).then_inc(sem("second_rel"), 1)
                step.reach(fine)
                step(positions(hot_b[:]))
                step(least(pos_f, hot_b[:]))
                step(one_hot(hot_b[:], pos_f))
                step(v.tensor_tensor(rest[:], hot_a[:], hot_b[:], ALU.add))
                hot_rows = group_of_row.unsqueeze(2).to_broadcast([P, TC * GROUPS, PER])
                v.tensor_tensor(member[:].rearrange("p t (g j) -> p (t g) j", g=GROUPS), rest[:], hot_rows,
                                ALU.mult).then_inc(sem("member"), 1)
                await_full(dve, f"m{l}_pos")
                b = bank(f"m{l}_pos")
                placed = step.mark(v.tensor_tensor(place[:, :, 0:NE], b[:, 0:2 * NE].rearrange("p (t e) -> p t e", t=TC),
                                                   member[:], ALU.mult))
                freed(v.tensor_reduce(counts[:].unsqueeze(2), b[:, 2 * NE:4 * NE].rearrange("p (t e) -> p e t", t=TC),
                                      AX, ALU.add), f"m{l}_pos")
                step.reach(placed)

            def gates_of(l):
                group_of_row = hot_g[:].rearrange("p t g -> p (t g)")
                total = best_g[:, 2, :]
                second, g1, g2 = (best_f[:, i, :] for i in (3, 4, 5))
                dve.wait_ge(sem("coarse_exp"), l + 1)
                step(v.tensor_reduce(total.unsqueeze(2), rel[:], AX, ALU.add))
                dve.wait_ge(sem("second_exp"), l + 1)
                step(v.tensor_scalar(g2, second, 1.0, None, ALU.add))
                step(v.tensor_tensor(g2.rearrange("p (t g) -> p t g", t=TC), g2.rearrange("p (t g) -> p t g", t=TC),
                                     total.unsqueeze(2).to_broadcast([P, TC, GROUPS]), ALU.mult))
                step(v.reciprocal(g1, g2))
                step(v.tensor_tensor(g1, g1, group_of_row, ALU.mult))
                step(v.tensor_tensor(g2, g1, second, ALU.mult))
                v.tensor_tensor(rest[:], hot_b[:], g2.unsqueeze(2).to_broadcast([P, TC * GROUPS, PER]), ALU.mult)
                step(v.tensor_tensor(hot_a[:], hot_a[:], g1.unsqueeze(2).to_broadcast([P, TC * GROUPS, PER]),
                                     ALU.mult))
                step(v.tensor_tensor(gates[:, :, 0:NE], hot_a[:].rearrange("p (t g) j -> p t (g j)", t=TC),
                                     rest[:].rearrange("p (t g) j -> p t (g j)", t=TC), ALU.add))

            def rounds(ph, gain):
                span = UNROLL * PIECES
                sel4 = sel.rearrange("p t (j s) -> p t j s", j=JB)
                wsel4 = wsel.rearrange("p t (j s) -> p t j s", j=JB)
                s_bc = slot[:].unsqueeze(1).to_broadcast([P, JB, SLOTS])

                def body(it):
                    for u in range(UNROLL):
                        r = UNROLL * it + u + ph.before + START
                        cols = bass.ds(ph.col0 + JB * (UNROLL * it + u), JB)
                        dve.wait_ge(ph.wsel_turned, r)
                        for t in range(TC):
                            ins = v.tensor_tensor(sel4[:, t], s_bc,
                                                  place[:, t, cols].unsqueeze(2).to_broadcast([P, JB, SLOTS]),
                                                  ALU.is_equal)
                        ins.then_inc(ph.sel_ready, 1)
                        if isinstance(it, int) and u == 0:
                            gates_of(ph.layer)
                        dve.wait_ge(ph.sel_ready, r + 1)
                        for t in range(TC):
                            ins = v.tensor_tensor(wsel4[:, t], sel4[:, t],
                                                  gates[:, t, cols].unsqueeze(2).to_broadcast([P, JB, SLOTS]),
                                                  ALU.mult)
                        ins.then_inc(ph.wsel_ready, 1)
                        dve.wait_ge(ph.pieces_used, ph.used(span * it + max(u * PIECES - 4, 0)))
                        for a in range(2):
                            cs = slice(4 * a, 4 * a + 4)
                            dve.wait_ge(ph.gathered, at_round(r, 2, a + 1))
                            v.tensor_tensor(xgT[:, cs, :], PS[:, 4 + a, :].rearrange("p (c s) -> p c s", c=4),
                                            gains[:, gain, cs].unsqueeze(2).to_broadcast([P, 4, P]),
                                            ALU.mult).then_inc(ph.xg_ready, 1)
                        dve.wait_ge(ph.silu_done, r + 1)
                        dve.wait_ge(ph.hid_turned, r)
                        dve.wait_ge(ph.pieces_used, ph.used(span * it + u * PIECES + 8))
                        v.tensor_tensor(hid, silu_g, PS[:, 1, :], ALU.mult).then_inc(ph.hid_ready, 1)
                        for q in range(QUARTERS):
                            half, t = q // TC, q % TC
                            hs = h[:, t, half * HALF:(half + 1) * HALF]
                            dve.wait_ge(ph.combined, at_round(r, QUARTERS, q + 1))
                            v.tensor_tensor(hs, hs, PS[:, 4 + 2 * t + half, :], ALU.add).then_inc(ph.h_added, 1)

                ph.iterations(dve, body)

            def moe(l):
                router(l)
                rounds(main[l], (1, 4)[l])
                dve.wait_ge(sem("tables_ready"), l + 1)
                need = dve.value_load(flag[0:1, 0:1], min_val=0, max_val=EXTRA)
                with dve.If(need > 0):
                    rounds(over[l], (1, 4)[l])
                    dve.wait_ge(over[l].h_added, EXTRA // JB * QUARTERS + START)
                dve.wait_ge(main[l].h_added, (l + 1) * ROUNDS * QUARTERS + START)

            moe(0)
            mean_square(0)
            dve.wait_ge(sem("squared"), TC + 1)
            mean(1)
            for t in range(TC):
                scale("f", t)
            for t in range(TC):
                take_half("f", t, 0, kvT, 2).then_inc(sem("kvT_left"), 1)
            for t in range(TC):
                freed(take_half("f", t, 0, xT, 3), f"f_xT{t}0")
            await_full(dve, "f_f")
            dve.wait_ge(sem("wf_in"), 32)
            freed(v.tensor_scalar(lfT, bank("f_f")[0:FH, 0:T], bf[:, 0:1], None, ALU.add), "f_f")
            await_evacuated(dve, "f_f")
            dve.wait_ge(sem("f_soft"), 1)
            v.scalar_tensor_tensor(out=lfT, in0=lfT, scalar=0.0, in1=c_neg[:], op0=ALU.min,
                                   op1=ALU.subtract).then_inc(sem("lfT_ready"), 1)
            await_full(dve, "f_lf")
            freed(v.tensor_copy(lf_n[:], bank("f_lf")[:, 0:TC * FH].rearrange("p (t n) -> p t n", t=TC)), "f_lf")
            for i in range(2):
                for t in range(TC):
                    await_full(dve, f"f_v{i}{t}")
                    freed(v.tensor_copy(v_f[:, t, i * HALF:(i + 1) * HALF], bank(f"f_v{i}{t}")), f"f_v{i}{t}")
            dve.wait_ge(sem("qk_halves"), 1)
            for i in range(4):
                await_full(dve, f"f_q{i}")
                src = bank(f"f_q{i}").rearrange("p (u t) -> p u t", u=2)
                dst = q_f[0:FD, 4 * i:4 * i + 4, :].rearrange("p (u o) t -> p u o t", o=2)
                v.tensor_copy(dst[:, :, 0, :], src[0:FD])
                freed(v.tensor_copy(dst[:, :, 1, :], src[FD:P]), f"f_q{i}")
            for i in range(FH + 5):
                if i < FH:
                    await_full(dve, f"f_s{i}")
                    if i >= PBUF:
                        await_full(dve, f"f_pT{i - PBUF}")
                    b = bank(f"f_s{i}")
                    for t, (c0, c1) in enumerate(((0, P), (P, 3 * P))):
                        ins = v.tensor_tensor_reduce(out=p_f[:, i % PBUF, c0:c1], in0=b[:, c0:c1], in1=causal[:, c0:c1],
                                                     scale=float(FD) ** -0.5, scalar=NEG, op0=ALU.add, op1=ALU.max,
                                                     accum_out=mx_f[:, i, t:t + 1])
                    freed(ins, f"f_s{i}")
                if 1 <= i <= FH:
                    n = i - 1
                    dve.wait_ge(sem("exp_done"), n + 1)
                    inverted = step.mark(v.reciprocal(inv_f[:, n, :], sum_f[:, n, :]))
                if i < FH:
                    await_evacuated(dve, f"f_s{i}")
                    v.tensor_scalar(nm_f[:, i, :], mx_f[:, i, :], -1.0, None, ALU.mult).then_inc(sem("nm_ready"), 1)
                if 1 <= i <= FH:
                    step.reach(inverted)
                    v.tensor_scalar(p_f[:, n % PBUF, 0:P], p_f[:, n % PBUF, 0:P], inv_f[:, n, 0:1], None, ALU.mult)
                    v.tensor_scalar(p_f[:, n % PBUF, P:], p_f[:, n % PBUF, P:], inv_f[:, n, 1:2], None,
                                    ALU.mult).then_inc(sem("p_ready"), 1)
                if i >= 6 and i % 2 == 0:
                    m = (i - 6) // 2
                    if m == 0:
                        await_evacuated(dve, *[f"f_g{j}" for j in range(4)])
                    await_full(dve, f"f_o{m}")
                    freed(v.tensor_tensor(gT_f[:, m, :], gT_f[:, m, :], bank(f"f_o{m}")[:, 0:T], ALU.mult), f"f_o{m}")
            finish_mixer("f", 1)
            moe(1)
            dve.wait_ge(sem("final_in"), 16)
            for t in range(TC):
                weighted = step.mark(v.tensor_tensor(y_out[:, t, :], h[:, t, :], final_g, ALU.mult))
                dve.wait_ge(sem("squared"), 2 * TC + 2 + t)
                mean(t)
            inverse("last", 0)
            dve.wait_ge(sem("rstd_ready"), NORMS["last"] + 2)
            v.reciprocal(stat[:, 2, 1:2], stat[:, 2, 1:2]).then_inc(sem("last_inverse"), 1)
            step.reach(weighted)
            v.tensor_scalar(y_out[:, 0, :], y_out[:, 0, :], stat[:, 2, 0:1], None, ALU.mult).then_inc(out_ready[0], 1)


_INS = ['x', 'gla_norm', 'gla_w_in', 'gla_w_a2', 'gla_b_a', 'gla_out_norm', 'gla_w_out', 'kv_norm', 'kv_w',
        'kv_b_f', 'fox_norm', 'fox_w_in', 'fox_w_out', 'ffn_norm', 'router_coarse_w', 'router_coarse_b',
        'router_fine_w', 'router_fine_b', 'expert_w_gate', 'expert_w_up', 'expert_w_down', 'final_norm']


def kernel(**inputs):
    import numpy as _np
    import concourse.bacc as _bacc
    from concourse.bass_utils import run_bass_kernel_spmd as _run

    nc = _bacc.Bacc("TRN2", target_bir_lowering=False, num_devices=1, dynamic_dma_scratch_size=1024)
    arrays, args = {}, []
    for name in _INS:
        a = _np.ascontiguousarray(inputs[name])
        arrays[f"in_{name}_dram"] = a
        args.append(nc.dram_tensor(f"in_{name}_dram", a.shape, mybir.dt.from_np(a.dtype), kind="ExternalInput").ap())
    out = nc.dram_tensor("out_0_dram", (1, T, D), F32, kind="ExternalOutput").ap()
    trunk(nc, *args, out)
    r = _run(nc, [arrays], core_ids=[0])
    return r.results[0]["out_0_dram"]
```
